# Optimizing a Trainium2 kernel written in Bass

```python
import math
import jax, jax.numpy as jnp
from jax import lax
import numpy as np

D_MODEL = 1024
BATCH = 1
SEQ = 256
DEPTH = 2

HEAD_DIM = 64
A_HEADS = 6
A_PAIRS = ((128, 1), (512, 4), (2048, 16))
B_HEADS = 4
B_QK_DIM = 32
B_V_DIM = 2 * B_QK_DIM
C_HEADS = 6
C_Q_LORA = 256
C_KV_LORA = 128
C_NOPE = 64
C_ROPE = 32
C_V = 64
ROPE_THETA = 10000.0
MIX_WIDTH = (A_HEADS + B_HEADS + C_HEADS) * HEAD_DIM
A_COLS = 3 * A_HEADS * HEAD_DIM
B_COLS = B_HEADS * (2 * 2 * B_QK_DIM + B_V_DIM)
C_COLS = C_Q_LORA + C_KV_LORA + C_ROPE
IN_COLS = A_COLS + B_COLS + C_COLS
NUM_BUCKETS = 32
MAX_DISTANCE = 2048
BIAS_HEADS = A_HEADS + B_HEADS
FF_DIM = -(-8 * D_MODEL // (3 * 256)) * 256
Q_BLOCK = 128
DEEPNORM_ALPHA = (2 * DEPTH) ** 0.25
DEEPNORM_BETA = (8 * DEPTH) ** -0.25
LN_EPS = 1e-5
LATENT_EPS = 1e-6
SUBLN_EPS = 1e-5


def layer_norm(x, g, b):
    xf = x.astype(jnp.float32)
    mu = jnp.mean(xf, axis=-1, keepdims=True)
    var = jnp.mean(jnp.square(xf - mu), axis=-1, keepdims=True)
    return ((xf - mu) * lax.rsqrt(var + LN_EPS) * g + b).astype(x.dtype)

def rms_norm(x, g, eps):
    xf = x.astype(jnp.float32)
    return (xf * lax.rsqrt(jnp.mean(xf * xf, axis=-1, keepdims=True) + eps) * g).astype(x.dtype)

def t5_bucket(dist):
    max_exact = NUM_BUCKETS // 2
    d = jnp.maximum(dist, 0)
    df = jnp.maximum(d, 1).astype(jnp.float32)
    large = max_exact + (jnp.log(df / max_exact) / math.log(MAX_DISTANCE / max_exact)
                         * (NUM_BUCKETS - max_exact)).astype(jnp.int32)
    large = jnp.minimum(large, NUM_BUCKETS - 1)
    return jnp.where(d < max_exact, d, large)

def apply_rope(x):
    S, half = x.shape[1], x.shape[-1] // 2
    inv = ROPE_THETA ** (-jnp.arange(half, dtype=jnp.float32) / half)
    ang = jnp.arange(S, dtype=jnp.float32)[:, None] * inv[None, :]
    cos, sin = jnp.cos(ang)[None, :, None, :], jnp.sin(ang)[None, :, None, :]
    xf = x.astype(jnp.float32)
    x1, x2 = xf[..., :half], xf[..., half:]
    return jnp.concatenate([x1 * cos - x2 * sin, x2 * cos + x1 * sin], axis=-1).astype(x.dtype)

def dilated_pair(q, k, v, bias_tab, window, dil):
    Bn, S, H, Dh = q.shape
    blk = window // dil
    L = S // dil
    nb = -(-L // blk)
    pad = nb * blk - L

    def to_blocks(a):
        a = a.reshape(Bn, L, dil, H, Dh)
        a = jnp.pad(a, ((0, 0), (0, pad), (0, 0), (0, 0), (0, 0)))
        return a.reshape(Bn, nb, blk, dil, H, Dh)

    def with_prev(a):
        prev = jnp.pad(a, ((0, 0), (1, 0), (0, 0), (0, 0), (0, 0), (0, 0)))[:, :nb]
        return jnp.concatenate([prev, a], axis=2)

    qb = to_blocks(q)
    kb = with_prev(to_blocks(k))
    vb = with_prev(to_blocks(v))
    rel = jnp.arange(blk)[:, None] + blk - jnp.arange(2 * blk)[None, :]
    band = (rel >= 0) & (rel <= blk)
    not_first = (jnp.arange(nb)[:, None, None] > 0) | (jnp.arange(2 * blk)[None, None, :] >= blk)
    mask = band[None] & not_first
    bias = bias_tab[t5_bucket(rel * dil)].astype(jnp.float32).transpose(2, 0, 1)
    s = jnp.einsum('bnqrhd,bnkrhd->bnrhqk', qb, kb).astype(jnp.float32) * (Dh ** -0.5) + bias
    s = jnp.where(mask[None, :, None, None], s, -jnp.inf)
    lse = jax.nn.logsumexp(s, axis=-1)
    p = jnp.exp(s - lse[..., None]).astype(v.dtype)
    o = jnp.einsum('bnrhqk,bnkrhd->bnqrhd', p, vb)
    o = o.reshape(Bn, nb * blk, dil, H, Dh)[:, :L].reshape(Bn, S, H, Dh)
    lse = lse.transpose(0, 1, 4, 2, 3).reshape(Bn, nb * blk, dil, H)[:, :L].reshape(Bn, S, H)
    return o, lse

def dilated_mixture(q, k, v, bias_tab):
    outs, lses = [], []
    for window, dil in A_PAIRS:
        o, lse = dilated_pair(q, k, v, bias_tab, window, dil)
        outs.append(o)
        lses.append(lse)
    w = jax.nn.softmax(jnp.stack(lses, axis=0), axis=0)
    o = jnp.sum(w[..., None] * jnp.stack(outs, axis=0).astype(jnp.float32), axis=0)
    return o.astype(q.dtype)

def sweep_query_blocks(block_fn, n_pos):
    o = lax.map(block_fn, jnp.arange(n_pos // Q_BLOCK))
    o = jnp.moveaxis(o, 0, 1)
    return o.reshape((o.shape[0], n_pos) + o.shape[3:])

def diff_attention(q1, q2, k1, k2, v, lam, bias_tab):
    S = q1.shape[1]
    scale = q1.shape[-1] ** -0.5
    kpos = jnp.arange(S)

    def block(i):
        start = i * Q_BLOCK
        sl = lambda a: lax.dynamic_slice_in_dim(a, start, Q_BLOCK, axis=1)
        rel = (start + jnp.arange(Q_BLOCK))[:, None] - kpos[None, :]
        causal = rel >= 0
        bias = bias_tab[t5_bucket(rel)].astype(jnp.float32).transpose(2, 0, 1)

        def probs(q, k):
            s = jnp.einsum('bqhd,bkhd->bhqk', sl(q), k).astype(jnp.float32) * scale + bias
            return jax.nn.softmax(jnp.where(causal, s, -jnp.inf), axis=-1)

        a = probs(q1, k1) - lam * probs(q2, k2)
        return jnp.einsum('bhqk,bkhd->bqhd', a.astype(v.dtype), v)

    return sweep_query_blocks(block, S)

def causal_attention(q, k, v):
    S = q.shape[1]
    scale = q.shape[-1] ** -0.5
    kpos = jnp.arange(S)

    def block(i):
        start = i * Q_BLOCK
        qs = lax.dynamic_slice_in_dim(q, start, Q_BLOCK, axis=1)
        causal = (start + jnp.arange(Q_BLOCK))[:, None] >= kpos[None, :]
        s = jnp.einsum('bqhd,bkhd->bhqk', qs, k).astype(jnp.float32) * scale
        p = jax.nn.softmax(jnp.where(causal, s, -jnp.inf), axis=-1)
        return jnp.einsum('bhqk,bkhd->bqhd', p.astype(v.dtype), v)

    return sweep_query_blocks(block, S)

def hybrid_layer(x, layer_idx, rel_bias, w_in, q_norm_g, kv_norm_g, w_uq, w_ukv,
                 diff_lambda, subln_g, w_o, ln1_g, ln1_b, ln2_g, ln2_b, w_gate, w_up, w_down):
    Bn, S, _ = x.shape
    proj = x @ w_in
    a_in, b_in, c_in = jnp.split(proj, [A_COLS, A_COLS + B_COLS], axis=-1)

    a = a_in.reshape(Bn, S, 3, A_HEADS, HEAD_DIM)
    o_a = dilated_mixture(a[:, :, 0], a[:, :, 1], a[:, :, 2], rel_bias[:, :A_HEADS])

    qk_cols = B_HEADS * 2 * B_QK_DIM
    bq = b_in[..., :qk_cols].reshape(Bn, S, B_HEADS, 2, B_QK_DIM)
    bk = b_in[..., qk_cols:2 * qk_cols].reshape(Bn, S, B_HEADS, 2, B_QK_DIM)
    bv = b_in[..., 2 * qk_cols:].reshape(Bn, S, B_HEADS, B_V_DIM)
    lam_init = 0.8 - 0.6 * math.exp(-0.3 * layer_idx)
    lf = diff_lambda.astype(jnp.float32)
    lam = jnp.exp(jnp.sum(lf[0] * lf[1])) - jnp.exp(jnp.sum(lf[2] * lf[3])) + lam_init
    o_b = diff_attention(bq[..., 0, :], bq[..., 1, :], bk[..., 0, :], bk[..., 1, :], bv, lam,
                         rel_bias[:, A_HEADS:])
    o_b = (rms_norm(o_b, subln_g, SUBLN_EPS) * (1.0 - lam_init)).astype(x.dtype)

    c_q, c_kv, k_r = jnp.split(c_in, [C_Q_LORA, C_Q_LORA + C_KV_LORA], axis=-1)
    q = (rms_norm(c_q, q_norm_g, LATENT_EPS) @ w_uq).reshape(Bn, S, C_HEADS, C_NOPE + C_ROPE)
    kv = (rms_norm(c_kv, kv_norm_g, LATENT_EPS) @ w_ukv).reshape(Bn, S, C_HEADS, C_NOPE + C_V)
    q_c = jnp.concatenate([q[..., :C_NOPE], apply_rope(q[..., C_NOPE:])], axis=-1)
    k_rope = apply_rope(k_r[:, :, None, :])
    k_c = jnp.concatenate([kv[..., :C_NOPE],
                           jnp.broadcast_to(k_rope, (Bn, S, C_HEADS, C_ROPE))], axis=-1)
    o_c = causal_attention(q_c, k_c, kv[..., C_NOPE:])

    heads = jnp.concatenate([o_a.reshape(Bn, S, -1), o_b.reshape(Bn, S, -1),
                             o_c.reshape(Bn, S, -1)], axis=-1)
    h = layer_norm(DEEPNORM_ALPHA * x + heads @ w_o, ln1_g, ln1_b)

    ffn = (jax.nn.silu(h @ w_gate) * (h @ w_up)) @ w_down
    return layer_norm(DEEPNORM_ALPHA * h + ffn, ln2_g, ln2_b)

def first_inputs(seed: int = 0) -> dict:
    key = jax.random.key(seed)
    ks = jax.random.split(key, 20)
    f32 = jnp.float32
    nrm = lambda k, shape, scale: jax.random.normal(k, shape, f32) * scale
    return {
        "x": nrm(ks[0], (BATCH, SEQ, D_MODEL), 1.0),
        "rel_bias": nrm(ks[1], (NUM_BUCKETS, BIAS_HEADS), 0.5),
        "w_in": nrm(ks[2], (DEPTH, D_MODEL, IN_COLS), D_MODEL ** -0.5),
        "q_norm_g": 1.0 + nrm(ks[3], (DEPTH, C_Q_LORA), 0.05),
        "kv_norm_g": 1.0 + nrm(ks[4], (DEPTH, C_KV_LORA), 0.05),
        "w_uq": nrm(ks[5], (DEPTH, C_Q_LORA, C_HEADS * (C_NOPE + C_ROPE)), C_Q_LORA ** -0.5),
        "w_ukv": nrm(ks[6], (DEPTH, C_KV_LORA, C_HEADS * (C_NOPE + C_V)), C_KV_LORA ** -0.5),
        "diff_lambda": nrm(ks[7], (DEPTH, 4, B_QK_DIM), 0.1),
        "subln_g": 1.0 + nrm(ks[8], (DEPTH, B_V_DIM), 0.05),
        "w_o": nrm(ks[9], (DEPTH, MIX_WIDTH, D_MODEL), MIX_WIDTH ** -0.5 * DEEPNORM_BETA),
        "ln1_g": 1.0 + nrm(ks[10], (DEPTH, D_MODEL), 0.05),
        "ln1_b": nrm(ks[11], (DEPTH, D_MODEL), 0.02),
        "ln2_g": 1.0 + nrm(ks[12], (DEPTH, D_MODEL), 0.05),
        "ln2_b": nrm(ks[13], (DEPTH, D_MODEL), 0.02),
        "w_gate": nrm(ks[14], (DEPTH, D_MODEL, FF_DIM), D_MODEL ** -0.5),
        "w_up": nrm(ks[15], (DEPTH, D_MODEL, FF_DIM), D_MODEL ** -0.5),
        "w_down": nrm(ks[16], (DEPTH, FF_DIM, D_MODEL), FF_DIM ** -0.5 * DEEPNORM_BETA),
    }

def first_block(x, rel_bias, w_in, q_norm_g, kv_norm_g, w_uq, w_ukv, diff_lambda, subln_g, w_o,
              ln1_g, ln1_b, ln2_g, ln2_b, w_gate, w_up, w_down):
    for l in range(DEPTH):
        x = hybrid_layer(x, l, rel_bias, w_in[l], q_norm_g[l], kv_norm_g[l], w_uq[l], w_ukv[l],
                         diff_lambda[l], subln_g[l], w_o[l], ln1_g[l], ln1_b[l], ln2_g[l], ln2_b[l],
                         w_gate[l], w_up[l], w_down[l])
    return x


DEPTH_2 = 1

ROPE_DIM = HEAD_DIM // 4
ROPE_THETA_2 = 500000.0
EPS = 1e-6
NEG_INF = -1e30
FORCED_SCORE = 1e6
NSA_HEADS = 8
NSA_KV_HEADS = 2
NSA_GROUP = NSA_HEADS // NSA_KV_HEADS
CMP_LEN = 32
CMP_STRIDE = 16
CMP_HIDDEN = 128
SLC_BLOCK = 64
SLC_TOPN = 8
WINDOW = 512
DSA_HEADS = 8
KV_LORA = 128
NOPE_DIM = HEAD_DIM - ROPE_DIM
IDX_HEADS = 8
IDX_DIM = 64
IDX_TOPK_MAX = 256
D_FF = ((8 * D_MODEL + 3 * 256 - 1) // (3 * 256)) * 256
IN_SPLITS = (NSA_HEADS * HEAD_DIM,) + (NSA_KV_HEADS * HEAD_DIM,) * 6 + (
    3 * NSA_HEADS, DSA_HEADS * HEAD_DIM, KV_LORA, ROPE_DIM, IDX_HEADS * IDX_DIM, IDX_DIM, IDX_HEADS)
IN_WIDTH = sum(IN_SPLITS)


def _rms_norm(x, g):
    xf = x.astype(jnp.float32)
    y = xf * lax.rsqrt(jnp.mean(xf * xf, axis=-1, keepdims=True) + EPS)
    return (y * g.astype(jnp.float32)).astype(x.dtype)

def _rope_tables(seq):
    inv_freq = 1.0 / (ROPE_THETA_2 ** (jnp.arange(0, ROPE_DIM, 2, dtype=jnp.float32) / ROPE_DIM))
    ang = jnp.arange(seq, dtype=jnp.float32)[:, None] * inv_freq[None, :]
    return jnp.cos(ang), jnp.sin(ang)

def _rope(x, cos, sin):
    half = ROPE_DIM // 2
    xr = x[..., :ROPE_DIM].astype(jnp.float32)
    x1, x2 = xr[..., :half], xr[..., half:]
    c, s = cos[:, None, :], sin[:, None, :]
    rot = jnp.concatenate([x1 * c - x2 * s, x2 * c + x1 * s], axis=-1)
    return jnp.concatenate([rot.astype(x.dtype), x[..., ROPE_DIM:]], axis=-1)

def _masked_softmax(s, mask):
    s = jnp.where(mask, s.astype(jnp.float32), NEG_INF)
    m = jnp.max(s, axis=-1, keepdims=True)
    e = jnp.where(mask, jnp.exp(s - m), 0.0)
    return e / jnp.maximum(jnp.sum(e, axis=-1, keepdims=True), 1e-30)

def _q_blocks(a):
    b, s = a.shape[:2]
    return jnp.moveaxis(a.reshape((b, s // Q_BLOCK, Q_BLOCK) + a.shape[2:]), 1, 0)

def _from_blocks(o):
    nb, b, tq = o.shape[:3]
    return jnp.moveaxis(o, 0, 1).reshape((b, nb * tq) + o.shape[3:])

def _compress(k, pe, w1, b1, w2, b2):
    b, s, g, dh = k.shape
    n_cmp = (s - CMP_LEN) // CMP_STRIDE + 1
    idx = np.arange(n_cmp)[:, None] * CMP_STRIDE + np.arange(CMP_LEN)[None, :]
    blocks = k[:, idx] + pe[:, None, :]
    flat = jnp.transpose(blocks, (0, 3, 1, 2, 4)).reshape(b, g, n_cmp, CMP_LEN * dh)
    hid = jax.nn.gelu(flat @ w1 + b1)
    return hid @ w2 + b2

def _nsa_group(q, k_cmp, v_cmp, k_slc, v_slc, k_win, v_win, gates, cos, sin,
               cmp_pe, cmp_w1, cmp_b1, cmp_w2, cmp_b2):
    b, s = q.shape[:2]
    g_, r_, dh = NSA_KV_HEADS, NSA_GROUP, HEAD_DIM
    scale = HEAD_DIM ** -0.5
    tpos = jnp.arange(s)
    qg = _rope(q.reshape(b, s, NSA_HEADS, dh), cos, sin).reshape(b, s, g_, r_, dh)
    kc = _compress(_rope(k_cmp.reshape(b, s, g_, dh), cos, sin), cmp_pe[0], cmp_w1[0], cmp_b1[0], cmp_w2[0], cmp_b2[0])
    vc = _compress(v_cmp.reshape(b, s, g_, dh), cmp_pe[1], cmp_w1[1], cmp_b1[1], cmp_w2[1], cmp_b2[1])
    n_cmp = kc.shape[2]
    cmp_end = jnp.arange(n_cmp) * CMP_STRIDE + CMP_LEN - 1
    mask_c = cmp_end[None, :] <= tpos[:, None]
    p_c = _masked_softmax(jnp.einsum('bsgrd,bgnd->bgrsn', qg, kc) * scale, mask_c)
    o_cmp = jnp.einsum('bgrsn,bgnd->bsgrd', p_c.astype(vc.dtype), vc).reshape(b, s, NSA_HEADS, dh)
    n_slc = s // SLC_BLOCK
    ci = np.arange(n_cmp)[:, None] * CMP_STRIDE
    sj = np.arange(n_slc)[None, :] * SLC_BLOCK
    overlap = ((ci < sj + SLC_BLOCK) & (ci + CMP_LEN > sj)).astype(np.float32)
    imp = jnp.einsum('bgrsn,nj->bgsj', p_c, jnp.asarray(overlap))
    blk_t = (tpos // SLC_BLOCK)[:, None]
    j = jnp.arange(n_slc)[None, :]
    visible = j <= blk_t
    forced = (j == 0) | (j == blk_t) | (j == blk_t - 1)
    imp = jnp.where(visible, jnp.where(forced, FORCED_SCORE, imp), -jnp.inf)
    n_sel = min(SLC_TOPN, n_slc)
    _, sel = lax.top_k(imp, n_sel)
    ks_blocks = jnp.transpose(_rope(k_slc.reshape(b, s, g_, dh), cos, sin).reshape(b, n_slc, SLC_BLOCK, g_, dh), (0, 3, 1, 2, 4))
    vs_blocks = jnp.transpose(v_slc.reshape(b, n_slc, SLC_BLOCK, g_, dh), (0, 3, 1, 2, 4))
    pad = ((0, 0), (WINDOW, 0), (0, 0), (0, 0))
    kw = jnp.pad(_rope(k_win.reshape(b, s, g_, dh), cos, sin), pad)
    vw = jnp.pad(v_win.reshape(b, s, g_, dh), pad)
    gather = jax.vmap(jax.vmap(lambda tab, ix: tab[ix]))

    def block_fn(args):
        q_b, sel_b, t0 = args
        sel_b = jnp.transpose(sel_b, (0, 2, 1, 3))
        tq = t0 + jnp.arange(Q_BLOCK)
        kg = gather(ks_blocks, sel_b).reshape(b, g_, Q_BLOCK, n_sel * SLC_BLOCK, dh)
        vg = gather(vs_blocks, sel_b).reshape(b, g_, Q_BLOCK, n_sel * SLC_BLOCK, dh)
        kpos = (sel_b[..., None] * SLC_BLOCK + jnp.arange(SLC_BLOCK)).reshape(b, g_, Q_BLOCK, n_sel * SLC_BLOCK)
        mask_s = (kpos <= tq[None, None, :, None])[:, :, None]
        p_s = _masked_softmax(jnp.einsum('btgrd,bgtkd->bgrtk', q_b, kg) * scale, mask_s)
        o_s = jnp.einsum('bgrtk,bgtkd->btgrd', p_s.astype(vg.dtype), vg)
        kwb = lax.dynamic_slice_in_dim(kw, t0, Q_BLOCK + WINDOW, axis=1)
        vwb = lax.dynamic_slice_in_dim(vw, t0, Q_BLOCK + WINDOW, axis=1)
        wpos = t0 - WINDOW + jnp.arange(Q_BLOCK + WINDOW)
        mask_w = (wpos[None, :] <= tq[:, None]) & (wpos[None, :] > tq[:, None] - WINDOW) & (wpos[None, :] >= 0)
        p_w = _masked_softmax(jnp.einsum('btgrd,bsgd->bgrts', q_b, kwb) * scale, mask_w)
        o_w = jnp.einsum('bgrts,bsgd->btgrd', p_w.astype(vwb.dtype), vwb)
        return o_s, o_w

    starts = jnp.arange(s // Q_BLOCK, dtype=jnp.int32) * Q_BLOCK
    o_s, o_w = lax.map(block_fn, (_q_blocks(qg), _q_blocks(jnp.transpose(sel, (0, 2, 1, 3))), starts))
    o_s = _from_blocks(o_s).reshape(b, s, NSA_HEADS, dh)
    o_w = _from_blocks(o_w).reshape(b, s, NSA_HEADS, dh)
    gt = jax.nn.sigmoid(gates.astype(jnp.float32)).astype(q.dtype).reshape(b, s, 3, NSA_HEADS, 1)
    o = gt[:, :, 0] * o_cmp + gt[:, :, 1] * o_s + gt[:, :, 2] * o_w
    return o.reshape(b, s, NSA_HEADS * dh)

def _dsa_group(q, c_kv, k_rope, q_idx, k_idx, w_idx, cos, sin, g_kv, w_uk, w_uv):
    b, s = q.shape[:2]
    scale = HEAD_DIM ** -0.5
    q = _rope(q.reshape(b, s, DSA_HEADS, HEAD_DIM), cos, sin)
    q_rope, q_nope = q[..., :ROPE_DIM], q[..., ROPE_DIM:]
    c_kv = _rms_norm(c_kv, g_kv)
    k_rope = _rope(k_rope[:, :, None, :], cos, sin)[:, :, 0]
    q_lat = jnp.einsum('bshe,hre->bshr', q_nope, w_uk)
    q_idx = _rope(q_idx.reshape(b, s, IDX_HEADS, IDX_DIM), cos, sin)
    k_idx = _rope(k_idx[:, :, None, :], cos, sin)[:, :, 0]
    w_idx = w_idx.astype(jnp.float32) * (IDX_HEADS ** -0.5 * IDX_DIM ** -0.5)
    k_sel = min(IDX_TOPK_MAX, s // 4)
    spos = jnp.arange(s)
    gather = jax.vmap(lambda tab, ix: tab[ix])

    def block_fn(args):
        ql_b, qr_b, qi_b, wi_b, t0 = args
        tq = t0 + jnp.arange(Q_BLOCK)
        logits = jnp.einsum('bthd,bsd->bths', qi_b, k_idx).astype(jnp.float32)
        score = jnp.einsum('bths,bth->bts', jax.nn.relu(logits), wi_b)
        score = jnp.where(spos[None, None, :] <= tq[None, :, None], score, -jnp.inf)
        _, idx = lax.top_k(score, k_sel)
        cg = gather(c_kv, idx)
        krg = gather(k_rope, idx)
        sc = (jnp.einsum('bthr,btkr->bhtk', ql_b, cg) + jnp.einsum('bthe,btke->bhtk', qr_b, krg)) * scale
        mask = (idx <= tq[None, :, None])[:, None]
        p = _masked_softmax(sc, mask)
        return jnp.einsum('bhtk,btkr->bthr', p.astype(cg.dtype), cg)

    starts = jnp.arange(s // Q_BLOCK, dtype=jnp.int32) * Q_BLOCK
    o_lat = _from_blocks(lax.map(block_fn, (_q_blocks(q_lat), _q_blocks(q_rope), _q_blocks(q_idx), _q_blocks(w_idx), starts)))
    o = jnp.einsum('bshr,hrd->bshd', o_lat, w_uv)
    return o.reshape(b, s, DSA_HEADS * HEAD_DIM)

def _hybrid_mixer(h, cos, sin, w_in, cmp_pe, cmp_w1, cmp_b1, cmp_w2, cmp_b2, g_kv, w_uk, w_uv, w_out):
    proj = h @ w_in
    split_points = [int(v) for v in np.cumsum(IN_SPLITS)[:-1]]
    (nq, nkc, nvc, nks, nvs, nkw, nvw, ngate, dq, dckv, dkr, iq, ik, iw) = jnp.split(proj, split_points, axis=-1)
    o_a = _nsa_group(nq, nkc, nvc, nks, nvs, nkw, nvw, ngate, cos, sin, cmp_pe, cmp_w1, cmp_b1, cmp_w2, cmp_b2)
    o_b = _dsa_group(dq, dckv, dkr, iq, ik, iw, cos, sin, g_kv, w_uk, w_uv)
    return jnp.concatenate([o_a, o_b], axis=-1) @ w_out

def _swiglu(h, w_gate_up, w_down):
    gate, up = jnp.split(h @ w_gate_up, 2, axis=-1)
    return (jax.nn.silu(gate) * up) @ w_down

def second_inputs(seed: int = 0) -> dict:
    key = jax.random.key(seed)
    ks = jax.random.split(key, 20)
    L = DEPTH_2

    def nrm(k, shape, scale):
        return jax.random.normal(k, shape, jnp.float32) * scale

    def gain(k, shape):
        return 1.0 + 0.05 * jax.random.normal(k, shape, jnp.float32)

    return {
        'x': nrm(ks[0], (BATCH, SEQ, D_MODEL), 1.0),
        'c': nrm(ks[1], (BATCH, D_MODEL), 1.0),
        'w_ada': nrm(ks[2], (L, D_MODEL, 6 * D_MODEL), 0.5 * D_MODEL ** -0.5),
        'b_ada': nrm(ks[3], (L, 6 * D_MODEL), 0.01),
        'g_pre_mix': gain(ks[4], (L, D_MODEL)),
        'g_post_mix': gain(ks[5], (L, D_MODEL)),
        'g_pre_ffn': gain(ks[6], (L, D_MODEL)),
        'g_post_ffn': gain(ks[7], (L, D_MODEL)),
        'w_in': nrm(ks[8], (L, D_MODEL, IN_WIDTH), D_MODEL ** -0.5),
        'cmp_pe': nrm(ks[9], (L, 2, CMP_LEN, HEAD_DIM), 0.1),
        'cmp_w1': nrm(ks[10], (L, 2, CMP_LEN * HEAD_DIM, CMP_HIDDEN), (CMP_LEN * HEAD_DIM) ** -0.5),
        'cmp_b1': nrm(ks[11], (L, 2, CMP_HIDDEN), 0.01),
        'cmp_w2': nrm(ks[12], (L, 2, CMP_HIDDEN, HEAD_DIM), CMP_HIDDEN ** -0.5),
        'cmp_b2': nrm(ks[13], (L, 2, HEAD_DIM), 0.01),
        'g_kv_norm': gain(ks[14], (L, KV_LORA)),
        'w_uk': nrm(ks[15], (L, DSA_HEADS, KV_LORA, NOPE_DIM), KV_LORA ** -0.5),
        'w_uv': nrm(ks[16], (L, DSA_HEADS, KV_LORA, HEAD_DIM), KV_LORA ** -0.5),
        'w_out': nrm(ks[17], (L, D_MODEL, D_MODEL), D_MODEL ** -0.5),
        'w_gate_up': nrm(ks[18], (L, D_MODEL, 2 * D_FF), D_MODEL ** -0.5),
        'w_down': nrm(ks[19], (L, D_FF, D_MODEL), D_FF ** -0.5),
    }

def second_block(x, c, w_ada, b_ada, g_pre_mix, g_post_mix, g_pre_ffn, g_post_ffn, w_in,
              cmp_pe, cmp_w1, cmp_b1, cmp_w2, cmp_b2, g_kv_norm, w_uk, w_uv, w_out,
              w_gate_up, w_down):
    cos, sin = _rope_tables(x.shape[1])
    c_act = jax.nn.silu(c)
    for l in range(DEPTH_2):
        mod = (c_act @ w_ada[l] + b_ada[l])[:, None, :]
        sh_m, sc_m, ga_m, sh_f, sc_f, ga_f = jnp.split(mod, 6, axis=-1)
        h = _rms_norm(x, g_pre_mix[l]) * (1.0 + sc_m) + sh_m
        y = _hybrid_mixer(h, cos, sin, w_in[l], cmp_pe[l], cmp_w1[l], cmp_b1[l], cmp_w2[l], cmp_b2[l],
                          g_kv_norm[l], w_uk[l], w_uv[l], w_out[l])
        x = x + ga_m * _rms_norm(y, g_post_mix[l])
        h = _rms_norm(x, g_pre_ffn[l]) * (1.0 + sc_f) + sh_f
        x = x + ga_f * _rms_norm(_swiglu(h, w_gate_up[l], w_down[l]), g_post_ffn[l])
    return x


def setup_inputs(seed=0):
    out = dict(first_inputs(seed))
    for name, value in second_inputs(seed + 1).items():
        if name != "x":
            out[name + "_2"] = value
    return out


def reference(
    x, rel_bias, w_in, q_norm_g, kv_norm_g, w_uq, w_ukv, diff_lambda, subln_g, w_o, ln1_g,
    ln1_b, ln2_g, ln2_b, w_gate, w_up, w_down, c_2, w_ada_2, b_ada_2, g_pre_mix_2, g_post_mix_2,
    g_pre_ffn_2, g_post_ffn_2, w_in_2, cmp_pe_2, cmp_w1_2, cmp_b1_2, cmp_w2_2, cmp_b2_2,
    g_kv_norm_2, w_uk_2, w_uv_2, w_out_2, w_gate_up_2, w_down_2,
):
    x = first_block(
        x, rel_bias, w_in, q_norm_g, kv_norm_g, w_uq, w_ukv, diff_lambda, subln_g, w_o, ln1_g,
        ln1_b, ln2_g, ln2_b, w_gate, w_up, w_down,
    )
    return second_block(
        x, c_2, w_ada_2, b_ada_2, g_pre_mix_2, g_post_mix_2, g_pre_ffn_2, g_post_ffn_2, w_in_2,
        cmp_pe_2, cmp_w1_2, cmp_b1_2, cmp_w2_2, cmp_b2_2, g_kv_norm_2, w_uk_2, w_uv_2, w_out_2,
        w_gate_up_2, w_down_2,
    )


_drawn_inputs = setup_inputs


def setup_inputs(seed=0):
    import zlib

    import numpy as np

    out = dict(_drawn_inputs(seed))
    spreads = {}
    factors = {'q_norm_g': 8.0,
     'kv_norm_g': 6.632,
     'diff_lambda': 3.542,
     'subln_g': 3.78,
     'b_ada_2': 2.835,
     'g_post_mix_2': 3.644,
     'g_pre_ffn_2': 2.976,
     'g_post_ffn_2': 4.039,
     'cmp_pe_2': 3.973,
     'cmp_b1_2': 64.0,
     'cmp_b2_2': 39.838,
     'g_kv_norm_2': 4.821}
    for name, (base, spread) in spreads.items():
        noise = np.random.default_rng([zlib.crc32(name.encode()), seed]).standard_normal(out[name].shape)
        drawn = base * np.exp(spread * noise) if base else spread * noise
        out[name] = __import__('jax').numpy.asarray(drawn.astype(out[name].dtype))
    for name, factor in factors.items():
        out[name] = (out[name] * factor).astype(out[name].dtype)
    return out
```

```python
import math
from contextlib import ExitStack

import numpy as np
import concourse.bass as bass
from concourse import mybir

F32 = mybir.dt.float32
ALU = mybir.AluOpType
ACT = mybir.ActivationFunctionType
AX = mybir.AxisListType

P, S, TT, D = 128, 256, 2, 1024
KC = D // P
FF = 2816
FC = FF // P
DEPTH = 2
ALPHA = (2 * DEPTH) ** 0.25
HD = 64
A_H, B_H, C_H = 6, 4, 6
BQ = 32
QL, KVL, NOPE, ROPE = 256, 128, 64, 32
CQ = NOPE + ROPE
IN1 = 2336
IN2 = 2544
A_K, A_V = A_H * HD, 2 * A_H * HD
B_Q, B_K, B_V = 1152, 1408, 1664
C_IN = 1920
C_KR = C_IN + QL + KVL
NEG = -1e30
TAKEN = -3e38
NQ, NKC, NVC, NKS, NVS, NKW, NVW, NGT, DQ, DCKV, DKR, IQ, IK, IW = (
    0, 512, 640, 768, 896, 1024, 1152, 1280, 1304, 1816, 1944, 1960, 2472, 2536)
R2 = 16
NCMP = 15
TOPK = 64
SLOTW = 4096
NSLOT = 4
GELU_C = math.sqrt(2.0 / math.pi)
SC_A, SC_B, SC_C = HD ** -0.5, BQ ** -0.5, CQ ** -0.5
LAM0 = [0.8 - 0.6 * math.exp(-0.3 * l) for l in range(DEPTH)]

CC = {}


def _const_layout():
    at = 0
    for name, n in (("ident", P), ("flip", P), ("causal", S), ("cos1", TT * 16), ("sin1", TT * 16), ("cos2", TT * 8),
                    ("sin2", TT * 8), ("cmpmask", TT * 16), ("cmpvalid", TT), ("biasscale", 1)):
        CC[name] = (at, at + n)
        at += n
    return at


NCONST = _const_layout()


def constants():
    c = np.zeros((P, NCONST), np.float32)

    def put(name, value):
        a, b = CC[name]
        c[:, a:b] = np.asarray(value, np.float32).reshape(P, b - a)

    p = np.arange(P)[:, None]
    put("ident", np.eye(P))
    put("flip", np.eye(P)[::-1])
    put("causal", np.where(np.arange(S)[None] <= P + p, 0.0, NEG))
    tok = (np.arange(TT)[None, :] * P + p).astype(np.float32)
    inv1 = (np.float32(10000.0) ** (-np.arange(16, dtype=np.float32) / np.float32(16))).astype(np.float32)
    inv2 = (np.float32(1.0) / (np.float32(500000.0) ** (np.arange(0, R2, 2, dtype=np.float32) / np.float32(R2)))).astype(np.float32)
    for n, inv in (("1", inv1), ("2", inv2)):
        ang = (tok[:, :, None] * inv[None, None, :]).astype(np.float32).astype(np.float64)
        put("cos" + n, np.cos(ang))
        put("sin" + n, np.sin(ang))
    ends = np.arange(16) * 16 + 31
    put("cmpmask", np.where((ends[None, None] <= tok[:, :, None]) & (np.arange(16) < NCMP), 0.0, NEG))
    put("cmpvalid", tok >= 31)
    put("biasscale", np.where(p < A_H, 1 / SC_A, 1 / SC_B))
    d = 255 - np.arange(384)
    pos = np.maximum(d, 1).astype(np.float32)
    large = 16 + (np.log(pos / np.float32(16)) / math.log(2048 / 16) * 16).astype(np.int32)
    bucket = np.where(d < 16, np.maximum(d, 0), np.minimum(large, 31))
    hot = np.zeros((34, 384), np.float32)
    hot[bucket[d >= 0], np.nonzero(d >= 0)[0]] = 1.0
    times = (d <= 128).astype(int) + (d % 4 == 0) + (d % 16 == 0)
    hot[32] = np.where((d >= 0) & (times > 0), np.log(np.maximum(times, 1)), NEG)
    hot[33] = np.where(d >= 0, 0.0, NEG)
    which = np.zeros((2, A_H + B_H), np.float32)
    which[0, :A_H] = 1.0
    which[1, A_H:] = 1.0
    return c, hot, which


ROWS_A = [("ln1_g", 16), ("ln1_b", 16), ("ln2_g", 16), ("ln2_b", 16), ("q_norm_g", 4), ("kv_norm_g", 2),
          ("g_pre_mix_2", 8), ("g_post_mix_2", 8), ("g_pre_ffn_2", 8), ("g_post_ffn_2", 8), ("c_2", 8),
          ("g_kv_norm_2", 1), ("cmp_b1_2", 2)]
ROWS_B = [("b_ada_2", 48), ("cmp_pe_2", 32)]
FVAT = {}
_at = 0
for _rows in (ROWS_A, ROWS_B):
    for _n, _k in _rows:
        FVAT[_n] = _at
        _at += _k
N_A = sum(k for _, k in ROWS_A)
N_B = sum(k for _, k in ROWS_B)
B2K = 113
N_A += 1
for _n, _ in ROWS_B:
    FVAT[_n] += 1


class Job:
    def __init__(self, kind, q, k, kk, mask, scale, v, col, group, last):
        self.kind, self.q, self.k, self.kk, self.mask, self.scale = kind, q, k, kk, mask, scale
        self.v, self.col, self.group, self.last = v, col, group, last


GROUPS = {0: ["A", "B", "C"], 1: ["A", "B", "C"], 2: ["slc", "win", "cmp", "dsa"]}


def jobs_of(L):
    out = []
    if L < 2:
        for h in range(A_H):
            out.append(Job("A", (h // 2, 64 * (h % 2)), (3 + h // 2, 64 * (h % 2)), 64, ("bias", h), SC_A, ("proj", A_V + h * HD), h, 0, h == 5))
        for h in range(B_H):
            for i in range(2):
                n = 2 * h + i
                out.append(Job("B", (6 + n // 4, 32 * (n % 4)), (8 + n // 4, 32 * (n % 4)), 32, ("bias", A_H + h), SC_B, ("proj", B_V + h * HD), n, 1, n == 7))
        for h in range(C_H):
            out.append(Job("C", (10 + h, 0), (16 + h, 0), CQ, ("causal", 0), SC_C, ("cv", h), h, 2, h == 5))
        return out
    for g, (kind, kslot, v) in enumerate((("slc", 12, NVS), ("win", 13, NVW))):
        for h in range(8):
            out.append(Job(kind, (h % 4, 64 * (h // 4)), (kslot, 64 * (h // 4)), 64, ("causal", 0), SC_A, ("proj", v + 64 * (h // 4)), h, g, h == 7))
    for h in range(8):
        out.append(Job("cmp", (h % 4, 64 * (h // 4)), None, 64, ("cmp", 0), SC_A, ("vcmp", h // 4), h, 2, h == 7))
    for h in range(8):
        out.append(Job("dsa", (4 + h // 2, 64 * (h % 2)), (8 + h // 2, 64 * (h % 2)), 64, ("dsa", 0), SC_A, ("vd", h), h, 3, h == 7))
    return out


JOBS = {L: jobs_of(L) for L in range(3)}
JOB0 = {0: 0, 1: len(JOBS[0]), 2: 2 * len(JOBS[0])}
OBANK = {L: {g: 2 * (g % 2) for g in range(4)} for L in range(3)}


def alt(n):
    return "act" if n % 2 == 0 else "dve"


def plan():
    fills, empties = [], []

    def put(key, bank, eng, later=False):
        fills.append((key, bank, eng))
        if not later:
            empties.append(key)

    def product(key, L, eng="dve"):
        for t in range(TT):
            for h in range(2):
                put((key, L, t, h), 2 * t + h, eng)

    for n in range(2):
        put(("fv", n), 4 + n, "dve")
    put(("relb",), 6, "dve")
    for n in range(4):
        put(("xT", 0, n), 4 + n, alt(n))
    for L in range(3):
        if L == 2:
            for v in range(2):
                for h in range(2):
                    put(("G", v, h), 2 * v + h, "act")
        for i in range(5):
            for t in range(TT):
                put(("win", L, i, t), (2 * i + t) % 4, alt(t))
        if L < 2:
            for n in range(5):
                put(("ab", L, n), 4 + n % 4, alt(n))
            for n in range(2):
                put(("c", L, n), 5 + n, "act")
            product("uq", L, "act")
            for t in range(TT):
                for h in range(2):
                    put(("ukv", L, t, h), 4 + 2 * t + h, "dve")
            for n in range(6):
                put(("ct", L, n), n % 4, alt(n))
            if L == 0:
                for n in range(5):
                    put(("flip", n), (2 + n) % 4, "dve")
        else:
            for n in range(3):
                put(("idxT", n), 4 + n, alt(n))
            for h in range(8):
                put(("lg", h), h % 4, "act")
            put(("ckvT",), 7, "act")
            for t in range(TT):
                put(("kd", t), t, "dve")
            for t in range(TT):
                put(("vd", t), 2 + t, "act")
            for n in range(7):
                put(("nT", n), 4 + n % 4, alt(n))
            put(("cmp1",), 7, "dve")
            put(("nT", 7), 5, "dve")
            put(("nT", 8), 6, "act")
            put(("cmp2",), 7, "dve")
        js, held = JOBS[L], []
        for k in range(len(js) + 3):
            if k < len(js):
                put(("s", L, k), 4 + k % 2, "dve")
            if 0 <= k - 2 < len(js):
                put(("pt", L, k - 2), 6 + k % 2, alt(k))
            empties += held
            held = []
            if 0 <= k - 3 < len(js) and js[k - 3].last:
                g = js[k - 3].group
                for t in range(TT):
                    put(("o", L, g, t), OBANK[L][g] + t, "dve", later=True)
                    held.append(("o", L, g, t))
        empties += held
        for n in range(4):
            put(("ht", L, n), 4 + n, alt(n))
        product("y", L)
        if L < 2:
            put(("ada", 2 * L), 7, "dve")
        for n in range(4):
            put(("hT", L, n), 4 + n, alt(n))
        for i in range(11):
            put(("g", L, i), 4 + 2 * (i % 2), "act")
            put(("u", L, i), 5 + 2 * (i % 2), "dve")
        product("d", L)
        if L < 2:
            put(("ada", 2 * L + 1), 7, "dve")
            for n in range(4):
                put(("xT", L + 1, n), 4 + n, alt(n))
    return fills, empties


class Units:

    def __init__(self):
        self.full, self.mine, self.bank, self.eng, self.prev = {}, {}, {}, {}, {}
        counts, last = {"act": 0, "dve": 0}, {}
        fills, empties = plan()
        for n, (key, bank, eng) in enumerate(fills):
            assert key not in self.full, key
            self.full[key], self.bank[key], self.eng[key] = n + 1, bank, eng
            self.prev[key] = last.get(bank)
            last[bank] = ("u",) + key[1:] if key[0] == "g" else key
        for key in empties:
            counts[self.eng[key]] += 1
            self.mine[key] = counts[self.eng[key]]


U = Units()


def stream():
    out = []
    for L in range(3):
        w = IN1 if L < 2 else IN2
        out += [("win", L, i) for i in range(5)]
        out += [("lora", L)] if L < 2 else [("small",), ("w1",)]
        out += [("wo", L, i) for i in range(2)]
        if L < 2:
            out += [("ada", 2 * L, i) for i in range(3)]
        out += [("gu", L, i) for i in range(11)]
        out += [("dn", L, i) for i in range(6)]
        if L < 2:
            out += [("ada", 2 * L + 1, i) for i in range(3)]
    return out


ITEMS = stream()
ITEM = {k: n for n, k in enumerate(ITEMS)}


def dmas_of(item):
    return {"gu": 2, "lora": 2, "small": 3, "w1": 2}.get(item[0], 1)


LANDED = {}
_c = [0] * NSLOT
for _n, _k in enumerate(ITEMS):
    _c[_n % NSLOT] += 16 * dmas_of(_k)
    LANDED[_k] = _c[_n % NSLOT]


def released(item):
    k = item[0]
    if k == "win":
        return ("full", ("win", item[1], item[2], 1))
    if k == "lora":
        return ("full", ("ukv", item[1], 1, 1))
    if k == "gu":
        return ("full", ("u", item[1], item[2]))
    if k == "wo" and item[2] == 1:
        return ("full", ("y", item[1], 1, 1))
    if k == "dn" and item[2] == 5:
        return ("full", ("d", item[1], 1, 1))
    if k == "ada" and item[2] == 2:
        return ("full", ("ada", item[1]))
    if k == "w1":
        return ("full", ("cmp1",))
    if k == "small":
        return ("full", ("cmp2",))
    return ("used", None)


USED = {}
for _k in ITEMS:
    if released(_k)[0] == "used":
        USED[_k] = len(USED) + 1


class Steps:

    def __init__(self, eng, own, done=None, name=None):
        self.eng, self.own, self.done, self.name = eng, own, done, name
        self.n, self.last, self.emptied_n = {}, None, 0

    def go(self, ins, sem=None):
        sem = sem or self.own
        self.n[sem.name] = self.n.get(sem.name, 0) + 1
        ins.then_inc(sem, 1)
        self.last = (sem, self.n[sem.name])
        return self.last

    def settle(self):
        self.eng.wait_ge(*self.last)

    def empty(self, ins, key):
        self.emptied_n += 1
        assert U.mine[key] == self.emptied_n and U.eng[key] == self.name, key
        self.go(ins, self.done)


def program(nc, A, out):
    with ExitStack() as ctx:
        def sb(name, shape):
            return ctx.enter_context(nc.sbuf_tensor(name, shape, F32))

        def sem(name):
            return ctx.enter_context(nc.semaphore(name))

        ps = ctx.enter_context(nc.psum_tensor("ps", [P, 8, 512], F32))
        bias_dram = nc.dram_tensor("bias_rows", [A_H + B_H, 384], F32, kind="Internal").ap()

        ring = sb("ring", [P, NSLOT, SLOTW])
        x = sb("x", [P, TT, D])
        z = sb("z", [P, TT, D])
        xT = sb("xT", [P, KC, S])
        proj = sb("proj", [P, TT, IN2])
        ut = sb("ut", [P, 22, S])
        cbuf = sb("cbuf", [P, TT, 1536])
        cT = sb("cT", [P, 3, S])
        probs = sb("probs", [P, 4, 384])
        pT = sb("pT", [P, 2, 384])
        bias = sb("bias", [P, A_H + B_H, S])
        dmask = sb("dmask", [P, 384])
        lnb = sb("lnb", [P, 2, D])
        tw = sb("tw", [P, TT, 512])
        junk = sb("junk", [P, D])
        cst = sb("cst", [P, NCONST])
        rowsA = sb("rowsA", [P, P])
        rowsB = sb("rowsB", [P, P])
        fv = sb("fv", [P, N_A + N_B])
        modv = sb("modv", [P, 48])
        cact = sb("cact", [P, KC])
        ctmp = sb("ctmp", [P, KC])
        aff = sb("aff", [P, 4, KC])
        ones = sb("ones", [P, P])
        half = sb("half", [P, 8])
        hot = sb("hot", [34, 384])
        relb = sb("relb", [34, A_H + B_H])
        brow = sb("brow", [A_H + B_H, 384])
        nmx = sb("nmx", [P, 4, TT])
        mx = sb("mx", [P, 4, TT])
        sums = sb("sums", [P, 2, TT, 8])
        rec = sb("rec", [P, 2, TT, 8])
        lamin = sb("lamin", [P, DEPTH, 128])
        lamp = sb("lamp", [P, DEPTH, 2])
        neglam = sb("neglam", [P, DEPTH])
        sg = sb("sg", [P, DEPTH, HD])
        st = sb("st", [P, TT, 2, 6])
        mv = sb("mv", [P, TT, 2])
        va = sb("va", [P, TT, 4])
        rs = sb("rs", [P, TT, 4])
        vb = sb("vb", [P, TT, 4])
        rb = sb("rb", [P, TT, 4])
        gt = sb("gt", [P, TT, 24])
        wi = sb("wi", [P, TT, 8])
        m8 = sb("m8", [P, TT, 8])
        hid = sb("hid", [P, 4, 60])
        hb = sb("hb", [P, 2])
        kcmp = sb("kcmp", [P, 16])
        vcmp = sb("vcmp", [P, P])
        b2v = sb("b2v", [P, HD])

        def cv(name):
            a, b = CC[name]
            return cst[:, a:b]

        ident = cv("ident")
        vc = cbuf[:, :, 576:960]
        vd = cbuf[:, :, 512:1024]
        dup = cbuf[:, :, 1024:1536]
        etmp = proj[:, 0, 0:1024].rearrange("p (s n) -> p s n", s=2)
        gtmp = proj[:, 1, 0:1024].rearrange("p (s n) -> p s n", s=2)

        full, done_act, done_dve, used = sem("full"), sem("done_act"), sem("done_dve"), sem("used")
        done = {"act": done_act, "dve": done_dve}
        landed = [sem(f"landed{i}") for i in range(NSLOT)]
        s_const, s_x, s_vec, s_bias_out, s_bias_in, s_out = (sem(n) for n in ("s_const", "s_x", "s_vec", "s_bias_out", "s_bias_in", "s_out"))
        s_lnb = sem("s_lnb")
        probs_ready = sem("probs_ready")
        act_step, dve_step, pool_step = sem("act_step"), sem("dve_step"), sem("pool_step")
        events = {}

        def ev(*name):
            if name not in events:
                events[name] = sem("ev_" + "_".join(map(str, name)))
            return events[name]

        def wait_full(eng, key):
            eng.wait_ge(full, U.full[key])

        def wait_done(eng, key):
            eng.wait_ge(done[U.eng[key]], U.mine[key])

        def mask_of(job, t):
            kind, h = job.mask
            if kind == "bias":
                return bias[:, h, P:S] if t == 0 else bias[:, h, :]
            if kind == "causal":
                return cv("causal")[:, P:S] if t == 0 else cv("causal")
            if kind == "dsa":
                return dmask[:, 0:P] if t == 0 else dmask[:, P:384]
            return cv("cmpmask").rearrange("p (t n) -> p t n", t=TT)[:, t, 0:NCMP]

        def score_cols(job, t):
            if job.kind == "cmp":
                return (16 * t, 16 * t + NCMP)
            return (0, P) if t == 0 else (P, 384)

        def value_of(job, kt):
            kind, a = job.v
            if kind == "proj":
                return proj[:, kt, a:a + HD]
            if kind == "cv":
                return vc[:, kt, a * HD:(a + 1) * HD]
            if kind == "vd":
                return vd[:, kt, a * HD:(a + 1) * HD]
            return vcmp[0:NCMP, a * HD:(a + 1) * HD]

        def win_views(L, i, t, n, b):
            if L == 2 and i == 0:
                return (proj[:, t, 0:512].rearrange("p (r g d) -> p g r d", g=2, d=HD),
                        ps[:, b, 0:512].rearrange("p (g r d) -> p g r d", g=2, d=HD))
            return proj[:, t, 512 * i:512 * i + n], ps[:, b, 0:n]

        def pt_views(L, n):
            b = U.bank[("pt", L, n)]
            if JOBS[L][n].kind == "cmp":
                return pT[0:NCMP, n % 2, 0:S], ps[0:NCMP, b, 0:S]
            return pT[:, n % 2, :], ps[:, b, 0:384]

        def proj_gates(eng):
            wait_done(eng, ("win", 2, 4, 1))
            wait_done(eng, ("win", 2, 4, 0))
            return proj[:, :, NGT:NGT + 24]

        def turned(n):
            s = {0: 0, 1: 2, 2: 4, 3: 6, 4: 12, 7: 8, 8: 10}[n]
            return ut[:, s:s + 2, :], ps[:, U.bank[("nT", n)], :].rearrange("p (c n) -> p c n", c=2)

        def shifted(copy, n, func):
            s = 15 + 2 * (n - 5)
            src = ps[:, U.bank[("nT", n)], :].rearrange("p (c n) -> p c n", c=2)
            copy(ut[0:64, s:s + 2, :], src[0:64], func)
            return copy(ut[64:P, s:s + 2, 0:S - 1], src[64:P, :, 1:S], func)

        block = ctx.enter_context(nc.Block())

        @block.sync
        def _(sp):
            def cols(w, a, n, k=KC):
                return w[:, a:a + n].rearrange("(k p) n -> p k n", p=P)

            def slot(n, a, k, w):
                return ring[:, n % NSLOT, a:a + k * w].rearrange("p (k n) -> p k n", k=k)

            sp.dma_start(x[:, :, :], A["x"][0].rearrange("(t p) d -> p t d", p=P)).then_inc(s_x, 16)
            for n, item in enumerate(ITEMS):
                if n >= NSLOT:
                    how, key = released(ITEMS[n - NSLOT])
                    if how == "full":
                        wait_full(sp, key)
                    else:
                        sp.wait_ge(used, USED[ITEMS[n - NSLOT]])
                got = landed[n % NSLOT]
                kind, L = item[0], item[1] if len(item) > 1 else 2
                if kind == "win":
                    w, width = (A["w_in"][L], IN1) if L < 2 else (A["w_in_2"][0], IN2)
                    m = min(512, width - 512 * item[2])
                    sp.dma_start(slot(n, 0, KC, m), cols(w, 512 * item[2], m)).then_inc(got, 16)
                elif kind == "lora":
                    sp.dma_start(slot(n, 0, 2, 576), cols(A["w_uq"][L], 0, 576)).then_inc(got, 16)
                    sp.dma_start(ring[:, n % NSLOT, 1152:1920], A["w_ukv"][L]).then_inc(got, 16)
                elif kind == "small":
                    sp.dma_start(slot(n, 0, 8, 48), A["w_uk_2"][0].rearrange("h r e -> r h e")).then_inc(got, 16)
                    sp.dma_start(slot(n, 384, 8, 64), A["w_uv_2"][0].rearrange("h r e -> r h e")).then_inc(got, 16)
                    sp.dma_start(slot(n, 896, 2, 64), A["cmp_w2_2"][0].rearrange("v r e -> r v e")).then_inc(got, 16)
                elif kind == "w1":
                    for v in range(2):
                        sp.dma_start(slot(n, 2048 * v, 16, P), A["cmp_w1_2"][0, v].rearrange("(c p) n -> p c n", p=P)).then_inc(got, 16)
                elif kind in ("wo", "dn"):
                    w = {"wo": (A["w_o"], A["w_out_2"]), "dn": (A["w_down"], A["w_down_2"])}[kind]
                    w = w[0][L] if L < 2 else w[1][0]
                    k = min(4, w.shape[0] // P - 4 * item[2])
                    sp.dma_start(slot(n, 0, k, D), w[512 * item[2]:512 * item[2] + P * k, :].rearrange("(k p) n -> p k n", p=P)).then_inc(got, 16)
                elif kind == "ada":
                    sp.dma_start(slot(n, 0, KC, 512), cols(A["w_ada_2"][0], 512 * (3 * L + item[2]), 512)).then_inc(got, 16)
                elif kind == "gu":
                    for v in range(2):
                        if L < 2:
                            src = cols(A[("w_gate", "w_up")[v]][L], 256 * item[2], 256)
                        else:
                            src = cols(A["w_gate_up_2"][0], FF * v + 256 * item[2], 256)
                        sp.dma_start(slot(n, 2048 * v, KC, 256), src).then_inc(got, 16)
            for t in range(TT):
                sp.wait_ge(ev("out_rows", t), 1)
                sp.dma_start(out[0, t * P:(t + 1) * P, :], x[:, t, :]).then_inc(s_out, 16)
            sp.wait_ge(s_out, 32)

        @block.tensor
        def _(pe):
            filled = [0]
            use = [0]

            def fill(ins, key):
                filled[0] += 1
                assert U.full[key] == filled[0], key
                ins.then_inc(full, 1)

            def claim(key):
                if U.prev[key] is not None:
                    wait_done(pe, U.prev[key])
                return U.bank[key]

            def arrive(item):
                pe.wait_ge(landed[ITEM[item] % NSLOT], LANDED[item])
                return ring[:, ITEM[item] % NSLOT, :]

            def leave(ins, item):
                use[0] += 1
                assert USED[item] == use[0]
                ins.then_inc(used, 1)

            mm = nc.tensor.matmul

            def to_columns(name, L, src, wait_rows):
                for t in range(TT):
                    wait_rows(t)
                    for u in range(4):
                        key = (name, L, u)
                        b = claim(key) if t == 0 else U.bank[key]
                        for c in range(2):
                            o = c * S + t * P
                            ins = nc.tensor.transpose(ps[:, b, o:o + P], src[:, t, (2 * u + c) * P:(2 * u + c + 1) * P], ident)
                        if t == 1:
                            fill(ins, key)

            def columns_done(name, L):
                wait_done(pe, (name, L, 2))
                wait_done(pe, (name, L, 3))

            def product_win(L):
                width = IN1 if L < 2 else IN2
                for i in range(5):
                    n = min(512, width - 512 * i)
                    w = arrive(("win", L, i))[:, 0:KC * n].rearrange("p (k n) -> p k n", k=KC)
                    for t in range(TT):
                        b = claim(("win", L, i, t))
                        for k in range(KC):
                            ins = mm(ps[:, b, 0:n], xT[:, k, t * P:(t + 1) * P], w[:, k, :], start=k == 0, stop=k == KC - 1)
                        fill(ins, ("win", L, i, t))

            def product_rows(kind, unit, L, srcT, nk, ready=None):
                ni = -(-nk // 4)
                for t in range(TT):
                    for h in range(2):
                        claim((unit, L, t, h))
                for i in range(ni):
                    w = arrive((kind, L, i)).rearrange("p (k n) -> p k n", k=4)
                    ks = range(4 * i, min(nk, 4 * i + 4))
                    if i < ni - 1:
                        for k in ks:
                            if ready:
                                ready(k)
                            for t in range(TT):
                                for h in range(2):
                                    ins = mm(ps[:, 2 * t + h, :], srcT[:, k, t * P:(t + 1) * P], w[:, k % 4, h * 512:(h + 1) * 512], start=k == 0, stop=False)
                        leave(ins, (kind, L, i))
                    else:
                        if ready:
                            ready(nk - 1)
                        for t in range(TT):
                            for h in range(2):
                                for k in ks:
                                    ins = mm(ps[:, 2 * t + h, :], srcT[:, k, t * P:(t + 1) * P], w[:, k % 4, h * 512:(h + 1) * 512], start=k == 0, stop=k == nk - 1)
                                fill(ins, (unit, L, t, h))

            def ada(q):
                key = ("ada", q)
                b = claim(key)
                for i in range(3):
                    w = arrive(("ada", q, i)).rearrange("p (k n) -> p k n", k=KC)
                    if q == 0 and i == 0:
                        pe.wait_ge(ev("cact"), 1)
                    for c in range(4):
                        for k in range(KC):
                            ins = mm(ps[:, b, 4 * i + c:4 * i + c + 1], w[:, k, c * P:(c + 1) * P], cact[:, k:k + 1], start=k == 0, stop=k == KC - 1)
                    if i < 2:
                        leave(ins, ("ada", q, i))
                    else:
                        fill(ins, key)

            def ffn(L):
                columns_done("hT", L)
                for i in range(11):
                    w = arrive(("gu", L, i)).rearrange("p (v k n) -> p v k n", v=2, k=KC)
                    for v, name in enumerate(("g", "u")):
                        b = claim((name, L, i))
                        for c in range(2):
                            for k in range(KC):
                                ins = mm(ps[:, b, c * S:(c + 1) * S], w[:, v, k, c * P:(c + 1) * P], xT[:, k, :], start=k == 0, stop=k == KC - 1)
                        fill(ins, (name, L, i))
                product_rows("dn", "d", L, ut, FC, ready=lambda k: wait_done(pe, ("u", L, k // 2)))

            def attention(L):
                js = JOBS[L]
                for k in range(len(js) + 3):
                    if k < len(js):
                        j = js[k]
                        b = claim(("s", L, k))
                        if k == 0 and L == 2:
                            wait_done(pe, ("nT", 8))
                            wait_done(pe, ("cmp2",))
                        (qs, qp), kk = j.q, j.kk
                        for t in range(TT):
                            a, e = score_cols(j, t)
                            if j.kind == "cmp":
                                keys = kcmp[qp:qp + kk, 0:NCMP]
                            else:
                                keys = ut[j.k[1]:j.k[1] + kk, j.k[0], 0:(t + 1) * P]
                            ins = mm(ps[:, b, a:e], ut[qp:qp + kk, qs, t * P:(t + 1) * P], keys, start=True, stop=True)
                        fill(ins, ("s", L, k))
                    if 0 <= k - 2 < len(js):
                        j, n = js[k - 2], k - 2
                        b = claim(("pt", L, n))
                        pe.wait_ge(probs_ready, JOB0[L] + n + 1)
                        src = probs[:, n % 4, :]
                        if j.kind == "cmp":
                            for t in range(TT):
                                ins = nc.tensor.transpose(ps[0:NCMP, b, t * P:(t + 1) * P], src[:, 16 * t:16 * t + NCMP], ident)
                        else:
                            for c in range(3):
                                ins = nc.tensor.transpose(ps[:, b, c * P:(c + 1) * P], src[:, c * P:(c + 1) * P], ident)
                        fill(ins, ("pt", L, n))
                    if 0 <= k - 3 < len(js):
                        j, n = js[k - 3], k - 3
                        if n == 0 or js[n - 1].group != j.group:
                            for t in range(TT):
                                claim(("o", L, j.group, t))
                        wait_done(pe, ("pt", L, n))
                        b = OBANK[L][j.group]
                        o = slice(j.col * HD, (j.col + 1) * HD)
                        src = pT[:, n % 2, :]
                        if j.kind == "cmp":
                            for t in range(TT):
                                ins = mm(ps[:, b + t, o], src[0:NCMP, t * P:(t + 1) * P], value_of(j, t), start=True, stop=True)
                                if j.last:
                                    fill(ins, ("o", L, j.group, t))
                        else:
                            ins = mm(ps[:, b, o], src[:, 0:P], value_of(j, 0), start=True, stop=True)
                            if j.last:
                                fill(ins, ("o", L, j.group, 0))
                            mm(ps[:, b + 1, o], src[:, P:S], value_of(j, 0), start=True, stop=False)
                            ins = mm(ps[:, b + 1, o], src[:, S:384], value_of(j, 1), start=False, stop=True)
                            if j.last:
                                fill(ins, ("o", L, j.group, 1))

            pe.wait_ge(s_const, 16 * 4)
            pe.wait_ge(s_vec, 16 * 22)
            for n, (rows, cnt) in enumerate(((rowsA, N_A), (rowsB, N_B))):
                claim(("fv", n))
                fill(nc.tensor.transpose(ps[:, 4 + n, 0:cnt], rows[0:cnt, :], ident[0:cnt, 0:cnt]), ("fv", n))
            claim(("relb",))
            fill(mm(ps[0:A_H + B_H, 6, 0:384], relb[:, :], hot[:, :], start=True, stop=True), ("relb",))
            to_columns("xT", 0, x, lambda t: pe.wait_ge(s_x, 16))

            for L in range(DEPTH):
                columns_done("xT", L)
                product_win(L)
                wait_done(pe, ("win", L, 4, 0))
                wait_done(pe, ("win", L, 4, 1))
                for n in range(5):
                    b = claim(("ab", L, n))
                    for c in range(2):
                        s = 2 * n + c
                        col = s * P if s < 6 else B_Q + (s - 6) * P
                        for t in range(TT):
                            o = c * S + t * P
                            ins = nc.tensor.transpose(ps[:, b, o:o + P], proj[:, t, col:col + P], ident)
                    fill(ins, ("ab", L, n))
                pe.wait_ge(ev("latent", L), 1)
                for n, cs in enumerate(((0, 1), (2,))):
                    b = claim(("c", L, n))
                    for c in cs:
                        for t in range(TT):
                            o = (c % 2) * S + t * P
                            ins = nc.tensor.transpose(ps[:, b, o:o + P], z[:, t, c * P:(c + 1) * P], ident)
                    fill(ins, ("c", L, n))
                w = arrive(("lora", L))
                wait_done(pe, ("c", L, 1))
                for t in range(TT):
                    for h in range(2):
                        b = claim(("uq", L, t, h))
                        for k in range(2):
                            ins = mm(ps[:, b, 0:288], cT[:, k, t * P:(t + 1) * P], w[:, 576 * k + 288 * h:576 * k + 288 * h + 288], start=k == 0, stop=k == 1)
                        fill(ins, ("uq", L, t, h))
                for t in range(TT):
                    for h in range(2):
                        b = claim(("ukv", L, t, h))
                        fill(mm(ps[:, b, 0:384], cT[:, 2, t * P:(t + 1) * P], w[:, 1152 + 384 * h:1536 + 384 * h], start=True, stop=True), ("ukv", L, t, h))
                pe.wait_ge(ev("latent_q", L), 1)
                pe.wait_ge(ev("latent_k", L), 1)
                for n in range(6):
                    b = claim(("ct", L, n))
                    for c in range(2):
                        s = 2 * n + c
                        col = s * CQ if s < 6 else 960 + (s - 6) * CQ
                        for t in range(TT):
                            o = c * S + t * P
                            ins = nc.tensor.transpose(ps[0:CQ, b, o:o + P], cbuf[:, t, col:col + CQ], ident)
                    fill(ins, ("ct", L, n))
                if L == 0:
                    pe.wait_ge(s_bias_in, 16)
                    for n in range(5):
                        b = claim(("flip", n))
                        fill(mm(ps[:, b, :], cv("flip"), bias[:, 2 * n:2 * n + 2, :].rearrange("p h n -> p (h n)"), start=True, stop=True), ("flip", n))
                wait_done(pe, ("ct", L, 4))
                wait_done(pe, ("ct", L, 5))
                attention(L)
                wait_done(pe, ("o", L, 2, 1))
                to_columns("ht", L, z, lambda t: None)
                columns_done("ht", L)
                product_rows("wo", "y", L, xT, KC)
                ada(2 * L)
                to_columns("hT", L, z, lambda t: pe.wait_ge(ev("norm1", L), t + 1))
                ffn(L)
                ada(2 * L + 1)
                to_columns("xT", L + 1, z, lambda t: pe.wait_ge(ev("norm2" if L < 1 else "norm_in", L), t + 1))

            L = 2
            for v in range(2):
                pe.wait_ge(ev("diag", v), 1)
                for h in range(2):
                    b = claim(("G", v, h))
                    for c in range(4):
                        o = (4 * h + c) * P
                        ins = mm(ps[:, b, c * P:(c + 1) * P], ones[:, :], junk[:, o:o + P], start=True, stop=True)
                    fill(ins, ("G", v, h))
            columns_done("xT", L)
            product_win(L)
            pe.wait_ge(ev("idx_rows"), 1)
            for n in range(3):
                b = claim(("idxT", n))
                for c in range(2 if n < 2 else 1):
                    for t in range(TT):
                        o = c * S + t * P
                        src = proj[:, t, IQ + (2 * n + c) * P:IQ + (2 * n + c + 1) * P] if n < 2 else z[:, t, 0:P]
                        ins = nc.tensor.transpose(ps[:, b, o:o + P], src, ident)
                fill(ins, ("idxT", n))
            wait_done(pe, ("idxT", 2))
            wait_done(pe, ("idxT", 1))
            for h in range(8):
                b = claim(("lg", h))
                q = 64 * (h % 2)
                for t in range(TT):
                    ins = mm(ps[:, b, 0:P] if t == 0 else ps[:, b, P:384], ut[q:q + 64, 8 + h // 2, t * P:(t + 1) * P], ut[q:q + 64, 14, 0:(t + 1) * P], start=True, stop=True)
                fill(ins, ("lg", h))
            pe.wait_ge(ev("ckv_rows"), 1)
            b = claim(("ckvT",))
            for t in range(TT):
                ins = nc.tensor.transpose(ps[:, b, t * P:(t + 1) * P], z[:, t, P:S], ident)
            fill(ins, ("ckvT",))
            wait_done(pe, ("ckvT",))
            wsm = arrive(("small",))
            for t in range(TT):
                b = claim(("kd", t))
                fill(mm(ps[:, b, 0:384], cT[:, 0, t * P:(t + 1) * P], wsm[:, 0:384], start=True, stop=True), ("kd", t))
            for t in range(TT):
                b = claim(("vd", t))
                fill(mm(ps[:, b, :], cT[:, 0, t * P:(t + 1) * P], wsm[:, 384:896], start=True, stop=True), ("vd", t))
            pe.wait_ge(ev("rope_rows"), 1)
            rows_at = [(proj, NQ, P), (proj, NQ + 2 * P, P), (proj, DQ, P), (proj, DQ + 2 * P, P), (proj, NKS, NKW - NKS),
                       (cbuf, 1024, P), (cbuf, 1024 + 2 * P, P), (cbuf, 0, P), (cbuf, 2 * P, P)]

            def turn(n):
                src, col, step = rows_at[n]
                b = claim(("nT", n))
                for c in range(2):
                    for t in range(TT):
                        o = c * S + t * P
                        ins = nc.tensor.transpose(ps[:, b, o:o + P], src[:, t, col + c * step:col + c * step + P], ident)
                fill(ins, ("nT", n))

            for n in range(7):
                turn(n)
            wait_done(pe, ("nT", 5))
            wait_done(pe, ("nT", 6))
            w = arrive(("w1",)).rearrange("p (v c n) -> p v c n", v=2, c=16)
            b = claim(("cmp1",))
            for v in range(2):
                for c in range(16):
                    keys = ut[:, 15 + 2 * v:17 + 2 * v, 2 * c:2 * c + 16 * (NCMP - 1) + 1:16]
                    mm(ps[:, b, 32 * v:32 * v + 30].rearrange("p (g n) -> p g n", g=2), w[:, v, c, :], keys, start=c == 0, stop=c == 15)
                for c in range(16):
                    col = FVAT["cmp_pe_2"] + 16 * v + c
                    ins = mm(ps[:, b, 32 * v + 30:32 * v + 31], w[:, v, c, :], fv[:, col:col + 1], start=c == 0, stop=c == 15)
            fill(ins, ("cmp1",))
            pe.wait_ge(ev("dk_rows"), 1)
            turn(7)
            turn(8)
            pe.wait_ge(ev("hidden"), 1)
            b = claim(("cmp2",))
            for g in range(2):
                mm(ps[64 * g:64 * g + 64, b, 0:NCMP], wsm[:, 896:960], hid[:, 3, NCMP * g:NCMP * (g + 1)], start=True, stop=True)
            for g in range(2):
                ins = mm(ps[0:NCMP, b, 64 + 64 * g:128 + 64 * g], hid[:, 3, 30 + NCMP * g:30 + NCMP * (g + 1)], wsm[:, 960:1024], start=True, stop=True)
            fill(ins, ("cmp2",))
            attention(L)
            wait_done(pe, ("o", L, 3, 1))
            to_columns("ht", L, z, lambda t: None)
            columns_done("ht", L)
            product_rows("wo", "y", L, xT, KC)
            to_columns("hT", L, z, lambda t: pe.wait_ge(ev("norm1", L), t + 1))
            ffn(L)

        def affine(name, L, c):
            if name == "xT" and L == 2:
                return aff[:, 0, c:c + 1], modv[:, c:c + 1]
            if name == "hT" and L == 2:
                return aff[:, 1, c:c + 1], modv[:, 24 + c:25 + c]
            k = ("ln2", L - 1) if name == "xT" else ("ln1", L)
            g, b = FVAT[k[0] + "_g"] + 8 * k[1] + c, FVAT[k[0] + "_b"] + 8 * k[1] + c
            return fv[:, g:g + 1], fv[:, b:b + 1]

        @block.scalar
        def _(act):
            me = Steps(act, act_step, done_act, "act")
            activation = nc.scalar.activation

            def copy(dst, src, key):
                wait_full(act, key)
                me.empty(activation(dst, src, ACT.Copy), key)

            def columns(name, L):
                for u in (0, 2):
                    wait_full(act, (name, L, u))
                    b = U.bank[(name, L, u)]
                    if name == "ht" or (name, L) == ("xT", 0):
                        me.empty(activation(xT[:, 2 * u:2 * u + 2, :], ps[:, b, :].rearrange("p (c n) -> p c n", c=2), ACT.Copy), (name, L, u))
                        continue
                    if name == "xT" and L == 2:
                        act.wait_ge(ev("mod"), 1)
                    for c in range(2):
                        g, s = affine(name, L, 2 * u + c)
                        ins = activation(xT[:, 2 * u + c, :], ps[:, b, c * S:(c + 1) * S], ACT.Identity, bias=s, scale=g)
                    me.empty(ins, (name, L, u))

            def win(L):
                width = IN1 if L < 2 else IN2
                for i in range(5):
                    n = min(512, width - 512 * i)
                    b = U.bank[("win", L, i, 0)]
                    copy(*win_views(L, i, 0, n, b), ("win", L, i, 0))

            def softmax(L):
                js = JOBS[L]
                for k in range(len(js) + 3):
                    if k < len(js):
                        j = js[k]
                        wait_done(act, ("s", L, k))
                        for t in range(TT):
                            a, e = score_cols(j, t)
                            ins = activation(probs[:, k % 4, a:e], probs[:, k % 4, a:e], ACT.Exp, bias=nmx[:, k % 4, t:t + 1],
                                             accum_out=sums[:, j.group % 2, t, j.col:j.col + 1])
                        me.go(ins, probs_ready)
                    n = k - 2
                    if 0 <= n < len(js) and alt(n) == "act":
                        copy(*pt_views(L, n), ("pt", L, n))

            def squares(L, unit):
                for t in range(TT):
                    wait_full(act, (unit, L, t, 1))
                    if t == 1:
                        me.settle()
                    me.go(activation(tw[:, :, :], ps[:, 2 * t:2 * t + 2, :], ACT.Square, accum_out=va[:, t, 0:1]), ev("squares", unit))

            def gates(L):
                for i in range(11):
                    key = ("g", L, i)
                    wait_full(act, key)
                    me.empty(activation(etmp[:, i % 2, :], ps[:, U.bank[key], :], ACT.Exp, scale=-1.0), key)

            act.wait_ge(ev("brow"), 1)
            act.dma_start(bias_dram, brow[:, :]).then_inc(s_bias_out, 16)
            act.wait_ge(s_bias_out, 16)
            act.dma_start(bias[:, :, :], bass.AP(bias_dram.tensor, bias_dram.offset, [[1, P], [384, A_H + B_H], [1, S]])).then_inc(s_bias_in, 16)
            act.wait_ge(ev("fv"), 1)
            act.wait_ge(ev("lamsum"), 1)
            me.go(activation(ctmp[:, :], fv[:, FVAT["c_2"]:FVAT["c_2"] + KC], ACT.Exp, scale=-1.0), ev("cexp"))
            me.go(activation(lamp[:, :, :], lamp[:, :, :], ACT.Exp), ev("lamexp"))
            columns("xT", 0)
            for L in range(DEPTH):
                win(L)
                for n in (0, 2, 4):
                    copy(ut[:, 2 * n:2 * n + 2, :], ps[:, U.bank[("ab", L, n)], :].rearrange("p (c n) -> p c n", c=2), ("ab", L, n))
                for n, cs in enumerate(((0, 1), (2,))):
                    key = ("c", L, n)
                    wait_full(act, key)
                    for c in cs:
                        g = FVAT["q_norm_g"] + 2 * L + c if c < 2 else FVAT["kv_norm_g"] + L
                        ins = activation(cT[:, c, :], ps[:, U.bank[key], (c % 2) * S:(c % 2 + 1) * S], ACT.Copy, scale=fv[:, g:g + 1])
                    me.empty(ins, key)
                for t in range(TT):
                    for h in range(2):
                        copy(cbuf[:, t, 288 * h:288 * h + 288], ps[:, U.bank[("uq", L, t, h)], 0:288], ("uq", L, t, h))
                for n in (0, 2, 4):
                    copy(ut[0:CQ, 10 + 2 * n:12 + 2 * n, :], ps[0:CQ, U.bank[("ct", L, n)], :].rearrange("p (c n) -> p c n", c=2), ("ct", L, n))
                softmax(L)
                columns("ht", L)
                columns("hT", L)
                gates(L)
                if L == 1:
                    for t in range(TT):
                        act.wait_ge(ev("resid", 1, 2), t + 1)
                        if t == 1:
                            me.settle()
                        me.go(activation(tw[:, :, :].rearrange("p a b -> p (a b)"), x[:, t, :], ACT.Square, accum_out=va[:, t, 0:1]), ev("squares", "in"))
                columns("xT", L + 1)
            L = 2
            for v in range(2):
                for h in range(2):
                    copy(lnb[:, v, 512 * h:512 * h + 512], ps[:, U.bank[("G", v, h)], :], ("G", v, h))
            win(L)
            me.go(activation(gt[:, :, :], proj_gates(act), ACT.Exp, scale=-1.0), ev("gexp"))
            for n in (0, 2):
                w = 2 if n == 0 else 1
                copy(ut[:, 8 if n == 0 else 14, :] if w == 1 else ut[:, 8:10, :], ps[:, U.bank[("idxT", n)], 0:w * S] if w == 1 else
                     ps[:, U.bank[("idxT", n)], :].rearrange("p (c n) -> p c n", c=2), ("idxT", n))
            for h in range(8):
                if h >= 4:
                    act.wait_ge(ev("idx_added"), h - 3)
                wait_full(act, ("lg", h))
                me.empty(activation(probs[:, h % 4, :], ps[:, U.bank[("lg", h)], 0:384], ACT.Relu), ("lg", h))
            key = ("ckvT",)
            g = FVAT["g_kv_norm_2"]
            wait_full(act, key)
            me.empty(activation(cT[:, 0, :], ps[:, U.bank[key], 0:S], ACT.Copy, scale=fv[:, g:g + 1]), key)
            for t in range(TT):
                copy(vd[:, t, :], ps[:, U.bank[("vd", t)], :], ("vd", t))
            for n in (0, 2, 4, 6):
                if n == 6:
                    wait_full(act, ("nT", n))
                    me.empty(shifted(activation, n, ACT.Copy), ("nT", n))
                else:
                    copy(*turned(n), ("nT", n))
            act.wait_ge(ev("gelu_arg"), 1)
            me.go(activation(hid[:, 2, :], hid[:, 1, :], ACT.Exp, scale=-2.0 * GELU_C), ev("gelu_exp"))
            copy(*turned(8), ("nT", 8))
            softmax(L)
            columns("ht", L)
            squares(L, "y")
            for t in range(TT):
                act.wait_ge(ev("mixed"), t + 1)
                if t == 1:
                    me.settle()
                me.go(activation(tw[:, :, :].rearrange("p a b -> p (a b)"), x[:, t, :], ACT.Square, accum_out=va[:, t, 1:2]), ev("squares", "mid"))
            columns("hT", L)
            gates(L)
            squares(L, "d")

        @block.vector
        def _(dve):
            me = Steps(dve, dve_step, done_dve, "dve")
            V = nc.vector

            def copy(dst, src, key):
                wait_full(dve, key)
                me.empty(V.tensor_copy(dst, src), key)

            def columns(name, L):
                for u in (1, 3):
                    wait_full(dve, (name, L, u))
                    b = U.bank[(name, L, u)]
                    if name == "ht" or (name, L) == ("xT", 0):
                        me.empty(V.tensor_copy(xT[:, 2 * u:2 * u + 2, :], ps[:, b, :].rearrange("p (c n) -> p c n", c=2)), (name, L, u))
                        continue
                    for c in range(2):
                        g, s = affine(name, L, 2 * u + c)
                        ins = V.tensor_scalar(xT[:, 2 * u + c, :], ps[:, b, c * S:(c + 1) * S], g, s, ALU.mult, ALU.add)
                    me.empty(ins, (name, L, u))

            def win(L):
                width = IN1 if L < 2 else IN2
                for i in range(5):
                    n = min(512, width - 512 * i)
                    copy(*win_views(L, i, 1, n, U.bank[("win", L, i, 1)]), ("win", L, i, 1))
                wait_done(dve, ("win", L, 4, 0))
                me.settle()

            def norm(L, unit, ln):
                for t in range(TT):
                    if t == 0:
                        if (L, unit) != (0, "y"):
                            dve.wait_ge(ev("resid", *((L, 1) if unit == "d" else (L - 1, 2))), 2)
                    for h in range(2):
                        key = (unit, L, t, h)
                        wait_full(dve, key)
                        xs = x[:, t, 512 * h:512 * h + 512]
                        me.empty(V.scalar_tensor_tensor(out=xs, in0=xs, scalar=ALPHA, in1=ps[:, U.bank[key], :], op0=ALU.mult, op1=ALU.add), key)
                    me.settle()
                    for h in range(2):
                        me.go(V.bn_stats(st[:, t, h, :], x[:, t, 512 * h:512 * h + 512]))
                    me.settle()
                    me.go(V.bn_aggr(mv[:, t, :], st[:, t, :, :].rearrange("p a b -> p (a b)")))
                    me.settle()
                    me.go(V.tensor_scalar(va[:, t, 0:1], mv[:, t, 1:2], 1e-5, None, ALU.add), ev("var", ln, L))
                    dve.wait_ge(ev("rstd", ln, L), t + 1)
                    me.go(V.tensor_scalar(z[:, t, :], x[:, t, :], mv[:, t, 0:1], rs[:, t, 0:1], ALU.subtract, ALU.mult), ev("norm%d" % ln, L))

            def ada(q):
                key = ("ada", q)
                wait_full(dve, key)
                a = FVAT["b_ada_2"] + 12 * q
                me.empty(V.tensor_tensor(modv[:, 12 * q:12 * q + 12], ps[:, U.bank[key], 0:12], fv[:, a:a + 12], ALU.add), key)

            def ffn(L):
                for i in range(11):
                    key = ("u", L, i)
                    wait_done(dve, ("g", L, i))
                    e = etmp[:, i % 2, :]
                    me.go(V.tensor_scalar(e, e, 1.0, None, ALU.add))
                    me.settle()
                    me.go(V.reciprocal(e, e))
                    me.settle()
                    me.go(V.tensor_tensor(gtmp[:, i % 2, :], ps[:, U.bank[("g", L, i)], :], e, ALU.mult))
                    me.settle()
                    wait_full(dve, key)
                    me.empty(V.tensor_tensor(ut[:, 2 * i:2 * i + 2, :].rearrange("p c n -> p (c n)"), gtmp[:, i % 2, :], ps[:, U.bank[key], :], ALU.mult), key)

            def outputs(L, g):
                gp, n = g % 2, {0: (6, 8, 6), 1: (6, 8, 6), 2: (8, 8, 8, 8)}[L][g]
                kind = GROUPS[L][g]
                r = rec[:, gp, :, 0:n]
                for t in range(TT):
                    wait_full(dve, ("o", L, g, t))
                me.go(V.reciprocal(r, sums[:, gp, :, 0:n]))
                me.settle()
                if kind == "B":
                    me.go(V.tensor_scalar(rec[:, gp, :, 1:8:2], rec[:, gp, :, 1:8:2], neglam[:, L:L + 1], None, ALU.mult))
                    me.settle()
                if kind in ("slc", "win", "cmp"):
                    a = {"cmp": 0, "slc": 8, "win": 16}[kind]
                    me.go(V.tensor_tensor(r, r, gt[:, :, a:a + 8], ALU.mult))
                    me.settle()
                for t in range(TT):
                    key = ("o", L, g, t)
                    o = ps[:, U.bank[key], 0:n * HD].rearrange("p (h d) -> p h d", d=HD)
                    rr = rec[:, gp, t, 0:n].unsqueeze(2).broadcast_to([P, n, HD])
                    dst = {"A": (z, 0), "B": (tw, 0), "C": (z, 640), "slc": (z, 0), "win": (tw, 0), "cmp": (tw, 0), "dsa": (z, 512)}[kind]
                    d = dst[0][:, t, dst[1]:dst[1] + n * HD]
                    ins = V.tensor_tensor(d.rearrange("p (h d) -> p h d", d=HD), o, rr, ALU.mult)
                    if t == 0 or kind not in ("A", "C", "slc", "dsa"):
                        me.empty(ins, key)
                    else:
                        me.empty(ins, key)
                if kind in ("win", "cmp"):
                    me.settle()
                    for t in range(TT):
                        me.go(V.tensor_tensor(z[:, t, 0:512], z[:, t, 0:512], tw[:, t, :], ALU.add))
                    me.settle()
                if kind == "B":
                    me.settle()
                    for t in range(TT):
                        w = tw[:, t, :].rearrange("p (h i d) -> p h i d", i=2, d=HD)
                        me.go(V.tensor_tensor(z[:, t, 384:640].rearrange("p (h d) -> p h d", d=HD), w[:, :, 0, :], w[:, :, 1, :], ALU.add))
                    me.settle()
                    for t in range(TT):
                        me.go(V.tensor_tensor(tw[:, t, 0:256], z[:, t, 384:640], z[:, t, 384:640], ALU.mult))
                    me.settle()
                    for t in range(TT):
                        me.go(V.tensor_reduce(vb[:, t, :], tw[:, t, 0:256].rearrange("p (h d) -> p h d", d=HD), AX.X, ALU.add))
                    me.settle()
                    me.go(V.tensor_scalar(vb[:, :, :], vb[:, :, :], 1.0 / HD, 1e-5, ALU.mult, ALU.add), ev("var_b", L))

            def subnorm(L):
                dve.wait_ge(ev("rstd_b", L), 1)
                for t in range(TT):
                    o = z[:, t, 384:640].rearrange("p (h d) -> p h d", d=HD)
                    me.go(V.tensor_tensor(o, o, rb[:, t, :].unsqueeze(2).broadcast_to([P, B_H, HD]), ALU.mult))
                me.settle()
                for t in range(TT):
                    o = z[:, t, 384:640].rearrange("p (h d) -> p h d", d=HD)
                    me.go(V.tensor_tensor(o, o, sg[:, L, :].unsqueeze(1).broadcast_to([P, B_H, HD]), ALU.mult))

            def softmax(L):
                js = JOBS[L]
                todo = {}
                for k in range(len(js) + 3):
                    if k < len(js):
                        j, key = js[k], ("s", L, k)
                        wait_full(dve, key)
                        for t in range(TT):
                            a, e = score_cols(j, t)
                            me.go(V.tensor_tensor_reduce(out=probs[:, k % 4, a:e], in0=ps[:, U.bank[key], a:e], in1=mask_of(j, t), scale=j.scale,
                                                         scalar=-3.4e38, op0=ALU.add, op1=ALU.max, accum_out=mx[:, k % 4, t:t + 1]))
                        me.settle()
                        me.empty(V.tensor_scalar(nmx[:, k % 4, :], mx[:, k % 4, :], -1.0, None, ALU.mult), key)
                    n = k - 2
                    if 0 <= n < len(js) and alt(n) == "dve":
                        copy(*pt_views(L, n), ("pt", L, n))
                    for f in todo.pop(k, []):
                        f()
                    if 0 <= k - 3 < len(js) and js[k - 3].last:
                        g = js[k - 3].group
                        todo.setdefault(k + 1, []).append(lambda g=g: outputs(L, g))
                        if L < 2 and g == 1:
                            todo.setdefault(k + 3, []).append(lambda: subnorm(L))
                for k in sorted(todo):
                    for f in todo[k]:
                        f()

            def mean_rms(t, unit, col, sem_in, want, out_sem):
                dve.wait_ge(sem_in, want)
                me.go(V.tensor_scalar(va[:, t, col:col + 1], va[:, t, col:col + 1], 1.0 / D, 1e-6, ALU.mult, ALU.add), out_sem)

            def add_gated(L, unit, v, out_ev):
                for t in range(TT):
                    mean_rms(t, unit, 0, ev("squares", unit), t + 1, ev("var_" + unit))
                for t in range(TT):
                    dve.wait_ge(ev("rstd_" + unit), t + 1)
                    for h in range(2):
                        key = (unit, L, t, h)
                        me.empty(V.scalar_tensor_tensor(out=junk[:, 512 * h:512 * h + 512], in0=ps[:, U.bank[key], :], scalar=rs[:, t, 0:1],
                                                        in1=lnb[:, v, 512 * h:512 * h + 512], op0=ALU.mult, op1=ALU.mult), key)
                    me.settle()
                    me.go(V.tensor_tensor(x[:, t, :], x[:, t, :], junk[:, :], ALU.add), out_ev(t))
                    me.settle()

            dve.wait_ge(s_vec, 16 * 22)
            dve.wait_ge(s_const, 16 * 4)
            for l in range(DEPTH):
                v = lamin[:, l, :].rearrange("p (i j d) -> p i j d", i=2, j=2)
                me.go(V.tensor_tensor(junk[:, 64 * l:64 * l + 64].rearrange("p (i d) -> p i d", i=2), v[:, :, 0, :], v[:, :, 1, :], ALU.mult))
            me.settle()
            me.go(V.tensor_reduce(lamp[:, :, :].rearrange("p a b -> p (a b)"), junk[:, 0:128].rearrange("p (i d) -> p i d", d=32), AX.X, ALU.add), ev("lamsum"))
            for n, cnt in enumerate((N_A, N_B)):
                wait_full(dve, ("fv", n))
                me.empty(V.tensor_copy(fv[:, n * N_A:n * N_A + cnt], ps[:, 4 + n, 0:cnt]), ("fv", n))
            me.settle()
            for l in range(DEPTH):
                ins = V.tensor_scalar(sg[:, l, :], sg[:, l, :], 1.0 - LAM0[l], None, ALU.mult)
            me.go(ins, ev("fv"))
            wait_full(dve, ("relb",))
            me.empty(V.tensor_scalar(brow[:, :], ps[0:A_H + B_H, 6, 0:384], cv("biasscale")[0:A_H + B_H, :], None, ALU.mult), ("relb",))
            me.settle()
            me.go(V.tensor_copy(mx[0:1, 0, 0:1], brow[0:1, 0:1]), ev("brow"))
            dve.wait_ge(ev("cexp"), 1)
            me.go(V.tensor_scalar(ctmp[:, :], ctmp[:, :], 1.0, None, ALU.add))
            me.settle()
            me.go(V.reciprocal(ctmp[:, :], ctmp[:, :]))
            me.settle()
            c0 = FVAT["c_2"]
            me.go(V.tensor_tensor(cact[:, :], ctmp[:, :], fv[:, c0:c0 + KC], ALU.mult), ev("cact"))
            dve.wait_ge(ev("lamexp"), 1)
            for l in range(DEPTH):
                me.go(V.tensor_tensor(neglam[:, l:l + 1], lamp[:, l, 1:2], lamp[:, l, 0:1], ALU.subtract))
            me.settle()
            for l in range(DEPTH):
                me.go(V.tensor_scalar(neglam[:, l:l + 1], neglam[:, l:l + 1], -LAM0[l], None, ALU.add))
            columns("xT", 0)

            def rope(xs, c, s, tmp, n, half, dst=None):
                a, b = xs[:, :, :, 0:half], xs[:, :, :, half:2 * half]
                cb, sb_ = (v.unsqueeze(2).broadcast_to([P, TT, n, half]) for v in (c, s))
                w = [tmp[:, i * TT * n * half:(i + 1) * TT * n * half].rearrange("p (t h d) -> p t h d", t=TT, h=n) for i in range(4)]
                for i, (u, v) in enumerate(((a, cb), (b, sb_), (b, cb), (a, sb_))):
                    me.go(V.tensor_tensor(w[i], u, v, ALU.mult))
                me.settle()
                me.go(V.tensor_tensor(a, w[0], w[1], ALU.subtract))
                return V.tensor_tensor(b, w[2], w[3], ALU.add)

            c1, s1, c2, s2 = (cv(n).rearrange("p (t d) -> p t d", t=TT) for n in ("cos1", "sin1", "cos2", "sin2"))
            for L in range(DEPTH):
                win(L)
                for t in range(TT):
                    for i, (a, n) in enumerate(((C_IN, QL), (C_IN + QL, KVL))):
                        v = proj[:, t, a:a + n]
                        me.go(V.tensor_tensor_reduce(out=junk[:, 512 * t + a - C_IN:512 * t + a - C_IN + n], in0=v, in1=v, scale=1.0, scalar=0.0, op0=ALU.mult, op1=ALU.add, accum_out=va[:, t, i:i + 1]))
                me.settle()
                me.go(V.tensor_scalar(va[:, :, 0:1], va[:, :, 0:1], 1.0 / QL, 1e-6, ALU.mult, ALU.add))
                me.go(V.tensor_scalar(va[:, :, 1:2], va[:, :, 1:2], 1.0 / KVL, 1e-6, ALU.mult, ALU.add), ev("var_lat", L))
                copy(ut[:, 2:4, :], ps[:, U.bank[("ab", L, 1)], :].rearrange("p (c n) -> p c n", c=2), ("ab", L, 1))
                copy(ut[:, 6:8, :], ps[:, U.bank[("ab", L, 3)], :].rearrange("p (c n) -> p c n", c=2), ("ab", L, 3))
                if L:
                    dve.wait_ge(ev("resid", L - 1, 2), 2)
                dve.wait_ge(ev("rstd_lat", L), 1)
                for t in range(TT):
                    for i, (a, n) in enumerate(((0, QL), (QL, KVL))):
                        ins = V.tensor_scalar(z[:, t, a:a + n], proj[:, t, C_IN + a:C_IN + a + n], rs[:, t, i:i + 1], None, ALU.mult)
                        me.go(ins, ev("latent", L) if (t, i) == (1, 1) else None)
                kr = proj[:, :, C_KR:C_KR + ROPE].unsqueeze(2)
                me.go(rope(kr, c1, s1, junk, 1, 16))
                for t in range(TT):
                    for h in range(2):
                        key = ("ukv", L, t, h)
                        wait_full(dve, key)
                        src = ps[:, U.bank[key], 0:384].rearrange("p (h d) -> p h d", d=P)
                        me.go(V.tensor_copy(cbuf[:, t, 960 + 288 * h:960 + 288 * h + 288].rearrange("p (h d) -> p h d", d=CQ)[:, :, 0:NOPE], src[:, :, 0:NOPE]))
                        me.empty(V.tensor_copy(vc[:, t, 192 * h:192 * h + 192].rearrange("p (h d) -> p h d", d=HD), src[:, :, NOPE:P]), key)
                me.settle()
                for t in range(TT):
                    ins = V.tensor_copy(cbuf[:, t, 960:1536].rearrange("p (h d) -> p h d", d=CQ)[:, :, NOPE:CQ],
                                        proj[:, t, C_KR:C_KR + ROPE].unsqueeze(1).broadcast_to([P, C_H, ROPE]))
                    me.go(ins, ev("latent_k", L) if t == 1 else None)
                wait_done(dve, ("uq", L, 1, 1))
                q = cbuf[:, :, 0:576].rearrange("p t (h d) -> p t h d", d=CQ)[:, :, :, NOPE:CQ]
                me.go(rope(q, c1, s1, junk, C_H, 16), ev("latent_q", L))
                for n in (1, 3, 5):
                    copy(ut[0:CQ, 10 + 2 * n:12 + 2 * n, :], ps[0:CQ, U.bank[("ct", L, n)], :].rearrange("p (c n) -> p c n", c=2), ("ct", L, n))
                if L == 0:
                    for n in range(5):
                        copy(bias[:, 2 * n:2 * n + 2, :].rearrange("p h n -> p (h n)"), ps[:, U.bank[("flip", n)], :], ("flip", n))
                    me.settle()
                softmax(L)
                columns("ht", L)
                norm(L, "y", 1)
                ada(2 * L)
                columns("hT", L)
                ffn(L)
                norm(L, "d", 2)
                ada(2 * L + 1)
                if L == 1:
                    me.settle()
                    for n, (m, add, g) in enumerate(((8, 1.0, "g_pre_mix_2"), (32, 1.0, "g_pre_ffn_2"), (16, 0.0, "g_post_mix_2"), (40, 0.0, "g_post_ffn_2"))):
                        me.go(V.scalar_tensor_tensor(out=aff[:, n, :], in0=modv[:, m:m + 8], scalar=add, in1=fv[:, FVAT[g]:FVAT[g] + 8], op0=ALU.add, op1=ALU.mult),
                              ev("mod") if n == 3 else None)
                    for t in range(TT):
                        mean_rms(t, "in", 0, ev("squares", "in"), t + 1, ev("var_in"))
                    for t in range(TT):
                        dve.wait_ge(ev("rstd_in"), t + 1)
                        me.go(V.tensor_scalar(z[:, t, :], x[:, t, :], rs[:, t, 0:1], None, ALU.mult), ev("norm_in", 1))
                columns("xT", L + 1)

            L = 2
            me.settle()
            for v in range(2):
                if v:
                    wait_full(dve, ("G", 0, 1))
                for c in range(KC):
                    me.go(V.tensor_scalar(junk[:, c * P:(c + 1) * P], ident, aff[:, 2 + v, c:c + 1], None, ALU.mult), ev("diag", v) if c == KC - 1 else None)
            win(L)

            def rope2(col, n, semaphore=None):
                xs = proj[:, :, col:col + n * HD] if n > 1 else proj[:, :, col:col + R2]
                xs = xs.rearrange("p t (h d) -> p t h d", h=n)[:, :, :, 0:R2]
                me.go(rope(xs, c2, s2, junk, n, R2 // 2), semaphore)

            wait_full(dve, ("G", 1, 1))
            rope2(IQ, 9)
            me.settle()
            me.go(V.tensor_scalar(wi[:, :, :], proj[:, :, IW:IW + 8], 8 ** -0.5 * 64 ** -0.5, None, ALU.mult))
            for i in range(2):
                me.go(V.tensor_copy(z[:, :, 64 * i:64 * i + 64], proj[:, :, IK:IK + 64]), ev("idx_rows") if i else None)
            for t in range(TT):
                v = proj[:, t, DCKV:DCKV + KVL]
                me.go(V.tensor_tensor_reduce(out=tw[:, t, 0:KVL], in0=v, in1=v, scale=1.0, scalar=0.0, op0=ALU.mult, op1=ALU.add, accum_out=va[:, t, 0:1]))
            me.settle()
            me.go(V.tensor_scalar(va[:, :, 0:1], va[:, :, 0:1], 1.0 / KVL, 1e-6, ALU.mult, ALU.add), ev("var_ckv"))
            copy(ut[:, 10:12, :], ps[:, U.bank[("idxT", 1)], :].rearrange("p (c n) -> p c n", c=2), ("idxT", 1))
            dve.wait_ge(ev("rstd_ckv"), 1)
            for t in range(TT):
                me.go(V.tensor_scalar(z[:, t, P:S], proj[:, t, DCKV:DCKV + KVL], rs[:, t, 0:1], None, ALU.mult), ev("ckv_rows") if t else None)
            for col, n in ((NQ, 10), (NKS, 2), (NKW, 2), (DQ, 8), (DKR, 1)):
                me.settle()
                rope2(col, n)
            me.settle()
            for v in range(2):
                for t in range(TT):
                    src = proj[:, t, (NKC, NVC)[v]:(NKC, NVC)[v] + P].rearrange("p (g d) -> p g d", g=2).unsqueeze(2).broadcast_to([P, 2, 2, HD])
                    me.go(V.tensor_copy(dup[:, t, S * v:S * v + S].rearrange("p (g r d) -> p g r d", g=2, r=2), src), ev("rope_rows") if (v, t) == (1, 1) else None)
            dve.wait_ge(ev("gexp"), 1)
            me.go(V.tensor_scalar(gt[:, :, :], gt[:, :, :], 1.0, None, ALU.add))
            me.settle()
            me.go(V.reciprocal(gt[:, :, :], gt[:, :, :]))
            me.settle()
            for t in range(TT):
                me.go(V.tensor_scalar(gt[:, t, 0:8], gt[:, t, 0:8], cv("cmpvalid")[:, t:t + 1], None, ALU.mult))
            for h in range(8):
                wait_done(dve, ("lg", h))
                if h:
                    me.settle()
                for t, (a, e) in enumerate(((0, P), (P, 384))):
                    prev = dmask[:, a:e] if h else (cv("causal")[:, P:S] if t == 0 else cv("causal"))
                    me.go(V.scalar_tensor_tensor(out=dmask[:, a:e], in0=probs[:, h % 4, a:e], scalar=wi[:, t, h:h + 1], in1=prev, op0=ALU.mult, op1=ALU.add),
                          ev("idx_added") if t else None)
            for t in range(TT):
                key = ("kd", t)
                wait_full(dve, key)
                kd = cbuf[:, t, 0:512].rearrange("p (h d) -> p h d", d=HD)
                me.empty(V.tensor_copy(kd[:, :, R2:HD], ps[:, U.bank[key], 0:384].rearrange("p (h d) -> p h d", d=48)), key)
                me.go(V.tensor_copy(kd[:, :, 0:R2], proj[:, t, DKR:DKR + R2].unsqueeze(1).broadcast_to([P, 8, R2])), ev("dk_rows") if t else None)
            for n in (1, 3, 5):
                if n == 5:
                    wait_full(dve, ("nT", n))
                    me.empty(shifted(lambda o, i, f: V.tensor_copy(o, i), n, None), ("nT", n))
                else:
                    copy(*turned(n), ("nT", n))
            key = ("cmp1",)
            b = U.bank[key]
            wait_full(dve, key)
            for v in range(2):
                a = FVAT["cmp_b1_2"] + v
                me.go(V.tensor_tensor(hb[:, v:v + 1], ps[:, b, 32 * v + 30:32 * v + 31], fv[:, a:a + 1], ALU.add))
            me.settle()
            me.go(V.tensor_scalar(hid[:, 0, 0:30], ps[:, b, 0:30], hb[:, 0:1], None, ALU.add))
            me.empty(V.tensor_scalar(hid[:, 0, 30:60], ps[:, b, 32:62], hb[:, 1:2], None, ALU.add), key)
            me.settle()
            me.go(V.tensor_tensor(hid[:, 1, :], hid[:, 0, :], hid[:, 0, :], ALU.mult))
            me.settle()
            me.go(V.tensor_scalar(hid[:, 1, :], hid[:, 1, :], 0.044715, 1.0, ALU.mult, ALU.add))
            me.settle()
            me.go(V.tensor_tensor(hid[:, 1, :], hid[:, 1, :], hid[:, 0, :], ALU.mult), ev("gelu_arg"))
            copy(*turned(7), ("nT", 7))
            dve.wait_ge(ev("gelu_exp"), 1)
            me.go(V.tensor_scalar(hid[:, 2, :], hid[:, 2, :], 1.0, None, ALU.add))
            me.settle()
            me.go(V.reciprocal(hid[:, 2, :], hid[:, 2, :]))
            me.settle()
            me.go(V.tensor_tensor(hid[:, 3, :], hid[:, 2, :], hid[:, 0, :], ALU.mult), ev("hidden"))
            key = ("cmp2",)
            b = U.bank[key]
            wait_full(dve, key)
            me.go(V.tensor_scalar(kcmp[:, 0:NCMP], ps[:, b, 0:NCMP], fv[:, B2K:B2K + 1], None, ALU.add))
            me.empty(V.tensor_tensor(vcmp[0:NCMP, :].rearrange("p (g d) -> p g d", g=2), ps[0:NCMP, b, 64:192].rearrange("p (g d) -> p g d", g=2),
                                     b2v[0:NCMP, :].unsqueeze(1).broadcast_to([NCMP, 2, HD]), ALU.add), key)
            for r in range(TOPK // 8):
                for t, (a, e) in enumerate(((0, P), (P, 384))):
                    me.go(V.max(m8[:, t, :], dmask[:, a:e]))
                me.settle()
                for t, (a, e) in enumerate(((0, P), (P, 384))):
                    me.go(V.match_replace(out=dmask[:, a:e], in_to_replace=m8[:, t, :], in_values=dmask[:, a:e], imm_value=TAKEN))
                me.settle()
            me.go(V.tensor_scalar(dmask[:, :], dmask[:, :], TAKEN / 1.5, NEG, ALU.is_gt, ALU.mult))
            me.settle()
            me.go(V.tensor_tensor(dmask[:, 0:P], dmask[:, 0:P], cv("causal")[:, P:S], ALU.add))
            me.go(V.tensor_tensor(dmask[:, P:384], dmask[:, P:384], cv("causal"), ALU.add))
            me.settle()
            softmax(L)
            columns("ht", L)
            add_gated(L, "y", 0, lambda t: ev("mixed"))
            for t in range(TT):
                mean_rms(t, "mid", 1, ev("squares", "mid"), t + 1, ev("var_mid"))
            for t in range(TT):
                dve.wait_ge(ev("rstd_mid"), t + 1)
                me.go(V.tensor_scalar(z[:, t, :], x[:, t, :], rs[:, t, 1:2], None, ALU.mult), ev("norm1", L))
            columns("hT", L)
            ffn(L)
            add_gated(L, "d", 1, lambda t: ev("out_rows", t))

        @block.gpsimd
        def _(gp):
            me = Steps(gp, pool_step)
            gp.dma_start(cst[:, :], A["consts"]).then_inc(s_const, 16)
            gp.dma_start(hot[:, :], A["hot"]).then_inc(s_const, 16)
            gp.dma_start(relb[0:32, :], A["rel_bias"]).then_inc(s_const, 16)
            gp.dma_start(relb[32:34, :], A["which"]).then_inc(s_const, 16)
            for rows, names, base in ((rowsA, ROWS_A, 0), (rowsB, ROWS_B, N_A)):
                for n, k in names:
                    at = FVAT[n] - base
                    gp.dma_start(rows[at:at + k, :], A["rows_" + n]).then_inc(s_vec, 16)
            for i in range(2):
                gp.dma_start(rowsA[B2K:B2K + 1, 64 * i:64 * i + 64], A["cmp_b2_2"][0, 0:1, :]).then_inc(s_vec, 16)
            for l in range(DEPTH):
                gp.dma_start(lamin[:, l, :], A["diff_lambda"][l].rearrange("a b -> (a b)").partition_broadcast(P)).then_inc(s_vec, 16)
                gp.dma_start(sg[:, l, :], A["subln_g"][l].partition_broadcast(P)).then_inc(s_vec, 16)
            gp.dma_start(b2v[0:NCMP, :], A["cmp_b2_2"][0, 1].partition_broadcast(NCMP)).then_inc(s_vec, 16)
            me.go(gp.memset(ones[:, :], 1.0))
            me.go(gp.memset(half[:, :], -0.5))
            me.settle()
            loads = [0]

            def load_affine(name, l):
                for i, s in enumerate("gb"):
                    gp.dma_start(lnb[:, i, :], A[name + "_" + s][l].partition_broadcast(P)).then_inc(s_lnb, 16)
                loads[0] += 1

            def power(dst, src, wait, value, signal):
                gp.wait_ge(wait, value)
                n = src.shape[-1]
                h = half[:, 0:n] if len(src.shape) == 2 else half[:, 0:2 * n].rearrange("p (a b) -> p a b", a=2)
                gp.tensor_tensor(dst, src, h, ALU.pow).then_inc(signal, 1)

            def residual(L, ln):
                gp.wait_ge(s_lnb, 32 * loads[0])
                for t in range(TT):
                    gp.wait_ge(ev("norm%d" % ln, L), t + 1)
                    me.go(gp.tensor_tensor(x[:, t, :], z[:, t, :], lnb[:, 0, :], ALU.mult))
                    me.settle()
                    me.go(gp.tensor_tensor(x[:, t, :], x[:, t, :], lnb[:, 1, :], ALU.add), ev("resid", L, ln))
                me.settle()

            load_affine("ln1", 0)
            for L in range(DEPTH):
                power(rs[:, :, 0:2], va[:, :, 0:2], ev("var_lat", L), 1, ev("rstd_lat", L))
                power(rb[:, :, :], vb[:, :, :], ev("var_b", L), 1, ev("rstd_b", L))
                for ln in (1, 2):
                    for t in range(TT):
                        power(rs[:, t, 0:1], va[:, t, 0:1], ev("var", ln, L), t + 1, ev("rstd", ln, L))
                    residual(L, ln)
                    if ln == 1:
                        load_affine("ln2", L)
                    elif L == 0:
                        load_affine("ln1", 1)
            for t in range(TT):
                power(rs[:, t, 0:1], va[:, t, 0:1], ev("var_in"), t + 1, ev("rstd_in"))
            power(rs[:, :, 0:1], va[:, :, 0:1], ev("var_ckv"), 1, ev("rstd_ckv"))
            for t in range(TT):
                power(rs[:, t, 0:1], va[:, t, 0:1], ev("var_y"), t + 1, ev("rstd_y"))
            for t in range(TT):
                power(rs[:, t, 1:2], va[:, t, 1:2], ev("var_mid"), t + 1, ev("rstd_mid"))
            for t in range(TT):
                power(rs[:, t, 0:1], va[:, t, 0:1], ev("var_d"), t + 1, ev("rstd_d"))


INPUTS = ["x", "rel_bias", "w_in", "q_norm_g", "kv_norm_g", "w_uq", "w_ukv", "diff_lambda", "subln_g", "w_o", "ln1_g",
          "ln1_b", "ln2_g", "ln2_b", "w_gate", "w_up", "w_down", "c_2", "w_ada_2", "b_ada_2", "g_pre_mix_2",
          "g_post_mix_2", "g_pre_ffn_2", "g_post_ffn_2", "w_in_2", "cmp_pe_2", "cmp_w1_2", "cmp_b1_2", "cmp_w2_2",
          "cmp_b2_2", "g_kv_norm_2", "w_uk_2", "w_uv_2", "w_out_2", "w_gate_up_2", "w_down_2"]


def kernel(**inputs):
    import concourse.bacc as bacc
    from concourse.bass_utils import run_bass_kernel_spmd

    nc = bacc.Bacc("TRN2", target_bir_lowering=False, num_devices=1)
    arrays = {}
    for name in INPUTS:
        arrays[name] = np.ascontiguousarray(inputs[name])
    arrays["consts"], arrays["hot"], arrays["which"] = constants()
    A = {}
    for name, a in arrays.items():
        A[name] = nc.dram_tensor("in_" + name, a.shape, mybir.dt.from_np(a.dtype), kind="ExternalInput").ap()
    for name, k in ROWS_A + ROWS_B:
        ap = A[name]
        A["rows_" + name] = bass.AP(ap.tensor, 0, [[P, k], [1, P]])
    out = nc.dram_tensor("out", (1, S, D), F32, kind="ExternalOutput").ap()
    program(nc, A, out)
    r = run_bass_kernel_spmd(nc, [{"in_" + n: a for n, a in arrays.items()}], core_ids=[0])
    return r.results[0]["out"]
```

```python
import math
from contextlib import ExitStack

import numpy as np
import concourse.bass as bass
from concourse import mybir

F32 = mybir.dt.float32
F32R = mybir.dt.float32r
ALU = mybir.AluOpType
ACT = mybir.ActivationFunctionType
AX = mybir.AxisListType

P, S, TT, D = 128, 256, 2, 1024
KC = D // P
FF = 2816
FC = FF // P
DEPTH = 2
ALPHA = (2 * DEPTH) ** 0.25
HD = 64
A_H, B_H, C_H = 6, 4, 6
BQ = 32
QL, KVL, NOPE, ROPE = 256, 128, 64, 32
CQ = NOPE + ROPE
IN1 = 2336
IN2 = 2544
A_K, A_V = A_H * HD, 2 * A_H * HD
B_Q, B_K, B_V = 1152, 1408, 1664
C_IN = 1920
C_KR = C_IN + QL + KVL
NEG = -1e30
TAKEN = -3e38
NQ, NKC, NVC, NKS, NVS, NKW, NVW, NGT, DQ, DCKV, DKR, IQ, IK, IW = (
    0, 512, 640, 768, 896, 1024, 1152, 1280, 1304, 1816, 1944, 1960, 2472, 2536)
R2 = 16
NCMP = 15
TOPK = 64
SLOTW = 2048
NRAW, NW = 3, 3
NGU = FC
ADA_ATT = {0: (0, 1, 2, 3), 1: (6, 7, 8, 9)}
ADA_NORM = {(0, "y"): 4, (0, "d"): 5, (1, "y"): 10, (1, "d"): 11}
GELU_C = math.sqrt(2.0 / math.pi)
SC_A, SC_B, SC_C = HD ** -0.5, BQ ** -0.5, CQ ** -0.5
LAM0 = [0.8 - 0.6 * math.exp(-0.3 * l) for l in range(DEPTH)]

CC = {}


def _const_layout():
    at = 0
    for name, n in (("ident", P), ("flip", P), ("causal", S), ("cos1", TT * 16), ("sin1", TT * 16), ("cos2", TT * 8),
                    ("sin2", TT * 8), ("cmpmask", TT * 16), ("cmpvalid", TT), ("biasscale", 1)):
        CC[name] = (at, at + n)
        at += n
    return at


NCONST = _const_layout()


def constants():
    c = np.zeros((P, NCONST), np.float32)

    def put(name, value):
        a, b = CC[name]
        c[:, a:b] = np.asarray(value, np.float32).reshape(P, b - a)

    p = np.arange(P)[:, None]
    put("ident", np.eye(P))
    put("flip", np.eye(P)[::-1])
    put("causal", np.where(np.arange(S)[None] <= P + p, 0.0, NEG))
    tok = (np.arange(TT)[None, :] * P + p).astype(np.float32)
    inv1 = (np.float32(10000.0) ** (-np.arange(16, dtype=np.float32) / np.float32(16))).astype(np.float32)
    inv2 = (np.float32(1.0) / (np.float32(500000.0) ** (np.arange(0, R2, 2, dtype=np.float32) / np.float32(R2)))).astype(np.float32)
    for n, inv in (("1", inv1), ("2", inv2)):
        ang = (tok[:, :, None] * inv[None, None, :]).astype(np.float32).astype(np.float64)
        put("cos" + n, np.cos(ang))
        put("sin" + n, np.sin(ang))
    ends = np.arange(16) * 16 + 31
    put("cmpmask", np.where((ends[None, None] <= tok[:, :, None]) & (np.arange(16) < NCMP), 0.0, NEG))
    put("cmpvalid", tok >= 31)
    put("biasscale", np.where(p < A_H, 1 / SC_A, 1 / SC_B))
    d = 255 - np.arange(384)
    pos = np.maximum(d, 1).astype(np.float32)
    large = 16 + (np.log(pos / np.float32(16)) / math.log(2048 / 16) * 16).astype(np.int32)
    bucket = np.where(d < 16, np.maximum(d, 0), np.minimum(large, 31))
    hot = np.zeros((34, 384), np.float32)
    hot[bucket[d >= 0], np.nonzero(d >= 0)[0]] = 1.0
    times = (d <= 128).astype(int) + (d % 4 == 0) + (d % 16 == 0)
    hot[32] = np.where((d >= 0) & (times > 0), np.log(np.maximum(times, 1)), NEG)
    hot[33] = np.where(d >= 0, 0.0, NEG)
    which = np.zeros((2, A_H + B_H), np.float32)
    which[0, :A_H] = 1.0
    which[1, A_H:] = 1.0
    return c, hot, which


ROWS_A = [("ln1_g", 16), ("ln1_b", 16), ("ln2_g", 16), ("ln2_b", 16), ("q_norm_g", 4), ("kv_norm_g", 2),
          ("g_pre_mix_2", 8), ("g_post_mix_2", 8), ("g_pre_ffn_2", 8), ("g_post_ffn_2", 8), ("c_2", 8),
          ("g_kv_norm_2", 1), ("cmp_b1_2", 2)]
ROWS_B = [("b_ada_2", 48), ("cmp_pe_2", 32)]
FVAT = {}
_at = 0
for _rows in (ROWS_A, ROWS_B):
    for _n, _k in _rows:
        FVAT[_n] = _at
        _at += _k
N_A = sum(k for _, k in ROWS_A)
N_B = sum(k for _, k in ROWS_B)
B2K = 113
N_A += 1
for _n, _ in ROWS_B:
    FVAT[_n] += 1


ARENA = 22 * S + TT * IN2 + TT * 1536 + 3 * S + 4 * 384 + 2 * 384 + 384


class Job:
    def __init__(self, kind, q, k, kk, mask, scale, v, col, group, last):
        self.kind, self.q, self.k, self.kk, self.mask, self.scale = kind, q, k, kk, mask, scale
        self.v, self.col, self.group, self.last = v, col, group, last


GROUPS = {0: ["A", "B", "C"], 1: ["A", "B", "C"], 2: ["slc", "win", "cmp", "dsa"]}


def jobs_of(L):
    out = []
    if L < 2:
        for h in range(A_H):
            out.append(Job("A", (h // 2, 64 * (h % 2)), (3 + h // 2, 64 * (h % 2)), 64, ("bias", h), SC_A, ("proj", A_V + h * HD), h, 0, h == 5))
        for h in range(B_H):
            for i in range(2):
                n = 2 * h + i
                out.append(Job("B", (6 + n // 4, 32 * (n % 4)), (8 + n // 4, 32 * (n % 4)), 32, ("bias", A_H + h), SC_B, ("proj", B_V + h * HD), n, 1, n == 7))
        for h in range(C_H):
            out.append(Job("C", (10 + h, 0), (16 + h, 0), CQ, ("causal", 0), SC_C, ("cv", h), h, 2, h == 5))
        return out
    for g, (kind, kslot, v) in enumerate((("slc", 12, NVS), ("win", 13, NVW))):
        for h in range(8):
            out.append(Job(kind, (h % 4, 64 * (h // 4)), (kslot, 64 * (h // 4)), 64, ("causal", 0), SC_A, ("proj", v + 64 * (h // 4)), h, g, h == 7))
    for h in range(8):
        out.append(Job("cmp", (h % 4, 64 * (h // 4)), None, 64, ("cmp", 0), SC_A, ("vcmp", h // 4), h, 2, h == 7))
    for h in range(8):
        out.append(Job("dsa", (4 + h // 2, 64 * (h % 2)), (8 + h // 2, 64 * (h % 2)), 64, ("dsa", 0), SC_A, ("vd", h), h, 3, h == 7))
    return out


JOBS = {L: jobs_of(L) for L in range(3)}
JOB0 = {0: 0, 1: len(JOBS[0]), 2: 2 * len(JOBS[0])}
OBANK = {L: {g: 2 * (g % 2) if L == 2 else 0 for g in range(4)} for L in range(3)}
ADA_STEP = {4 * n + 4: n for n in range(4)}


def alt(n):
    return "act" if n % 2 == 0 else "dve"


def plan():
    fills, empties = [], []

    def put(key, bank, eng, later=False):
        fills.append((key, bank, eng))
        if not later:
            empties.append(key)

    def product(key, L, eng="dve"):
        for t in range(TT):
            for h in range(2):
                put((key, L, t, h), 2 * t + h, eng)

    for n in range(2):
        put(("fv", n), 4 + n, "dve")
    put(("relb",), 6, "dve")
    for n in range(4):
        put(("xT", 0, n), 4 + n, "dve")
    for L in range(3):
        if L == 2:
            for v in range(2):
                for h in range(2):
                    put(("G", v, h), 2 * v + h, "act")
        for i in range(5):
            for t in range(TT):
                put(("win", L, i, t), (2 * i + t) % 4, alt(t))
        if L < 2:
            for n in range(5):
                put(("ab", L, n), 4 + n % 4, alt(n))
            for n in range(2):
                put(("c", L, n), 5 + n, "act")
            product("uq", L, "act")
            for t in range(TT):
                for h in range(2):
                    put(("ukv", L, t, h), 4 + 2 * t + h, "dve")
            for n in range(6):
                put(("ct", L, n), n % 4, alt(n))
            if L == 0:
                for n in range(5):
                    put(("flip", n), (2 + n) % 4, "dve")
        else:
            for n in range(3):
                put(("idxT", n), 4 + n, alt(n))
            for h in range(8):
                put(("lg", h), h % 4, "act")
            put(("ckvT",), 7, "act")
            for t in range(TT):
                put(("kd", t), t, "dve")
            for t in range(TT):
                put(("vd", t), 2 + t, "act")
            for n in range(7):
                put(("nT", n), 4 + n % 4, alt(n))
            put(("cmp1",), 7, "dve")
            put(("nT", 7), 5, "dve")
            put(("nT", 8), 6, "act")
            put(("cmp2",), 7, "dve")
        js, held = JOBS[L], []
        for k in range(len(js) + 3):
            if k < len(js):
                put(("s", L, k), 4 + k % 2, "dve")
            if 0 <= k - 2 < len(js):
                put(("pt", L, k - 2), 6 + k % 2, alt(k))
            empties += held
            held = []
            if 0 <= k - 3 < len(js) and js[k - 3].last:
                g = js[k - 3].group
                for t in range(TT):
                    put(("o", L, g, t), OBANK[L][g] + t, "dve", later=True)
                    held.append(("o", L, g, t))
            if L < 2 and k in ADA_STEP:
                q = ADA_ATT[L][ADA_STEP[k]]
                put(("ada", q), 2 + ADA_STEP[k] % 2, "dve", later=True)
                held.append(("ada", q))
        empties += held
        for n in range(4):
            put(("ht", L, n), 4 + n, "dve")
        product("y", L)
        if L < 2:
            put(("ada", ADA_NORM[L, "y"]), 7, "dve")
        for n in range(4):
            put(("hT", L, n), 4 + n, "act")
        for i in range(NGU):
            put(("gu", L, i), 4 + i % 4, "dve")
        product("d", L)
        if L < 2:
            put(("ada", ADA_NORM[L, "d"]), 7, "dve")
            for n in range(4):
                put(("xT", L + 1, n), 4 + n, "act")
    return fills, empties


class Units:

    def __init__(self):
        self.full, self.mine, self.bank, self.eng, self.prev = {}, {}, {}, {}, {}
        counts, last = {"act": 0, "dve": 0}, {}
        fills, empties = plan()
        for n, (key, bank, eng) in enumerate(fills):
            assert key not in self.full, key
            self.full[key], self.bank[key], self.eng[key] = n + 1, bank, eng
            self.prev[key] = last.get(bank)
            last[bank] = key
        for key in empties:
            counts[self.eng[key]] += 1
            self.mine[key] = counts[self.eng[key]]


U = Units()


def stream():
    out = []
    for L in range(3):
        out += [("win", L, i, h) for i in range(5) for h in range(2)]
        if L < 2:
            out += [("lora", L)] + [("ada", q, h) for q in ADA_ATT[L] for h in range(2)]
        else:
            out += [("small",), ("w1", 0), ("w1", 1)]
        out += [("wo", L, i) for i in range(KC // 2)]
        if L < 2:
            out += [("ada", ADA_NORM[L, "y"], h) for h in range(2)]
        out += [("gu", L, i) for i in range(NGU)]
        out += [("dn", L, i) for i in range(FC // 2)]
        if L < 2:
            out += [("ada", ADA_NORM[L, "d"], h) for h in range(2)]
    return out


ITEMS = stream()
ITEM = {k: n for n, k in enumerate(ITEMS)}
SPLITS = [k for k in ITEMS if k[0] in ("win", "wo", "gu", "dn")]
SPLIT = {k: m for m, k in enumerate(SPLITS)}
WIDTH = {"wo": SLOTW, "gu": SLOTW, "dn": SLOTW}


def win_width(L, i):
    return min(512, (IN1 if L < 2 else IN2) - 512 * i)


def split_width(item):
    return 4 * win_width(item[1], item[2]) if item[0] == "win" else SLOTW


def dmas_of(item):
    return {"gu": 2, "lora": 2, "small": 3}.get(item[0], 1)


LANDED = {}
_c = [0] * NRAW
for _n, _k in enumerate(ITEMS):
    _c[_n % NRAW] += 16 * dmas_of(_k)
    LANDED[_k] = _c[_n % NRAW]


def released(item):
    k = item[0]
    if k == "win" and item[3] == 1:
        return ("full", ("win", item[1], item[2], 1))
    if k == "lora":
        return ("full", ("ukv", item[1], 1, 1))
    if k == "gu":
        return ("full", item)
    if k == "wo" and item[2] == KC // 2 - 1:
        return ("full", ("y", item[1], 1, 1))
    if k == "dn" and item[2] == FC // 2 - 1:
        return ("full", ("d", item[1], 1, 1))
    if k == "ada" and item[2] == 1:
        return ("full", ("ada", item[1]))
    if k == "w1" and item[1] == 1:
        return ("full", ("cmp1",))
    if k == "small":
        return ("full", ("cmp2",))
    return ("used", None)


USED = {}
for _k in ITEMS:
    if released(_k)[0] == "used":
        USED[_k] = len(USED) + 1
COLS = {k: 4 * n for n, k in enumerate((("hT", 0), ("xT", 1), ("hT", 1), ("xT", 2), ("hT", 2)))}


class Steps:

    def __init__(self, eng, own, done=None, name=None):
        self.eng, self.own, self.done, self.name = eng, own, done, name
        self.n, self.last, self.emptied_n = {}, None, 0

    def go(self, ins, sem=None):
        sem = sem or self.own
        self.n[sem.name] = self.n.get(sem.name, 0) + 1
        ins.then_inc(sem, 1)
        self.last = (sem, self.n[sem.name])
        return self.last

    def settle(self):
        self.eng.wait_ge(*self.last)

    def empty(self, ins, key):
        self.emptied_n += 1
        assert U.mine[key] == self.emptied_n and U.eng[key] == self.name, key
        self.go(ins, self.done)


def program(nc, A, out):
    with ExitStack() as ctx:
        def sb(name, shape, dt=F32):
            return ctx.enter_context(nc.sbuf_tensor(name, shape, dt))

        def sem(name):
            return ctx.enter_context(nc.semaphore(name))

        ps = ctx.enter_context(nc.psum_tensor("ps", [P, 8, 512], F32))
        bias_dram = nc.dram_tensor("bias_rows", [A_H + B_H, 384], F32, kind="Internal").ap()

        raw = sb("raw", [P, NRAW, SLOTW])
        wh = sb("wh", [P, NW, SLOTW], F32R)
        wl = sb("wl", [P, NW, SLOTW], F32R)
        x = sb("x", [P, TT, D])
        z = sb("z", [P, TT, D])
        xh = sb("xh", [P, KC, S], F32R)
        xl = sb("xl", [P, KC, S], F32R)
        bias = sb("bias", [P, A_H + B_H, S])
        lnb = sb("lnb", [P, 2, D])
        scratch = sb("scratch", [P, 2, D])
        tw = scratch[:, 0, :].rearrange("p (t n) -> p t n", t=TT)
        junk = scratch[:, 1, :]
        arena = ctx.enter_context(nc.sbuf_tensor("arena", [P, ARENA], F32))
        base = nc.sbuf_base - 4 * ARENA
        place = [base]

        def at(name, shape, dt=F32, where=None):
            n = 4
            for v in shape[1:]:
                n *= v
            start = place[0] if where is None else where
            if where is None:
                place[0] += n
                assert place[0] <= base + 4 * ARENA
            return nc.alloc_sbuf_tensor_at(name, shape, dt, offset=start)

        ut = at("ut", [P, 22, S])
        proj = at("proj", [P, TT, IN2])
        cbuf_at = place[0]
        cbuf = at("cbuf", [P, TT, 1536])
        cT = at("cT", [P, 3, S])
        probs = at("probs", [P, 4, 384])
        pT = at("pT", [P, 2, 384])
        dmask = at("dmask", [P, 384])
        gh = at("gh", [P, FC, S], F32R, base)
        gl = at("gl", [P, FC, S], F32R, base + 4 * FC * S)
        rowsA = at("rowsA", [P, P], F32, cbuf_at)
        rowsB = at("rowsB", [P, P], F32, cbuf_at + 512)
        hot = at("hot", [34, 384], F32, cbuf_at + 1024)
        brow = at("brow", [A_H + B_H, 384], F32, cbuf_at + 1024 + 1536)
        lamin = at("lamin", [P, DEPTH, P], F32, cbuf_at + 4096)
        cst = sb("cst", [P, NCONST])
        fv = sb("fv", [P, N_A + N_B])
        modv = sb("modv", [P, 48])
        cact = sb("cact", [P, KC])
        ctmp = sb("ctmp", [P, KC])
        aff = sb("aff", [P, 4, KC])
        ones = sb("ones", [P, P])
        diagonal = sb("diagonal", [P, 4, P])
        half = sb("half", [P, 8])
        relb = sb("relb", [34, A_H + B_H])
        nmx = sb("nmx", [P, 4, TT])
        mx = sb("mx", [P, 4, TT])
        sums = sb("sums", [P, 2, TT, 8])
        rec = sb("rec", [P, 2, TT, 8])
        lamp = sb("lamp", [P, DEPTH, 2])
        neglam = sb("neglam", [P, DEPTH])
        sg = sb("sg", [P, DEPTH, HD])
        st = sb("st", [P, TT, 2, 6])
        mv = sb("mv", [P, TT, 2])
        va = sb("va", [P, TT, 4])
        rs = sb("rs", [P, TT, 4])
        vb = sb("vb", [P, TT, 4])
        rb = sb("rb", [P, TT, 4])
        gt = sb("gt", [P, TT, 24])
        wi = sb("wi", [P, TT, 8])
        m8 = sb("m8", [P, TT, 8])
        hid = sb("hid", [P, 4, 60])
        hb = sb("hb", [P, 2])
        kcmp = sb("kcmp", [P, 16])
        vcmp = sb("vcmp", [P, P])
        b2v = sb("b2v", [P, HD])

        def cv(name):
            a, b = CC[name]
            return cst[:, a:b]

        ident = cv("ident")
        vc = cbuf[:, :, 576:960]
        vd = cbuf[:, :, 512:1024]
        dup = cbuf[:, :, 1024:1536]
        vcols = scratch[:, :, :].rearrange("p a (b n) -> p (a b) n", b=2)
        gsilu = scratch[:, 0, :].rearrange("p (s n) -> p s n", s=4)
        gated = scratch[:, 1, :].rearrange("p (s n) -> p s n", s=4)

        full, done_act, done_dve, used = sem("full"), sem("done_act"), sem("done_dve"), sem("used")
        done = {"act": done_act, "dve": done_dve}
        landed = [sem(f"landed{i}") for i in range(NRAW)]
        wh_ready, wl_ready, cols_ready, silu_ready, gated_ready = (
            sem(n) for n in ("wh_ready", "wl_ready", "cols_ready", "silu_ready", "gated_ready"))
        s_const, s_x, s_vec, s_bias_out, s_bias_in, s_out = (sem(n) for n in ("s_const", "s_x", "s_vec", "s_bias_out", "s_bias_in", "s_out"))
        s_lnb = sem("s_lnb")
        probs_ready = sem("probs_ready")
        act_step, dve_step, pool_step = sem("act_step"), sem("dve_step"), sem("pool_step")
        events = {}

        def ev(*name):
            if name not in events:
                events[name] = sem("ev_" + "_".join(map(str, name)))
            return events[name]

        def wait_full(eng, key):
            eng.wait_ge(full, U.full[key])

        def wait_done(eng, key):
            eng.wait_ge(done[U.eng[key]], U.mine[key])

        def wait_released(eng, item):
            how, key = released(item)
            if how == "full":
                wait_full(eng, key)
            else:
                eng.wait_ge(used, USED[item])

        def mask_of(job, t):
            kind, h = job.mask
            if kind == "bias":
                return bias[:, h, P:S] if t == 0 else bias[:, h, :]
            if kind == "causal":
                return cv("causal")[:, P:S] if t == 0 else cv("causal")
            if kind == "dsa":
                return dmask[:, 0:P] if t == 0 else dmask[:, P:384]
            return cv("cmpmask").rearrange("p (t n) -> p t n", t=TT)[:, t, 0:NCMP]

        def score_cols(job, t):
            if job.kind == "cmp":
                return (16 * t, 16 * t + NCMP)
            return (0, P) if t == 0 else (P, 384)

        def value_of(job, kt):
            kind, a = job.v
            if kind == "proj":
                return proj[:, kt, a:a + HD]
            if kind == "cv":
                return vc[:, kt, a * HD:(a + 1) * HD]
            if kind == "vd":
                return vd[:, kt, a * HD:(a + 1) * HD]
            return vcmp[0:NCMP, a * HD:(a + 1) * HD]

        def win_views(L, i, t, n, b):
            if L == 2 and i == 0:
                return (proj[:, t, 0:512].rearrange("p (r g d) -> p g r d", g=2, d=HD),
                        ps[:, b, 0:512].rearrange("p (g r d) -> p g r d", g=2, d=HD))
            return proj[:, t, 512 * i:512 * i + n], ps[:, b, 0:n]

        def pt_views(L, n):
            b = U.bank[("pt", L, n)]
            if JOBS[L][n].kind == "cmp":
                return pT[0:NCMP, n % 2, 0:S], ps[0:NCMP, b, 0:S]
            return pT[:, n % 2, :], ps[:, b, 0:384]

        def proj_gates(eng):
            wait_done(eng, ("win", 2, 4, 1))
            wait_done(eng, ("win", 2, 4, 0))
            return proj[:, :, NGT:NGT + 24]

        def turned(n):
            s = {0: 0, 1: 2, 2: 4, 3: 6, 4: 12, 7: 8, 8: 10}[n]
            return ut[:, s:s + 2, :], ps[:, U.bank[("nT", n)], :].rearrange("p (c n) -> p c n", c=2)

        def shifted(copy, n, func):
            s = 15 + 2 * (n - 5)
            src = ps[:, U.bank[("nT", n)], :].rearrange("p (c n) -> p c n", c=2)
            copy(ut[0:64, s:s + 2, :], src[0:64], func)
            return copy(ut[64:P, s:s + 2, 0:S - 1], src[64:P, :, 1:S], func)

        block = ctx.enter_context(nc.Block())

        @block.sync
        def _(sp):
            def cols(w, a, n, k=KC):
                return w[:, a:a + n].rearrange("(k p) n -> p k n", p=P)

            def slot(n, a, k, w):
                return raw[:, n % NRAW, a:a + k * w].rearrange("p (k n) -> p k n", k=k)

            sp.dma_start(x[:, :, :], A["x"][0].rearrange("(t p) d -> p t d", p=P)).then_inc(s_x, 16)
            for n, item in enumerate(ITEMS):
                if n >= NRAW:
                    old = ITEMS[n - NRAW]
                    if old in SPLIT:
                        sp.wait_ge(wl_ready, SPLIT[old] + 1)
                    else:
                        wait_released(sp, old)
                got = landed[n % NRAW]
                kind, L = item[0], item[1] if len(item) > 1 else 2
                if kind == "win":
                    w = A["w_in"][L] if L < 2 else A["w_in_2"][0]
                    m, h = win_width(L, item[2]), item[3]
                    sp.dma_start(slot(n, 0, 4, m), cols(w[512 * h:512 * h + 512, :], 512 * item[2], m)).then_inc(got, 16)
                elif kind == "lora":
                    sp.dma_start(slot(n, 0, 2, 576), cols(A["w_uq"][L], 0, 576)).then_inc(got, 16)
                    sp.dma_start(raw[:, n % NRAW, 1152:1920], A["w_ukv"][L]).then_inc(got, 16)
                elif kind == "small":
                    sp.dma_start(slot(n, 0, 8, 48), A["w_uk_2"][0].rearrange("h r e -> r h e")).then_inc(got, 16)
                    sp.dma_start(slot(n, 384, 8, 64), A["w_uv_2"][0].rearrange("h r e -> r h e")).then_inc(got, 16)
                    sp.dma_start(slot(n, 896, 2, 64), A["cmp_w2_2"][0].rearrange("v r e -> r v e")).then_inc(got, 16)
                elif kind == "w1":
                    sp.dma_start(slot(n, 0, 16, P), A["cmp_w1_2"][0, item[1]].rearrange("(c p) n -> p c n", p=P)).then_inc(got, 16)
                elif kind in ("wo", "dn"):
                    w = {"wo": (A["w_o"], A["w_out_2"]), "dn": (A["w_down"], A["w_down_2"])}[kind]
                    w = w[0][L] if L < 2 else w[1][0]
                    sp.dma_start(slot(n, 0, 2, D), w[S * item[2]:S * item[2] + S, :].rearrange("(k p) n -> p k n", p=P)).then_inc(got, 16)
                elif kind == "ada":
                    w = A["w_ada_2"][0]
                    sp.dma_start(slot(n, 0, 4, 512), cols(w[512 * item[2]:512 * item[2] + 512, :], 512 * item[1], 512)).then_inc(got, 16)
                elif kind == "gu":
                    for v in range(2):
                        if L < 2:
                            src = cols(A[("w_gate", "w_up")[v]][L], P * item[2], P)
                        else:
                            src = cols(A["w_gate_up_2"][0], FF * v + P * item[2], P)
                        sp.dma_start(slot(n, 1024 * v, KC, P), src).then_inc(got, 16)
            for t in range(TT):
                sp.wait_ge(ev("out_rows", t), 1)
                sp.dma_start(out[0, t * P:(t + 1) * P, :], x[:, t, :]).then_inc(s_out, 16)
            sp.wait_ge(s_out, 32)

        @block.tensor
        def _(pe):
            filled = [0]
            use = [0]

            def fill(ins, key):
                filled[0] += 1
                assert U.full[key] == filled[0], key
                ins.then_inc(full, 1)

            def claim(key):
                if U.prev[key] is not None:
                    wait_done(pe, U.prev[key])
                return U.bank[key]

            def arrive(item):
                pe.wait_ge(landed[ITEM[item] % NRAW], LANDED[item])
                return raw[:, ITEM[item] % NRAW, :]

            def parts(item):
                m = SPLIT[item]
                pe.wait_ge(wl_ready, m + 1)
                return wh[:, m % NW, :], wl[:, m % NW, :]

            def columns_ready(name, L, u):
                if U.eng[name, L, u] == "dve":
                    wait_done(pe, (name, L, u))
                else:
                    pe.wait_ge(cols_ready, COLS[name, L] + u + 1)

            def leave(ins, item):
                use[0] += 1
                assert USED[item] == use[0]
                ins.then_inc(used, 1)

            mm = nc.tensor.matmul

            def to_columns(name, L, src, wait_rows):
                for t in range(TT):
                    wait_rows(t)
                    for u in range(4):
                        key = (name, L, u)
                        b = claim(key) if t == 0 else U.bank[key]
                        for c in range(2):
                            o = c * S + t * P
                            ins = nc.tensor.transpose(ps[:, b, o:o + P], src[:, t, (2 * u + c) * P:(2 * u + c + 1) * P], ident)
                        if t == 1:
                            fill(ins, key)

            def product_win(L):
                for i in range(5):
                    n = win_width(L, i)
                    for t in range(TT):
                        claim(("win", L, i, t))
                    for h in range(2):
                        a, b = (w[:, 0:4 * n].rearrange("p (k n) -> p k n", k=4) for w in parts(("win", L, i, h)))
                        for t in range(TT):
                            o = ps[:, U.bank["win", L, i, t], 0:n]
                            for k in range(4):
                                if i == 0 and t == 0 and k % 2 == 0:
                                    columns_ready("xT", L, (4 * h + k) // 2)
                                xs = slice(t * P, (t + 1) * P)
                                mm(o, xh[:, 4 * h + k, xs], a[:, k, :], start=h == k == 0, stop=False)
                                mm(o, xh[:, 4 * h + k, xs], b[:, k, :], start=False, stop=False)
                                ins = mm(o, xl[:, 4 * h + k, xs], a[:, k, :], start=False, stop=h == 1 and k == 3)
                            if h == 1:
                                fill(ins, ("win", L, i, t))
                        if h == 0:
                            leave(ins, ("win", L, i, h))

            def product_rows(kind, unit, L, sh, sl, nk, ready):
                ni = nk // 2
                for t in range(TT):
                    for h in range(2):
                        claim((unit, L, t, h))
                for i in range(ni):
                    a, b = (w.rearrange("p (k n) -> p k n", k=2) for w in parts((kind, L, i)))
                    for t in range(TT):
                        for k in (2 * i, 2 * i + 1):
                            if t == 0:
                                ready(k)
                            xs = slice(t * P, (t + 1) * P)
                            for x3, w3 in ((sh, a), (sh, b), (sl, a)):
                                for h in range(2):
                                    ins = mm(ps[:, 2 * t + h, :], x3[:, k, xs], w3[:, k % 2, h * 512:(h + 1) * 512],
                                             start=k == 0 and w3 is a and x3 is sh, stop=k == nk - 1 and x3 is sl)
                                    if k == nk - 1 and x3 is sl:
                                        fill(ins, (unit, L, t, h))
                    if i < ni - 1:
                        leave(ins, (kind, L, i))

            def ada_steps(qs, bank_of):
                for q in qs:
                    b = bank_of(q)
                    claim(("ada", q))
                    for h in range(2):
                        w = arrive(("ada", q, h)).rearrange("p (k n) -> p k n", k=4)
                        for k in range(4):
                            c = cact[:, 4 * h + k:4 * h + k + 1].broadcast_to([P, P])
                            ins = mm(ps[:, b, :], c, w[:, k, :], start=h == k == 0, stop=h == 1 and k == 3)
                            if k == 3:
                                if h:
                                    fill(ins, ("ada", q))
                                else:
                                    leave(ins, ("ada", q, 0))
                            yield

            def ada_norm(L, unit):
                for _ in ada_steps((ADA_NORM[L, unit],), lambda q: 7):
                    pass

            def ffn(L):
                for i in range(NGU):
                    a, b = (w.rearrange("p (v k n) -> p v k n", v=2, k=KC) for w in parts(("gu", L, i)))
                    bank = claim(("gu", L, i))
                    for v in range(2):
                        o = ps[:, bank, v * S:(v + 1) * S]
                        for k in range(KC):
                            if i == 0 and v == 0 and k % 2 == 0:
                                columns_ready("hT", L, k // 2)
                            mm(o, a[:, v, k, :], xh[:, k, :], start=k == 0, stop=False)
                            mm(o, a[:, v, k, :], xl[:, k, :], start=False, stop=False)
                            ins = mm(o, b[:, v, k, :], xh[:, k, :], start=False, stop=k == KC - 1)
                    fill(ins, ("gu", L, i))
                product_rows("dn", "d", L, gh, gl, FC, lambda k: pe.wait_ge(gated_ready, FC * L + k + 1))

            def attention(L):
                js = JOBS[L]
                filler = ada_steps(ADA_ATT[L], lambda q: 2 + ADA_ATT[L].index(q) % 2) if L < 2 else None
                if L == 0:
                    pe.wait_ge(ev("cact"), 1)
                for k in range(len(js) + 3):
                    if k < len(js):
                        j = js[k]
                        b = claim(("s", L, k))
                        if k == 0 and L == 2:
                            wait_done(pe, ("nT", 8))
                            wait_done(pe, ("cmp2",))
                        (qs, qp), kk = j.q, j.kk
                        for t in range(TT):
                            a, e = score_cols(j, t)
                            if j.kind == "cmp":
                                keys = kcmp[qp:qp + kk, 0:NCMP]
                            else:
                                keys = ut[j.k[1]:j.k[1] + kk, j.k[0], 0:(t + 1) * P]
                            ins = mm(ps[:, b, a:e], ut[qp:qp + kk, qs, t * P:(t + 1) * P], keys, start=True, stop=True)
                        fill(ins, ("s", L, k))
                    if 0 <= k - 2 < len(js):
                        j, n = js[k - 2], k - 2
                        b = claim(("pt", L, n))
                        pe.wait_ge(probs_ready, JOB0[L] + n + 1)
                        src = probs[:, n % 4, :]
                        if j.kind == "cmp":
                            for t in range(TT):
                                ins = nc.tensor.transpose(ps[0:NCMP, b, t * P:(t + 1) * P], src[:, 16 * t:16 * t + NCMP], ident)
                        else:
                            for c in range(3):
                                ins = nc.tensor.transpose(ps[:, b, c * P:(c + 1) * P], src[:, c * P:(c + 1) * P], ident)
                        fill(ins, ("pt", L, n))
                    if 0 <= k - 3 < len(js):
                        j, n = js[k - 3], k - 3
                        if n == 0 or js[n - 1].group != j.group:
                            for t in range(TT):
                                claim(("o", L, j.group, t))
                        wait_done(pe, ("pt", L, n))
                        b = OBANK[L][j.group]
                        o = slice(j.col * HD, (j.col + 1) * HD)
                        src = pT[:, n % 2, :]
                        if j.kind == "cmp":
                            for t in range(TT):
                                ins = mm(ps[:, b + t, o], src[0:NCMP, t * P:(t + 1) * P], value_of(j, t), start=True, stop=True)
                                if j.last:
                                    fill(ins, ("o", L, j.group, t))
                        else:
                            ins = mm(ps[:, b, o], src[:, 0:P], value_of(j, 0), start=True, stop=True)
                            if j.last:
                                fill(ins, ("o", L, j.group, 0))
                            mm(ps[:, b + 1, o], src[:, P:S], value_of(j, 0), start=True, stop=False)
                            ins = mm(ps[:, b + 1, o], src[:, S:384], value_of(j, 1), start=False, stop=True)
                            if j.last:
                                fill(ins, ("o", L, j.group, 1))
                    if filler and 1 <= k <= 16:
                        next(filler)
                        next(filler)

            pe.wait_ge(s_const, 16 * 4)
            pe.wait_ge(s_vec, 16 * 22)
            for n, (rows, cnt) in enumerate(((rowsA, N_A), (rowsB, N_B))):
                claim(("fv", n))
                fill(nc.tensor.transpose(ps[:, 4 + n, 0:cnt], rows[0:cnt, :], ident[0:cnt, 0:cnt]), ("fv", n))
            claim(("relb",))
            fill(mm(ps[0:A_H + B_H, 6, 0:384], relb[:, :], hot[:, :], start=True, stop=True), ("relb",))
            to_columns("xT", 0, x, lambda t: pe.wait_ge(s_x, 16))

            for L in range(DEPTH):
                product_win(L)
                wait_done(pe, ("win", L, 4, 0))
                wait_done(pe, ("win", L, 4, 1))
                for n in range(5):
                    b = claim(("ab", L, n))
                    for c in range(2):
                        s = 2 * n + c
                        col = s * P if s < 6 else B_Q + (s - 6) * P
                        for t in range(TT):
                            o = c * S + t * P
                            ins = nc.tensor.transpose(ps[:, b, o:o + P], proj[:, t, col:col + P], ident)
                    fill(ins, ("ab", L, n))
                pe.wait_ge(ev("latent", L), 1)
                for n, cs in enumerate(((0, 1), (2,))):
                    b = claim(("c", L, n))
                    for c in cs:
                        for t in range(TT):
                            o = (c % 2) * S + t * P
                            ins = nc.tensor.transpose(ps[:, b, o:o + P], z[:, t, c * P:(c + 1) * P], ident)
                    fill(ins, ("c", L, n))
                w = arrive(("lora", L))
                wait_done(pe, ("c", L, 1))
                for t in range(TT):
                    for h in range(2):
                        b = claim(("uq", L, t, h))
                        for k in range(2):
                            ins = mm(ps[:, b, 0:288], cT[:, k, t * P:(t + 1) * P], w[:, 576 * k + 288 * h:576 * k + 288 * h + 288], start=k == 0, stop=k == 1)
                        fill(ins, ("uq", L, t, h))
                for t in range(TT):
                    for h in range(2):
                        b = claim(("ukv", L, t, h))
                        fill(mm(ps[:, b, 0:384], cT[:, 2, t * P:(t + 1) * P], w[:, 1152 + 384 * h:1536 + 384 * h], start=True, stop=True), ("ukv", L, t, h))
                pe.wait_ge(ev("latent_q", L), 1)
                pe.wait_ge(ev("latent_k", L), 1)
                for n in range(6):
                    b = claim(("ct", L, n))
                    for c in range(2):
                        s = 2 * n + c
                        col = s * CQ if s < 6 else 960 + (s - 6) * CQ
                        for t in range(TT):
                            o = c * S + t * P
                            ins = nc.tensor.transpose(ps[0:CQ, b, o:o + P], cbuf[:, t, col:col + CQ], ident)
                    fill(ins, ("ct", L, n))
                if L == 0:
                    pe.wait_ge(s_bias_in, 16)
                    for n in range(5):
                        b = claim(("flip", n))
                        fill(mm(ps[:, b, :], cv("flip"), bias[:, 2 * n:2 * n + 2, :].rearrange("p h n -> p (h n)"), start=True, stop=True), ("flip", n))
                wait_done(pe, ("ct", L, 4))
                wait_done(pe, ("ct", L, 5))
                attention(L)
                wait_done(pe, ("o", L, 2, 1))
                to_columns("ht", L, z, lambda t: None)
                product_rows("wo", "y", L, xh, xl, KC, lambda k: columns_ready("ht", L, k // 2))
                ada_norm(L, "y")
                to_columns("hT", L, z, lambda t: pe.wait_ge(ev("norm1", L), t + 1))
                ffn(L)
                ada_norm(L, "d")
                to_columns("xT", L + 1, z, lambda t: pe.wait_ge(ev("norm2" if L < 1 else "norm_in", L), t + 1))

            L = 2
            for v in range(2):
                pe.wait_ge(ev("diag", v), 1)
                for h in range(2):
                    b = claim(("G", v, h))
                    for c in range(4):
                        o = (4 * h + c) * P
                        ins = mm(ps[:, b, c * P:(c + 1) * P], ones[:, :], junk[:, o:o + P], start=True, stop=True)
                    fill(ins, ("G", v, h))
            product_win(L)
            pe.wait_ge(ev("idx_rows"), 1)
            for n in range(3):
                b = claim(("idxT", n))
                for c in range(2 if n < 2 else 1):
                    for t in range(TT):
                        o = c * S + t * P
                        src = proj[:, t, IQ + (2 * n + c) * P:IQ + (2 * n + c + 1) * P] if n < 2 else z[:, t, 0:P]
                        ins = nc.tensor.transpose(ps[:, b, o:o + P], src, ident)
                fill(ins, ("idxT", n))
            wait_done(pe, ("idxT", 2))
            wait_done(pe, ("idxT", 1))
            for h in range(8):
                b = claim(("lg", h))
                q = 64 * (h % 2)
                for t in range(TT):
                    ins = mm(ps[:, b, 0:P] if t == 0 else ps[:, b, P:384], ut[q:q + 64, 8 + h // 2, t * P:(t + 1) * P], ut[q:q + 64, 14, 0:(t + 1) * P], start=True, stop=True)
                fill(ins, ("lg", h))
            pe.wait_ge(ev("ckv_rows"), 1)
            b = claim(("ckvT",))
            for t in range(TT):
                ins = nc.tensor.transpose(ps[:, b, t * P:(t + 1) * P], z[:, t, P:S], ident)
            fill(ins, ("ckvT",))
            wait_done(pe, ("ckvT",))
            wsm = arrive(("small",))
            for t in range(TT):
                b = claim(("kd", t))
                fill(mm(ps[:, b, 0:384], cT[:, 0, t * P:(t + 1) * P], wsm[:, 0:384], start=True, stop=True), ("kd", t))
            for t in range(TT):
                b = claim(("vd", t))
                fill(mm(ps[:, b, :], cT[:, 0, t * P:(t + 1) * P], wsm[:, 384:896], start=True, stop=True), ("vd", t))
            pe.wait_ge(ev("rope_rows"), 1)
            rows_at = [(proj, NQ, P), (proj, NQ + 2 * P, P), (proj, DQ, P), (proj, DQ + 2 * P, P), (proj, NKS, NKW - NKS),
                       (cbuf, 1024, P), (cbuf, 1024 + 2 * P, P), (cbuf, 0, P), (cbuf, 2 * P, P)]

            def turn(n):
                src, col, step = rows_at[n]
                b = claim(("nT", n))
                for c in range(2):
                    for t in range(TT):
                        o = c * S + t * P
                        ins = nc.tensor.transpose(ps[:, b, o:o + P], src[:, t, col + c * step:col + c * step + P], ident)
                fill(ins, ("nT", n))

            for n in range(7):
                turn(n)
            wait_done(pe, ("nT", 5))
            wait_done(pe, ("nT", 6))
            b = claim(("cmp1",))
            for v in range(2):
                w = arrive(("w1", v)).rearrange("p (c n) -> p c n", c=16)
                for c in range(16):
                    keys = ut[:, 15 + 2 * v:17 + 2 * v, 2 * c:2 * c + 16 * (NCMP - 1) + 1:16]
                    mm(ps[:, b, 32 * v:32 * v + 30].rearrange("p (g n) -> p g n", g=2), w[:, c, :], keys, start=c == 0, stop=c == 15)
                for c in range(16):
                    col = FVAT["cmp_pe_2"] + 16 * v + c
                    ins = mm(ps[:, b, 32 * v + 30:32 * v + 31], w[:, c, :], fv[:, col:col + 1], start=c == 0, stop=c == 15)
                if v == 0:
                    leave(ins, ("w1", 0))
            fill(ins, ("cmp1",))
            pe.wait_ge(ev("dk_rows"), 1)
            turn(7)
            turn(8)
            pe.wait_ge(ev("hidden"), 1)
            b = claim(("cmp2",))
            for g in range(2):
                mm(ps[64 * g:64 * g + 64, b, 0:NCMP], wsm[:, 896:960], hid[:, 3, NCMP * g:NCMP * (g + 1)], start=True, stop=True)
            for g in range(2):
                ins = mm(ps[0:NCMP, b, 64 + 64 * g:128 + 64 * g], hid[:, 3, 30 + NCMP * g:30 + NCMP * (g + 1)], wsm[:, 960:1024], start=True, stop=True)
            fill(ins, ("cmp2",))
            attention(L)
            wait_done(pe, ("o", L, 3, 1))
            to_columns("ht", L, z, lambda t: None)
            product_rows("wo", "y", L, xh, xl, KC, lambda k: columns_ready("ht", L, k // 2))
            to_columns("hT", L, z, lambda t: pe.wait_ge(ev("norm1", L), t + 1))
            ffn(L)

        def affine(name, L, c):
            if name == "xT" and L == 2:
                return aff[:, 0, c:c + 1], modv[:, c:c + 1]
            if name == "hT" and L == 2:
                return aff[:, 1, c:c + 1], modv[:, 24 + c:25 + c]
            k = ("ln2", L - 1) if name == "xT" else ("ln1", L)
            g, b = FVAT[k[0] + "_g"] + 8 * k[1] + c, FVAT[k[0] + "_b"] + 8 * k[1] + c
            return fv[:, g:g + 1], fv[:, b:b + 1]

        def feed(split, item, kind):
            m = SPLIT[item] + NW
            if m < len(SPLITS) and SPLITS[m][0] in kind:
                split(SPLITS[m])

        def start(split, kind, L, n=NW):
            m = SPLIT[(kind, L, 0, 0) if kind == "win" else (kind, L, 0)]
            for k in SPLITS[m:m + n]:
                split(k)

        @block.scalar
        def _(act):
            me = Steps(act, act_step, done_act, "act")
            activation = nc.scalar.activation

            def copy(dst, src, key):
                wait_full(act, key)
                me.empty(activation(dst, src, ACT.Copy), key)

            def split(item):
                m = SPLIT[item]
                if m >= NW:
                    wait_released(act, SPLITS[m - NW])
                act.wait_ge(landed[ITEM[item] % NRAW], LANDED[item])
                n = split_width(item)
                me.go(activation(wh[:, m % NW, 0:n], raw[:, ITEM[item] % NRAW, 0:n], ACT.Copy), wh_ready)

            def columns(name, L):
                if name == "xT" and L == 2:
                    act.wait_ge(ev("mod"), 1)
                for u in range(4):
                    key = (name, L, u)
                    wait_full(act, key)
                    b = U.bank[key]
                    if U.eng[key] == "dve":
                        me.go(activation(xh[:, 2 * u:2 * u + 2, :], ps[:, b, :].rearrange("p (c n) -> p c n", c=2), ACT.Copy), ev("upper"))
                        continue
                    for c in range(2):
                        g, s = affine(name, L, 2 * u + c)
                        ins = activation(vcols[:, u, c * S:(c + 1) * S], ps[:, b, c * S:(c + 1) * S], ACT.Identity, bias=s, scale=g)
                    me.empty(ins, key)

            def win(L):
                for i in range(5):
                    for h in range(2):
                        feed(split, ("win", L, i, h), "win")
                    copy(*win_views(L, i, 0, win_width(L, i), U.bank[("win", L, i, 0)]), ("win", L, i, 0))

            def softmax(L):
                js = JOBS[L]
                for k in range(len(js) + 3):
                    if k < len(js):
                        j = js[k]
                        wait_done(act, ("s", L, k))
                        for t in range(TT):
                            a, e = score_cols(j, t)
                            ins = activation(probs[:, k % 4, a:e], probs[:, k % 4, a:e], ACT.Exp, bias=nmx[:, k % 4, t:t + 1],
                                             accum_out=sums[:, j.group % 2, t, j.col:j.col + 1])
                        me.go(ins, probs_ready)
                    n = k - 2
                    if 0 <= n < len(js) and alt(n) == "act":
                        copy(*pt_views(L, n), ("pt", L, n))

            def squares(L, unit):
                for t in range(TT):
                    wait_full(act, (unit, L, t, 1))
                    if t == 1:
                        me.settle()
                    me.go(activation(tw[:, :, :], ps[:, 2 * t:2 * t + 2, :], ACT.Square, accum_out=va[:, t, 0:1]), ev("squares", unit))

            def gates(L):
                for i in range(NGU):
                    feed(split, ("gu", L, i), ("gu", "dn"))
                    key = ("gu", L, i)
                    wait_full(act, key)
                    me.go(activation(gsilu[:, i % 4, :], ps[:, U.bank[key], 0:S], ACT.Silu), silu_ready)
                for i in range(FC // 2):
                    feed(split, ("dn", L, i), "dn")

            def products_wo(L):
                start(split, "wo", L)
                for i in range(KC // 2):
                    feed(split, ("wo", L, i), "wo")

            start(split, "win", 0)
            act.wait_ge(ev("brow"), 1)
            act.dma_start(bias_dram, brow[:, :]).then_inc(s_bias_out, 16)
            act.wait_ge(s_bias_out, 16)
            act.dma_start(bias[:, :, :], bass.AP(bias_dram.tensor, bias_dram.offset, [[1, P], [384, A_H + B_H], [1, S]])).then_inc(s_bias_in, 16)
            act.wait_ge(ev("fv"), 1)
            act.wait_ge(ev("lamsum"), 1)
            me.go(activation(ctmp[:, :], fv[:, FVAT["c_2"]:FVAT["c_2"] + KC], ACT.Exp, scale=-1.0), ev("cexp"))
            me.go(activation(lamp[:, :, :], lamp[:, :, :], ACT.Exp), ev("lamexp"))
            columns("xT", 0)
            for L in range(DEPTH):
                win(L)
                for n in (0, 2, 4):
                    copy(ut[:, 2 * n:2 * n + 2, :], ps[:, U.bank[("ab", L, n)], :].rearrange("p (c n) -> p c n", c=2), ("ab", L, n))
                for n, cs in enumerate(((0, 1), (2,))):
                    key = ("c", L, n)
                    wait_full(act, key)
                    for c in cs:
                        g = FVAT["q_norm_g"] + 2 * L + c if c < 2 else FVAT["kv_norm_g"] + L
                        ins = activation(cT[:, c, :], ps[:, U.bank[key], (c % 2) * S:(c % 2 + 1) * S], ACT.Copy, scale=fv[:, g:g + 1])
                    me.empty(ins, key)
                for t in range(TT):
                    for h in range(2):
                        copy(cbuf[:, t, 288 * h:288 * h + 288], ps[:, U.bank[("uq", L, t, h)], 0:288], ("uq", L, t, h))
                for n in (0, 2, 4):
                    copy(ut[0:CQ, 10 + 2 * n:12 + 2 * n, :], ps[0:CQ, U.bank[("ct", L, n)], :].rearrange("p (c n) -> p c n", c=2), ("ct", L, n))
                softmax(L)
                columns("ht", L)
                products_wo(L)
                start(split, "gu", L)
                columns("hT", L)
                gates(L)
                start(split, "win", L + 1)
                if L == 1:
                    for t in range(TT):
                        act.wait_ge(ev("resid", 1, 2), t + 1)
                        if t == 1:
                            me.settle()
                        me.go(activation(tw[:, :, :].rearrange("p a b -> p (a b)"), x[:, t, :], ACT.Square, accum_out=va[:, t, 0:1]), ev("squares", "in"))
                columns("xT", L + 1)
            L = 2
            for v in range(2):
                for h in range(2):
                    copy(lnb[:, v, 512 * h:512 * h + 512], ps[:, U.bank[("G", v, h)], :], ("G", v, h))
            win(L)
            me.go(activation(gt[:, :, :], proj_gates(act), ACT.Exp, scale=-1.0), ev("gexp"))
            for n in (0, 2):
                w = 2 if n == 0 else 1
                copy(ut[:, 8 if n == 0 else 14, :] if w == 1 else ut[:, 8:10, :], ps[:, U.bank[("idxT", n)], 0:w * S] if w == 1 else
                     ps[:, U.bank[("idxT", n)], :].rearrange("p (c n) -> p c n", c=2), ("idxT", n))
            for h in range(8):
                if h >= 4:
                    act.wait_ge(ev("idx_added"), h - 3)
                wait_full(act, ("lg", h))
                me.empty(activation(probs[:, h % 4, :], ps[:, U.bank[("lg", h)], 0:384], ACT.Relu), ("lg", h))
            key = ("ckvT",)
            g = FVAT["g_kv_norm_2"]
            wait_full(act, key)
            me.empty(activation(cT[:, 0, :], ps[:, U.bank[key], 0:S], ACT.Copy, scale=fv[:, g:g + 1]), key)
            for t in range(TT):
                copy(vd[:, t, :], ps[:, U.bank[("vd", t)], :], ("vd", t))
            for n in (0, 2, 4, 6):
                if n == 6:
                    wait_full(act, ("nT", n))
                    me.empty(shifted(activation, n, ACT.Copy), ("nT", n))
                else:
                    copy(*turned(n), ("nT", n))
            act.wait_ge(ev("gelu_arg"), 1)
            me.go(activation(hid[:, 2, :], hid[:, 1, :], ACT.Exp, scale=-2.0 * GELU_C), ev("gelu_exp"))
            copy(*turned(8), ("nT", 8))
            softmax(L)
            columns("ht", L)
            products_wo(L)
            start(split, "gu", L)
            squares(L, "y")
            for t in range(TT):
                act.wait_ge(ev("mixed"), t + 1)
                if t == 1:
                    me.settle()
                me.go(activation(tw[:, :, :].rearrange("p a b -> p (a b)"), x[:, t, :], ACT.Square, accum_out=va[:, t, 1:2]), ev("squares", "mid"))
            columns("hT", L)
            gates(L)
            squares(L, "d")

        @block.vector
        def _(dve):
            me = Steps(dve, dve_step, done_dve, "dve")
            V = nc.vector

            def copy(dst, src, key):
                wait_full(dve, key)
                me.empty(V.tensor_copy(dst, src), key)

            def split(item):
                m = SPLIT[item]
                dve.wait_ge(wh_ready, m + 1)
                n = split_width(item)
                me.go(V.tensor_tensor(wl[:, m % NW, 0:n], raw[:, ITEM[item] % NRAW, 0:n], wh[:, m % NW, 0:n].bitcast(F32), ALU.subtract), wl_ready)

            uppers = [0]

            def columns(name, L):
                for u in range(4):
                    key = (name, L, u)
                    a, b = xh[:, 2 * u:2 * u + 2, :], xl[:, 2 * u:2 * u + 2, :]
                    if U.eng[key] == "dve":
                        uppers[0] += 1
                        dve.wait_ge(ev("upper"), uppers[0])
                        src = ps[:, U.bank[key], :].rearrange("p (c n) -> p c n", c=2)
                        me.empty(V.tensor_tensor(b, src, a.bitcast(F32), ALU.subtract), key)
                        continue
                    wait_done(dve, key)
                    v = vcols[:, u, :].rearrange("p (c n) -> p c n", c=2)
                    me.go(V.tensor_copy(a, v))
                    me.settle()
                    me.go(V.tensor_tensor(b, v, a.bitcast(F32), ALU.subtract), cols_ready)

            def win(L):
                for i in range(5):
                    for h in range(2):
                        feed(split, ("win", L, i, h), "win")
                    copy(*win_views(L, i, 1, win_width(L, i), U.bank[("win", L, i, 1)]), ("win", L, i, 1))
                wait_done(dve, ("win", L, 4, 0))
                me.settle()

            def norm(L, unit, ln):
                for t in range(TT):
                    if t == 0:
                        if (L, unit) != (0, "y"):
                            dve.wait_ge(ev("resid", *((L, 1) if unit == "d" else (L - 1, 2))), 2)
                    for h in range(2):
                        key = (unit, L, t, h)
                        wait_full(dve, key)
                        xs = x[:, t, 512 * h:512 * h + 512]
                        me.empty(V.scalar_tensor_tensor(out=xs, in0=xs, scalar=ALPHA, in1=ps[:, U.bank[key], :], op0=ALU.mult, op1=ALU.add), key)
                    me.settle()
                    for h in range(2):
                        me.go(V.bn_stats(st[:, t, h, :], x[:, t, 512 * h:512 * h + 512]))
                    me.settle()
                    me.go(V.bn_aggr(mv[:, t, :], st[:, t, :, :].rearrange("p a b -> p (a b)")))
                    me.settle()
                    me.go(V.tensor_scalar(va[:, t, 0:1], mv[:, t, 1:2], 1e-5, None, ALU.add), ev("var", ln, L))
                    dve.wait_ge(ev("rstd", ln, L), t + 1)
                    me.go(V.tensor_scalar(z[:, t, :], x[:, t, :], mv[:, t, 0:1], rs[:, t, 0:1], ALU.subtract, ALU.mult), ev("norm%d" % ln, L))

            def ada(q):
                key = ("ada", q)
                wait_full(dve, key)
                for c in range(4):
                    ins = V.tensor_tensor_reduce(out=diagonal[:, c, :], in0=ps[:, U.bank[key], c * P:(c + 1) * P], in1=ident, scale=1.0, scalar=0.0,
                                                 op0=ALU.mult, op1=ALU.add, accum_out=modv[:, 4 * q + c:4 * q + c + 1])
                    if c < 3:
                        me.go(ins)
                me.empty(ins, key)
                me.settle()

            def ffn(L):
                for i in range(NGU):
                    feed(split, ("gu", L, i), ("gu", "dn"))
                    key = ("gu", L, i)
                    dve.wait_ge(silu_ready, NGU * L + i + 1)
                    g = gated[:, i % 4, :]
                    me.empty(V.tensor_tensor(g, gsilu[:, i % 4, :], ps[:, U.bank[key], S:2 * S], ALU.mult), key)
                    me.settle()
                    me.go(V.tensor_copy(gh[:, i, :], g))
                    me.settle()
                    me.go(V.tensor_tensor(gl[:, i, :], g, gh[:, i, :].bitcast(F32), ALU.subtract), gated_ready)
                for i in range(FC // 2):
                    feed(split, ("dn", L, i), "dn")

            def products_wo(L):
                start(split, "wo", L)
                for i in range(KC // 2):
                    feed(split, ("wo", L, i), "wo")

            def outputs(L, g):
                gp, n = g % 2, {0: (6, 8, 6), 1: (6, 8, 6), 2: (8, 8, 8, 8)}[L][g]
                kind = GROUPS[L][g]
                r = rec[:, gp, :, 0:n]
                for t in range(TT):
                    wait_full(dve, ("o", L, g, t))
                me.go(V.reciprocal(r, sums[:, gp, :, 0:n]))
                me.settle()
                if kind == "B":
                    me.go(V.tensor_scalar(rec[:, gp, :, 1:8:2], rec[:, gp, :, 1:8:2], neglam[:, L:L + 1], None, ALU.mult))
                    me.settle()
                if kind in ("slc", "win", "cmp"):
                    a = {"cmp": 0, "slc": 8, "win": 16}[kind]
                    me.go(V.tensor_tensor(r, r, gt[:, :, a:a + 8], ALU.mult))
                    me.settle()
                for t in range(TT):
                    key = ("o", L, g, t)
                    o = ps[:, U.bank[key], 0:n * HD].rearrange("p (h d) -> p h d", d=HD)
                    rr = rec[:, gp, t, 0:n].unsqueeze(2).broadcast_to([P, n, HD])
                    dst = {"A": (z, 0), "B": (tw, 0), "C": (z, 640), "slc": (z, 0), "win": (tw, 0), "cmp": (tw, 0), "dsa": (z, 512)}[kind]
                    d = dst[0][:, t, dst[1]:dst[1] + n * HD]
                    ins = V.tensor_tensor(d.rearrange("p (h d) -> p h d", d=HD), o, rr, ALU.mult)
                    if t == 0 or kind not in ("A", "C", "slc", "dsa"):
                        me.empty(ins, key)
                    else:
                        me.empty(ins, key)
                if kind in ("win", "cmp"):
                    me.settle()
                    for t in range(TT):
                        me.go(V.tensor_tensor(z[:, t, 0:512], z[:, t, 0:512], tw[:, t, :], ALU.add))
                    me.settle()
                if kind == "B":
                    me.settle()
                    for t in range(TT):
                        w = tw[:, t, :].rearrange("p (h i d) -> p h i d", i=2, d=HD)
                        me.go(V.tensor_tensor(z[:, t, 384:640].rearrange("p (h d) -> p h d", d=HD), w[:, :, 0, :], w[:, :, 1, :], ALU.add))
                    me.settle()
                    for t in range(TT):
                        me.go(V.tensor_tensor(tw[:, t, 0:256], z[:, t, 384:640], z[:, t, 384:640], ALU.mult))
                    me.settle()
                    for t in range(TT):
                        me.go(V.tensor_reduce(vb[:, t, :], tw[:, t, 0:256].rearrange("p (h d) -> p h d", d=HD), AX.X, ALU.add))
                    me.settle()
                    me.go(V.tensor_scalar(vb[:, :, :], vb[:, :, :], 1.0 / HD, 1e-5, ALU.mult, ALU.add), ev("var_b", L))

            def subnorm(L):
                dve.wait_ge(ev("rstd_b", L), 1)
                for t in range(TT):
                    o = z[:, t, 384:640].rearrange("p (h d) -> p h d", d=HD)
                    me.go(V.tensor_tensor(o, o, rb[:, t, :].unsqueeze(2).broadcast_to([P, B_H, HD]), ALU.mult))
                me.settle()
                for t in range(TT):
                    o = z[:, t, 384:640].rearrange("p (h d) -> p h d", d=HD)
                    me.go(V.tensor_tensor(o, o, sg[:, L, :].unsqueeze(1).broadcast_to([P, B_H, HD]), ALU.mult))

            def softmax(L):
                js = JOBS[L]
                todo = {}
                for k in range(len(js) + 3):
                    if k < len(js):
                        j, key = js[k], ("s", L, k)
                        wait_full(dve, key)
                        for t in range(TT):
                            a, e = score_cols(j, t)
                            me.go(V.tensor_tensor_reduce(out=probs[:, k % 4, a:e], in0=ps[:, U.bank[key], a:e], in1=mask_of(j, t), scale=j.scale,
                                                         scalar=-3.4e38, op0=ALU.add, op1=ALU.max, accum_out=mx[:, k % 4, t:t + 1]))
                        me.settle()
                        me.empty(V.tensor_scalar(nmx[:, k % 4, :], mx[:, k % 4, :], -1.0, None, ALU.mult), key)
                    n = k - 2
                    if 0 <= n < len(js) and alt(n) == "dve":
                        copy(*pt_views(L, n), ("pt", L, n))
                    for f in todo.pop(k, []):
                        f()
                    if 0 <= k - 3 < len(js) and js[k - 3].last:
                        g = js[k - 3].group
                        todo.setdefault(k + 1, []).append(lambda g=g: outputs(L, g))
                        if L < 2 and g == 1:
                            todo.setdefault(k + 3, []).append(lambda: subnorm(L))
                    if L < 2 and k in ADA_STEP:
                        todo.setdefault(k + 1, []).append(lambda q=ADA_ATT[L][ADA_STEP[k]]: ada(q))
                for k in sorted(todo):
                    for f in todo[k]:
                        f()

            def mean_rms(t, unit, col, sem_in, want, out_sem):
                dve.wait_ge(sem_in, want)
                me.go(V.tensor_scalar(va[:, t, col:col + 1], va[:, t, col:col + 1], 1.0 / D, 1e-6, ALU.mult, ALU.add), out_sem)

            def add_gated(L, unit, v, out_ev):
                for t in range(TT):
                    mean_rms(t, unit, 0, ev("squares", unit), t + 1, ev("var_" + unit))
                for t in range(TT):
                    dve.wait_ge(ev("rstd_" + unit), t + 1)
                    for h in range(2):
                        key = (unit, L, t, h)
                        me.empty(V.scalar_tensor_tensor(out=junk[:, 512 * h:512 * h + 512], in0=ps[:, U.bank[key], :], scalar=rs[:, t, 0:1],
                                                        in1=lnb[:, v, 512 * h:512 * h + 512], op0=ALU.mult, op1=ALU.mult), key)
                    me.settle()
                    me.go(V.tensor_tensor(x[:, t, :], x[:, t, :], junk[:, :], ALU.add), out_ev(t))
                    me.settle()

            dve.wait_ge(s_vec, 16 * 22)
            dve.wait_ge(s_const, 16 * 4)
            for l in range(DEPTH):
                v = lamin[:, l, :].rearrange("p (i j d) -> p i j d", i=2, j=2)
                me.go(V.tensor_tensor(junk[:, 64 * l:64 * l + 64].rearrange("p (i d) -> p i d", i=2), v[:, :, 0, :], v[:, :, 1, :], ALU.mult))
            me.settle()
            start(split, "win", 0)
            me.go(V.tensor_reduce(lamp[:, :, :].rearrange("p a b -> p (a b)"), junk[:, 0:128].rearrange("p (i d) -> p i d", d=32), AX.X, ALU.add), ev("lamsum"))
            for n, cnt in enumerate((N_A, N_B)):
                wait_full(dve, ("fv", n))
                me.empty(V.tensor_copy(fv[:, n * N_A:n * N_A + cnt], ps[:, 4 + n, 0:cnt]), ("fv", n))
            me.settle()
            for l in range(DEPTH):
                ins = V.tensor_scalar(sg[:, l, :], sg[:, l, :], 1.0 - LAM0[l], None, ALU.mult)
            me.go(ins, ev("fv"))
            wait_full(dve, ("relb",))
            me.empty(V.tensor_scalar(brow[:, :], ps[0:A_H + B_H, 6, 0:384], cv("biasscale")[0:A_H + B_H, :], None, ALU.mult), ("relb",))
            me.settle()
            me.go(V.tensor_copy(mx[0:1, 0, 0:1], brow[0:1, 0:1]), ev("brow"))
            dve.wait_ge(ev("cexp"), 1)
            me.go(V.tensor_scalar(ctmp[:, :], ctmp[:, :], 1.0, None, ALU.add))
            me.settle()
            me.go(V.reciprocal(ctmp[:, :], ctmp[:, :]))
            me.settle()
            c0 = FVAT["c_2"]
            me.go(V.tensor_tensor(cact[:, :], ctmp[:, :], fv[:, c0:c0 + KC], ALU.mult), ev("cact"))
            dve.wait_ge(ev("lamexp"), 1)
            for l in range(DEPTH):
                me.go(V.tensor_tensor(neglam[:, l:l + 1], lamp[:, l, 1:2], lamp[:, l, 0:1], ALU.subtract))
            me.settle()
            for l in range(DEPTH):
                me.go(V.tensor_scalar(neglam[:, l:l + 1], neglam[:, l:l + 1], -LAM0[l], None, ALU.add))
            columns("xT", 0)

            def rope(xs, c, s, tmp, n, half, dst=None):
                a, b = xs[:, :, :, 0:half], xs[:, :, :, half:2 * half]
                cb, sb_ = (v.unsqueeze(2).broadcast_to([P, TT, n, half]) for v in (c, s))
                w = [tmp[:, i * TT * n * half:(i + 1) * TT * n * half].rearrange("p (t h d) -> p t h d", t=TT, h=n) for i in range(4)]
                for i, (u, v) in enumerate(((a, cb), (b, sb_), (b, cb), (a, sb_))):
                    me.go(V.tensor_tensor(w[i], u, v, ALU.mult))
                me.settle()
                me.go(V.tensor_tensor(a, w[0], w[1], ALU.subtract))
                return V.tensor_tensor(b, w[2], w[3], ALU.add)

            c1, s1, c2, s2 = (cv(n).rearrange("p (t d) -> p t d", t=TT) for n in ("cos1", "sin1", "cos2", "sin2"))
            for L in range(DEPTH):
                win(L)
                for t in range(TT):
                    for i, (a, n) in enumerate(((C_IN, QL), (C_IN + QL, KVL))):
                        v = proj[:, t, a:a + n]
                        me.go(V.tensor_tensor_reduce(out=junk[:, 512 * t + a - C_IN:512 * t + a - C_IN + n], in0=v, in1=v, scale=1.0, scalar=0.0, op0=ALU.mult, op1=ALU.add, accum_out=va[:, t, i:i + 1]))
                me.settle()
                me.go(V.tensor_scalar(va[:, :, 0:1], va[:, :, 0:1], 1.0 / QL, 1e-6, ALU.mult, ALU.add))
                me.go(V.tensor_scalar(va[:, :, 1:2], va[:, :, 1:2], 1.0 / KVL, 1e-6, ALU.mult, ALU.add), ev("var_lat", L))
                copy(ut[:, 2:4, :], ps[:, U.bank[("ab", L, 1)], :].rearrange("p (c n) -> p c n", c=2), ("ab", L, 1))
                copy(ut[:, 6:8, :], ps[:, U.bank[("ab", L, 3)], :].rearrange("p (c n) -> p c n", c=2), ("ab", L, 3))
                if L:
                    dve.wait_ge(ev("resid", L - 1, 2), 2)
                dve.wait_ge(ev("rstd_lat", L), 1)
                for t in range(TT):
                    for i, (a, n) in enumerate(((0, QL), (QL, KVL))):
                        ins = V.tensor_scalar(z[:, t, a:a + n], proj[:, t, C_IN + a:C_IN + a + n], rs[:, t, i:i + 1], None, ALU.mult)
                        me.go(ins, ev("latent", L) if (t, i) == (1, 1) else None)
                kr = proj[:, :, C_KR:C_KR + ROPE].unsqueeze(2)
                me.go(rope(kr, c1, s1, junk, 1, 16))
                for t in range(TT):
                    for h in range(2):
                        key = ("ukv", L, t, h)
                        wait_full(dve, key)
                        src = ps[:, U.bank[key], 0:384].rearrange("p (h d) -> p h d", d=P)
                        me.go(V.tensor_copy(cbuf[:, t, 960 + 288 * h:960 + 288 * h + 288].rearrange("p (h d) -> p h d", d=CQ)[:, :, 0:NOPE], src[:, :, 0:NOPE]))
                        me.empty(V.tensor_copy(vc[:, t, 192 * h:192 * h + 192].rearrange("p (h d) -> p h d", d=HD), src[:, :, NOPE:P]), key)
                me.settle()
                for t in range(TT):
                    ins = V.tensor_copy(cbuf[:, t, 960:1536].rearrange("p (h d) -> p h d", d=CQ)[:, :, NOPE:CQ],
                                        proj[:, t, C_KR:C_KR + ROPE].unsqueeze(1).broadcast_to([P, C_H, ROPE]))
                    me.go(ins, ev("latent_k", L) if t == 1 else None)
                wait_done(dve, ("uq", L, 1, 1))
                q = cbuf[:, :, 0:576].rearrange("p t (h d) -> p t h d", d=CQ)[:, :, :, NOPE:CQ]
                me.go(rope(q, c1, s1, junk, C_H, 16), ev("latent_q", L))
                for n in (1, 3, 5):
                    copy(ut[0:CQ, 10 + 2 * n:12 + 2 * n, :], ps[0:CQ, U.bank[("ct", L, n)], :].rearrange("p (c n) -> p c n", c=2), ("ct", L, n))
                if L == 0:
                    for n in range(5):
                        copy(bias[:, 2 * n:2 * n + 2, :].rearrange("p h n -> p (h n)"), ps[:, U.bank[("flip", n)], :], ("flip", n))
                    me.settle()
                softmax(L)
                columns("ht", L)
                products_wo(L)
                norm(L, "y", 1)
                start(split, "gu", L)
                ada(ADA_NORM[L, "y"])
                columns("hT", L)
                ffn(L)
                norm(L, "d", 2)
                start(split, "win", L + 1)
                ada(ADA_NORM[L, "d"])
                if L == 1:
                    a = FVAT["b_ada_2"]
                    me.go(V.tensor_tensor(modv[:, :], modv[:, :], fv[:, a:a + 48], ALU.add))
                    me.settle()
                    for n, (m, add, g) in enumerate(((8, 1.0, "g_pre_mix_2"), (32, 1.0, "g_pre_ffn_2"), (16, 0.0, "g_post_mix_2"), (40, 0.0, "g_post_ffn_2"))):
                        me.go(V.scalar_tensor_tensor(out=aff[:, n, :], in0=modv[:, m:m + 8], scalar=add, in1=fv[:, FVAT[g]:FVAT[g] + 8], op0=ALU.add, op1=ALU.mult),
                              ev("mod") if n == 3 else None)
                    for t in range(TT):
                        mean_rms(t, "in", 0, ev("squares", "in"), t + 1, ev("var_in"))
                    for t in range(TT):
                        dve.wait_ge(ev("rstd_in"), t + 1)
                        me.go(V.tensor_scalar(z[:, t, :], x[:, t, :], rs[:, t, 0:1], None, ALU.mult), ev("norm_in", 1))
                columns("xT", L + 1)

            L = 2
            me.settle()
            for v in range(2):
                if v:
                    wait_full(dve, ("G", 0, 1))
                for c in range(KC):
                    me.go(V.tensor_scalar(junk[:, c * P:(c + 1) * P], ident, aff[:, 2 + v, c:c + 1], None, ALU.mult), ev("diag", v) if c == KC - 1 else None)
            win(L)

            def rope2(col, n, semaphore=None):
                xs = proj[:, :, col:col + n * HD] if n > 1 else proj[:, :, col:col + R2]
                xs = xs.rearrange("p t (h d) -> p t h d", h=n)[:, :, :, 0:R2]
                me.go(rope(xs, c2, s2, junk, n, R2 // 2), semaphore)

            wait_full(dve, ("G", 1, 1))
            rope2(IQ, 9)
            me.settle()
            me.go(V.tensor_scalar(wi[:, :, :], proj[:, :, IW:IW + 8], 8 ** -0.5 * 64 ** -0.5, None, ALU.mult))
            for i in range(2):
                me.go(V.tensor_copy(z[:, :, 64 * i:64 * i + 64], proj[:, :, IK:IK + 64]), ev("idx_rows") if i else None)
            for t in range(TT):
                v = proj[:, t, DCKV:DCKV + KVL]
                me.go(V.tensor_tensor_reduce(out=tw[:, t, 0:KVL], in0=v, in1=v, scale=1.0, scalar=0.0, op0=ALU.mult, op1=ALU.add, accum_out=va[:, t, 0:1]))
            me.settle()
            me.go(V.tensor_scalar(va[:, :, 0:1], va[:, :, 0:1], 1.0 / KVL, 1e-6, ALU.mult, ALU.add), ev("var_ckv"))
            copy(ut[:, 10:12, :], ps[:, U.bank[("idxT", 1)], :].rearrange("p (c n) -> p c n", c=2), ("idxT", 1))
            dve.wait_ge(ev("rstd_ckv"), 1)
            for t in range(TT):
                me.go(V.tensor_scalar(z[:, t, P:S], proj[:, t, DCKV:DCKV + KVL], rs[:, t, 0:1], None, ALU.mult), ev("ckv_rows") if t else None)
            for col, n in ((NQ, 10), (NKS, 2), (NKW, 2), (DQ, 8), (DKR, 1)):
                me.settle()
                rope2(col, n)
            me.settle()
            for v in range(2):
                for t in range(TT):
                    src = proj[:, t, (NKC, NVC)[v]:(NKC, NVC)[v] + P].rearrange("p (g d) -> p g d", g=2).unsqueeze(2).broadcast_to([P, 2, 2, HD])
                    me.go(V.tensor_copy(dup[:, t, S * v:S * v + S].rearrange("p (g r d) -> p g r d", g=2, r=2), src), ev("rope_rows") if (v, t) == (1, 1) else None)
            dve.wait_ge(ev("gexp"), 1)
            me.go(V.tensor_scalar(gt[:, :, :], gt[:, :, :], 1.0, None, ALU.add))
            me.settle()
            me.go(V.reciprocal(gt[:, :, :], gt[:, :, :]))
            me.settle()
            for t in range(TT):
                me.go(V.tensor_scalar(gt[:, t, 0:8], gt[:, t, 0:8], cv("cmpvalid")[:, t:t + 1], None, ALU.mult))
            for h in range(8):
                wait_done(dve, ("lg", h))
                if h:
                    me.settle()
                for t, (a, e) in enumerate(((0, P), (P, 384))):
                    prev = dmask[:, a:e] if h else (cv("causal")[:, P:S] if t == 0 else cv("causal"))
                    me.go(V.scalar_tensor_tensor(out=dmask[:, a:e], in0=probs[:, h % 4, a:e], scalar=wi[:, t, h:h + 1], in1=prev, op0=ALU.mult, op1=ALU.add),
                          ev("idx_added") if t else None)
            for t in range(TT):
                key = ("kd", t)
                wait_full(dve, key)
                kd = cbuf[:, t, 0:512].rearrange("p (h d) -> p h d", d=HD)
                me.empty(V.tensor_copy(kd[:, :, R2:HD], ps[:, U.bank[key], 0:384].rearrange("p (h d) -> p h d", d=48)), key)
                me.go(V.tensor_copy(kd[:, :, 0:R2], proj[:, t, DKR:DKR + R2].unsqueeze(1).broadcast_to([P, 8, R2])), ev("dk_rows") if t else None)
            for n in (1, 3, 5):
                if n == 5:
                    wait_full(dve, ("nT", n))
                    me.empty(shifted(lambda o, i, f: V.tensor_copy(o, i), n, None), ("nT", n))
                else:
                    copy(*turned(n), ("nT", n))
            key = ("cmp1",)
            b = U.bank[key]
            wait_full(dve, key)
            for v in range(2):
                a = FVAT["cmp_b1_2"] + v
                me.go(V.tensor_tensor(hb[:, v:v + 1], ps[:, b, 32 * v + 30:32 * v + 31], fv[:, a:a + 1], ALU.add))
            me.settle()
            me.go(V.tensor_scalar(hid[:, 0, 0:30], ps[:, b, 0:30], hb[:, 0:1], None, ALU.add))
            me.empty(V.tensor_scalar(hid[:, 0, 30:60], ps[:, b, 32:62], hb[:, 1:2], None, ALU.add), key)
            me.settle()
            me.go(V.tensor_tensor(hid[:, 1, :], hid[:, 0, :], hid[:, 0, :], ALU.mult))
            me.settle()
            me.go(V.tensor_scalar(hid[:, 1, :], hid[:, 1, :], 0.044715, 1.0, ALU.mult, ALU.add))
            me.settle()
            me.go(V.tensor_tensor(hid[:, 1, :], hid[:, 1, :], hid[:, 0, :], ALU.mult), ev("gelu_arg"))
            copy(*turned(7), ("nT", 7))
            dve.wait_ge(ev("gelu_exp"), 1)
            me.go(V.tensor_scalar(hid[:, 2, :], hid[:, 2, :], 1.0, None, ALU.add))
            me.settle()
            me.go(V.reciprocal(hid[:, 2, :], hid[:, 2, :]))
            me.settle()
            me.go(V.tensor_tensor(hid[:, 3, :], hid[:, 2, :], hid[:, 0, :], ALU.mult), ev("hidden"))
            key = ("cmp2",)
            b = U.bank[key]
            wait_full(dve, key)
            me.go(V.tensor_scalar(kcmp[:, 0:NCMP], ps[:, b, 0:NCMP], fv[:, B2K:B2K + 1], None, ALU.add))
            me.empty(V.tensor_tensor(vcmp[0:NCMP, :].rearrange("p (g d) -> p g d", g=2), ps[0:NCMP, b, 64:192].rearrange("p (g d) -> p g d", g=2),
                                     b2v[0:NCMP, :].unsqueeze(1).broadcast_to([NCMP, 2, HD]), ALU.add), key)
            for r in range(TOPK // 8):
                for t, (a, e) in enumerate(((0, P), (P, 384))):
                    me.go(V.max(m8[:, t, :], dmask[:, a:e]))
                me.settle()
                for t, (a, e) in enumerate(((0, P), (P, 384))):
                    me.go(V.match_replace(out=dmask[:, a:e], in_to_replace=m8[:, t, :], in_values=dmask[:, a:e], imm_value=TAKEN))
                me.settle()
            me.go(V.tensor_scalar(dmask[:, :], dmask[:, :], TAKEN / 1.5, NEG, ALU.is_gt, ALU.mult))
            me.settle()
            me.go(V.tensor_tensor(dmask[:, 0:P], dmask[:, 0:P], cv("causal")[:, P:S], ALU.add))
            me.go(V.tensor_tensor(dmask[:, P:384], dmask[:, P:384], cv("causal"), ALU.add))
            me.settle()
            softmax(L)
            columns("ht", L)
            products_wo(L)
            start(split, "gu", L)
            add_gated(L, "y", 0, lambda t: ev("mixed"))
            for t in range(TT):
                mean_rms(t, "mid", 1, ev("squares", "mid"), t + 1, ev("var_mid"))
            for t in range(TT):
                dve.wait_ge(ev("rstd_mid"), t + 1)
                me.go(V.tensor_scalar(z[:, t, :], x[:, t, :], rs[:, t, 1:2], None, ALU.mult), ev("norm1", L))
            columns("hT", L)
            ffn(L)
            add_gated(L, "d", 1, lambda t: ev("out_rows", t))

        @block.gpsimd
        def _(gp):
            me = Steps(gp, pool_step)
            gp.dma_start(cst[:, :], A["consts"]).then_inc(s_const, 16)
            gp.dma_start(hot[:, :], A["hot"]).then_inc(s_const, 16)
            gp.dma_start(relb[0:32, :], A["rel_bias"]).then_inc(s_const, 16)
            gp.dma_start(relb[32:34, :], A["which"]).then_inc(s_const, 16)
            for rows, names, base in ((rowsA, ROWS_A, 0), (rowsB, ROWS_B, N_A)):
                for n, k in names:
                    at = FVAT[n] - base
                    gp.dma_start(rows[at:at + k, :], A["rows_" + n]).then_inc(s_vec, 16)
            for i in range(2):
                gp.dma_start(rowsA[B2K:B2K + 1, 64 * i:64 * i + 64], A["cmp_b2_2"][0, 0:1, :]).then_inc(s_vec, 16)
            for l in range(DEPTH):
                gp.dma_start(lamin[:, l, :], A["diff_lambda"][l].rearrange("a b -> (a b)").partition_broadcast(P)).then_inc(s_vec, 16)
                gp.dma_start(sg[:, l, :], A["subln_g"][l].partition_broadcast(P)).then_inc(s_vec, 16)
            gp.dma_start(b2v[0:NCMP, :], A["cmp_b2_2"][0, 1].partition_broadcast(NCMP)).then_inc(s_vec, 16)
            me.go(gp.memset(ones[:, :], 1.0))
            me.go(gp.memset(half[:, :], -0.5))
            me.settle()
            loads = [0]

            def load_affine(name, l):
                for i, s in enumerate("gb"):
                    gp.dma_start(lnb[:, i, :], A[name + "_" + s][l].partition_broadcast(P)).then_inc(s_lnb, 16)
                loads[0] += 1

            def power(dst, src, wait, value, signal):
                gp.wait_ge(wait, value)
                n = src.shape[-1]
                h = half[:, 0:n] if len(src.shape) == 2 else half[:, 0:2 * n].rearrange("p (a b) -> p a b", a=2)
                gp.tensor_tensor(dst, src, h, ALU.pow).then_inc(signal, 1)

            def residual(L, ln):
                gp.wait_ge(s_lnb, 32 * loads[0])
                for t in range(TT):
                    gp.wait_ge(ev("norm%d" % ln, L), t + 1)
                    me.go(gp.tensor_tensor(x[:, t, :], z[:, t, :], lnb[:, 0, :], ALU.mult))
                    me.settle()
                    me.go(gp.tensor_tensor(x[:, t, :], x[:, t, :], lnb[:, 1, :], ALU.add), ev("resid", L, ln))
                me.settle()

            load_affine("ln1", 0)
            for L in range(DEPTH):
                power(rs[:, :, 0:2], va[:, :, 0:2], ev("var_lat", L), 1, ev("rstd_lat", L))
                power(rb[:, :, :], vb[:, :, :], ev("var_b", L), 1, ev("rstd_b", L))
                for ln in (1, 2):
                    for t in range(TT):
                        power(rs[:, t, 0:1], va[:, t, 0:1], ev("var", ln, L), t + 1, ev("rstd", ln, L))
                    residual(L, ln)
                    if ln == 1:
                        load_affine("ln2", L)
                    elif L == 0:
                        load_affine("ln1", 1)
            for t in range(TT):
                power(rs[:, t, 0:1], va[:, t, 0:1], ev("var_in"), t + 1, ev("rstd_in"))
            power(rs[:, :, 0:1], va[:, :, 0:1], ev("var_ckv"), 1, ev("rstd_ckv"))
            for t in range(TT):
                power(rs[:, t, 0:1], va[:, t, 0:1], ev("var_y"), t + 1, ev("rstd_y"))
            for t in range(TT):
                power(rs[:, t, 1:2], va[:, t, 1:2], ev("var_mid"), t + 1, ev("rstd_mid"))
            for t in range(TT):
                power(rs[:, t, 0:1], va[:, t, 0:1], ev("var_d"), t + 1, ev("rstd_d"))


INPUTS = ["x", "rel_bias", "w_in", "q_norm_g", "kv_norm_g", "w_uq", "w_ukv", "diff_lambda", "subln_g", "w_o", "ln1_g",
          "ln1_b", "ln2_g", "ln2_b", "w_gate", "w_up", "w_down", "c_2", "w_ada_2", "b_ada_2", "g_pre_mix_2",
          "g_post_mix_2", "g_pre_ffn_2", "g_post_ffn_2", "w_in_2", "cmp_pe_2", "cmp_w1_2", "cmp_b1_2", "cmp_w2_2",
          "cmp_b2_2", "g_kv_norm_2", "w_uk_2", "w_uv_2", "w_out_2", "w_gate_up_2", "w_down_2"]


def kernel(**inputs):
    import concourse.bacc as bacc
    from concourse.bass_utils import run_bass_kernel_spmd

    nc = bacc.Bacc("TRN2", target_bir_lowering=False, num_devices=1)
    arrays = {}
    for name in INPUTS:
        arrays[name] = np.ascontiguousarray(inputs[name])
    arrays["consts"], arrays["hot"], arrays["which"] = constants()
    A = {}
    for name, a in arrays.items():
        A[name] = nc.dram_tensor("in_" + name, a.shape, mybir.dt.from_np(a.dtype), kind="ExternalInput").ap()
    for name, k in ROWS_A + ROWS_B:
        ap = A[name]
        A["rows_" + name] = bass.AP(ap.tensor, 0, [[P, k], [1, P]])
    out = nc.dram_tensor("out", (1, S, D), F32, kind="ExternalOutput").ap()
    program(nc, A, out)
    r = run_bass_kernel_spmd(nc, [{"in_" + n: a for n, a in arrays.items()}], core_ids=[0])
    return r.results[0]["out"]
```

```python
import math
from contextlib import ExitStack

import numpy as np
import concourse.bass as bass
from concourse import mybir

F32 = mybir.dt.float32
F32R = mybir.dt.float32r
ALU = mybir.AluOpType
ACT = mybir.ActivationFunctionType
AX = mybir.AxisListType

P, S, TT, D = 128, 256, 2, 1024
KC = D // P
FF = 2816
FC = FF // P
DEPTH = 2
ALPHA = (2 * DEPTH) ** 0.25
HD = 64
A_H, B_H, C_H = 6, 4, 6
BQ = 32
QL, KVL, NOPE, ROPE = 256, 128, 64, 32
CQ = NOPE + ROPE
IN1 = 2336
IN2 = 2544
A_K, A_V = A_H * HD, 2 * A_H * HD
B_Q, B_K, B_V = 1152, 1408, 1664
C_IN = 1920
C_KR = C_IN + QL + KVL
NEG = -1e30
TAKEN = -3e38
NQ, NKC, NVC, NKS, NVS, NKW, NVW, NGT, DQ, DCKV, DKR, IQ, IK, IW = (
    0, 512, 640, 768, 896, 1024, 1152, 1280, 1304, 1816, 1944, 1960, 2472, 2536)
R2 = 16
NCMP = 15
TOPK = 64
SLOTW = 2048
NRAW, NW = 3, 3
NGU = FC
ADA_ATT = {0: (0, 1), 1: (6, 7)}
ADA_FFN = {0: (2, 3, 4, 5), 1: (8, 9, 10, 11)}
ADA_AFTER = {2 + 3 * n: n for n in range(6)}
ADA_AFTER_DN = {2: 6, 5: 7}
ADA_DN = 9
GELU_C = math.sqrt(2.0 / math.pi)
SC_A, SC_B, SC_C = HD ** -0.5, BQ ** -0.5, CQ ** -0.5
LAM0 = [0.8 - 0.6 * math.exp(-0.3 * l) for l in range(DEPTH)]

CC = {}


def _const_layout():
    at = 0
    for name, n in (("ident", P), ("flip", P), ("causal", S), ("cos1", TT * 16), ("sin1", TT * 16), ("cos2", TT * 8),
                    ("sin2", TT * 8), ("cmpmask", TT * 16), ("cmpvalid", TT), ("biasscale", 1)):
        CC[name] = (at, at + n)
        at += n
    return at


NCONST = _const_layout()


def constants():
    c = np.zeros((P, NCONST), np.float32)

    def put(name, value):
        a, b = CC[name]
        c[:, a:b] = np.asarray(value, np.float32).reshape(P, b - a)

    p = np.arange(P)[:, None]
    put("ident", np.eye(P))
    put("flip", np.eye(P)[::-1])
    put("causal", np.where(np.arange(S)[None] <= P + p, 0.0, NEG))
    tok = (np.arange(TT)[None, :] * P + p).astype(np.float32)
    inv1 = (np.float32(10000.0) ** (-np.arange(16, dtype=np.float32) / np.float32(16))).astype(np.float32)
    inv2 = (np.float32(1.0) / (np.float32(500000.0) ** (np.arange(0, R2, 2, dtype=np.float32) / np.float32(R2)))).astype(np.float32)
    for n, inv in (("1", inv1), ("2", inv2)):
        ang = (tok[:, :, None] * inv[None, None, :]).astype(np.float32).astype(np.float64)
        put("cos" + n, np.cos(ang))
        put("sin" + n, np.sin(ang))
    ends = np.arange(16) * 16 + 31
    put("cmpmask", np.where((ends[None, None] <= tok[:, :, None]) & (np.arange(16) < NCMP), 0.0, NEG))
    put("cmpvalid", tok >= 31)
    put("biasscale", np.where(p < A_H, 1 / SC_A, 1 / SC_B))
    d = 255 - np.arange(384)
    pos = np.maximum(d, 1).astype(np.float32)
    large = 16 + (np.log(pos / np.float32(16)) / math.log(2048 / 16) * 16).astype(np.int32)
    bucket = np.where(d < 16, np.maximum(d, 0), np.minimum(large, 31))
    hot = np.zeros((34, 384), np.float32)
    hot[bucket[d >= 0], np.nonzero(d >= 0)[0]] = 1.0
    times = (d <= 128).astype(int) + (d % 4 == 0) + (d % 16 == 0)
    hot[32] = np.where((d >= 0) & (times > 0), np.log(np.maximum(times, 1)), NEG)
    hot[33] = np.where(d >= 0, 0.0, NEG)
    which = np.zeros((2, A_H + B_H), np.float32)
    which[0, :A_H] = 1.0
    which[1, A_H:] = 1.0
    return c, hot, which


ROWS_A = [("ln1_g", 16), ("ln1_b", 16), ("ln2_g", 16), ("ln2_b", 16), ("q_norm_g", 4), ("kv_norm_g", 2),
          ("g_pre_mix_2", 8), ("g_post_mix_2", 8), ("g_pre_ffn_2", 8), ("g_post_ffn_2", 8), ("c_2", 8),
          ("g_kv_norm_2", 1), ("cmp_b1_2", 2)]
ROWS_B = [("b_ada_2", 48), ("cmp_pe_2", 32)]
FVAT = {}
_at = 0
for _rows in (ROWS_A, ROWS_B):
    for _n, _k in _rows:
        FVAT[_n] = _at
        _at += _k
N_A = sum(k for _, k in ROWS_A)
N_B = sum(k for _, k in ROWS_B)
B2K = 113
N_A += 1
for _n, _ in ROWS_B:
    FVAT[_n] += 1


ARENA = 22 * S + TT * IN2 + TT * 1536 + 3 * S + 4 * 384 + 2 * 384 + 384


class Job:
    def __init__(self, kind, q, k, kk, mask, scale, v, col, group, last):
        self.kind, self.q, self.k, self.kk, self.mask, self.scale = kind, q, k, kk, mask, scale
        self.v, self.col, self.group, self.last = v, col, group, last


PIECES = {"A": 2, "B": 5, "C": 2, "slc": 2, "win": 4, "cmp": 4, "dsa": 2}
GROUPS = {0: ["A", "B", "C"], 1: ["A", "B", "C"], 2: ["slc", "win", "cmp", "dsa"]}


def jobs_of(L):
    out = []
    if L < 2:
        for h in range(A_H):
            out.append(Job("A", (h // 2, 64 * (h % 2)), (3 + h // 2, 64 * (h % 2)), 64, ("bias", h), SC_A, ("proj", A_V + h * HD), h, 0, h == 5))
        for h in range(B_H):
            for i in range(2):
                n = 2 * h + i
                out.append(Job("B", (6 + n // 4, 32 * (n % 4)), (8 + n // 4, 32 * (n % 4)), 32, ("bias", A_H + h), SC_B, ("proj", B_V + h * HD), n, 1, n == 7))
        for h in range(C_H):
            out.append(Job("C", (10 + h, 0), (16 + h, 0), CQ, ("causal", 0), SC_C, ("cv", h), h, 2, h == 5))
        return out
    for g, (kind, kslot, v) in enumerate((("slc", 12, NVS), ("win", 13, NVW))):
        for h in range(8):
            out.append(Job(kind, (h % 4, 64 * (h // 4)), (kslot, 64 * (h // 4)), 64, ("causal", 0), SC_A, ("proj", v + 64 * (h // 4)), h, g, h == 7))
    for h in range(8):
        out.append(Job("cmp", (h % 4, 64 * (h // 4)), None, 64, ("cmp", 0), SC_A, ("vcmp", h // 4), h, 2, h == 7))
    for h in range(8):
        out.append(Job("dsa", (4 + h // 2, 64 * (h % 2)), (8 + h // 2, 64 * (h % 2)), 64, ("dsa", 0), SC_A, ("vd", h), h, 3, h == 7))
    return out


JOBS = {L: jobs_of(L) for L in range(3)}
JOB0 = {0: 0, 1: len(JOBS[0]), 2: 2 * len(JOBS[0])}
OBANK = {g: 2 * (g % 2) for g in range(4)}
ADA_STEP = {12: 0, 20: 1}
ADA_EARLY = 2
LEFT = 640
ADA_GU = {6: 0, 12: 1, 18: 2}


def alt(n):
    return "act" if n % 2 == 0 else "dve"


def plan():
    fills, empties = [], []

    def put(key, bank, eng, later=False):
        fills.append((key, bank, eng))
        if not later:
            empties.append(key)

    def product(key, L, eng="dve"):
        for t in range(TT):
            for h in range(2):
                put((key, L, t, h), 2 * t + h, eng)

    for n in range(4):
        put(("xT", 0, n), 4 + n, "dve")
    for L in range(3):
        for i in range(5):
            for t in range(TT):
                put(("win", L, i, t), (2 * i + t) % 4, alt(t))
        if L == 0:
            for n in range(2):
                put(("fv", n), 4 + n, "dve")
            put(("relb",), 6, "dve")
        if L < 2:
            for n in range(5):
                put(("ab", L, n), 4 + n % 4, alt(n))
            for n in range(2):
                put(("c", L, n), 5 + n, "act")
            product("uq", L, "act")
            for t in range(TT):
                for h in range(2):
                    put(("ukv", L, t, h), 4 + 2 * t + h, "dve")
            for n in range(6):
                put(("ct", L, n), n % 4, alt(n))
            if L == 0:
                for n in range(5):
                    put(("flip", n), (2 + n) % 4, "dve")
        else:
            put(("nT", 5), 5, "dve")
            put(("nT", 6), 6, "act")
            put(("cmp1",), 7, "dve")
            for n in range(3):
                put(("idxT", n), 4 + n, alt(n))
            for h in range(8):
                put(("lg", h), h % 4, "act")
            put(("ckvT",), 7, "act")
            for t in range(TT):
                put(("kd", t), t, "dve")
            for t in range(TT):
                put(("vd", t), 2 + t, "act")
            for n in range(5):
                put(("nT", n), 4 + n % 4, alt(n))
            put(("nT", 7), 5, "dve")
            put(("nT", 8), 6, "act")
            put(("cmp2",), 7, "dve")
        js, held = JOBS[L], {}
        for k in range(len(js) + 3):
            if k < len(js):
                put(("s", L, k), 4 + k % 2, "dve")
            if 0 <= k - 2 < len(js):
                put(("pt", L, k - 2), 6 + k % 2, alt(k))
            empties += held.pop(k, [])
            if 0 <= k - 3 < len(js) and js[k - 3].last:
                g = js[k - 3].group
                for t in range(TT):
                    put(("o", L, g, t), OBANK[g] + t, "dve", later=True)
                    held.setdefault(k + 1 + t, []).append(("o", L, g, t))
            if L < 2 and k in ADA_STEP:
                q = ADA_ATT[L][ADA_STEP[k]]
                put(("ada", q), 2 * ADA_STEP[k], "dve", later=True)
                held.setdefault(k + 1, []).append(("ada", q))
        for k in sorted(held):
            empties += held[k]
        for n in range(4):
            put(("ht", L, n), 4 + n, "dve")
        product("y", L)
        for n in range(4):
            put(("hT", L, n), 4 + n, "act")
        for i in range(NGU):
            put(("gu", L, i), 4 + i % 4, "dve")
            if L < 2 and i in ADA_GU:
                put(("ada", ADA_FFN[L][ADA_GU[i]]), 0, "dve")
        if L < 2:
            put(("ada", ADA_FFN[L][3]), 7, "dve")
        product("d", L)
        if L == 1:
            for v in range(2):
                for h in range(2):
                    put(("G", v, h), 4 + 2 * v + h, "act")
        if L < 2:
            for n in range(4):
                put(("xT", L + 1, n), 4 + n, "act")
    return fills, empties


class Units:

    def __init__(self):
        self.full, self.mine, self.bank, self.eng, self.prev = {}, {}, {}, {}, {}
        counts, last = {"act": 0, "dve": 0}, {}
        fills, empties = plan()
        for n, (key, bank, eng) in enumerate(fills):
            assert key not in self.full, key
            self.full[key], self.bank[key], self.eng[key] = n + 1, bank, eng
            self.prev[key] = last.get(bank)
            last[bank] = key
        for key in empties:
            counts[self.eng[key]] += 1
            self.mine[key] = counts[self.eng[key]]


U = Units()


def stream():
    out = []
    for L in range(3):
        out += [("win", L, i, h) for i in range(5) for h in range(2)]
        if L < 2:
            out += [("lora", L)] + [("ada", q, h) for q in ADA_ATT[L] for h in range(2)]
        else:
            out += [("small",), ("w1", 0), ("w1", 1)]
        out += [("wo", L, i) for i in range(KC // 2)]
        for i in range(NGU):
            out.append(("gu", L, i))
            if L < 2 and i in ADA_AFTER:
                out.append(("ada", ADA_FFN[L][ADA_AFTER[i] // 2], ADA_AFTER[i] % 2))
        for i in range(FC // 2):
            out.append(("dn", L, i))
            if L < 2 and i in ADA_AFTER_DN:
                out.append(("ada", ADA_FFN[L][3], ADA_AFTER_DN[i] % 2))
    return out


ITEMS = stream()
ITEM = {k: n for n, k in enumerate(ITEMS)}
SPLITS = [k for k in ITEMS if k[0] in ("win", "wo", "gu", "dn")]
SPLIT = {k: m for m, k in enumerate(SPLITS)}
WIDTH = {"wo": SLOTW, "gu": SLOTW, "dn": SLOTW}


def win_width(L, i):
    return min(512, (IN1 if L < 2 else IN2) - 512 * i)


def split_width(item):
    return 4 * win_width(item[1], item[2]) if item[0] == "win" else SLOTW


def dmas_of(item):
    return {"gu": 2, "lora": 2, "small": 3}.get(item[0], 1)


LANDED = {}
_c = [0] * NRAW
for _n, _k in enumerate(ITEMS):
    _c[_n % NRAW] += 16 * dmas_of(_k)
    LANDED[_k] = _c[_n % NRAW]


def released(item):
    k = item[0]
    if k == "win" and item[3] == 1:
        return ("full", ("win", item[1], item[2], 1))
    if k == "lora":
        return ("full", ("ukv", item[1], 1, 1))
    if k == "gu":
        return ("full", item)
    if k == "wo" and item[2] == KC // 2 - 1:
        return ("full", ("y", item[1], 1, 1))
    if k == "dn" and item[2] == FC // 2 - 1:
        return ("full", ("d", item[1], 1, 1))
    if k == "ada":
        return ("summed", item[1:])
    if k == "w1":
        return ("full", ("cmp1",))
    if k == "small":
        return ("full", ("cmp2",))
    return ("used", None)


USED = {}
for _k in ITEMS:
    if released(_k)[0] == "used":
        USED[_k] = len(USED) + 1
COLS = {k: 4 * n for n, k in enumerate((("hT", 0), ("xT", 1), ("hT", 1), ("xT", 2), ("hT", 2)))}


class Steps:

    def __init__(self, eng, own, done=None, name=None):
        self.eng, self.own, self.done, self.name = eng, own, done, name
        self.n, self.last, self.emptied_n = {}, None, 0

    def go(self, ins, sem=None):
        sem = sem or self.own
        self.n[sem.name] = self.n.get(sem.name, 0) + 1
        ins.then_inc(sem, 1)
        self.last = (sem, self.n[sem.name])
        return self.last

    def settle(self):
        self.eng.wait_ge(*self.last)

    def empty(self, ins, key):
        self.emptied_n += 1
        assert U.mine[key] == self.emptied_n and U.eng[key] == self.name, key
        self.go(ins, self.done)


def program(nc, A, out):
    with ExitStack() as ctx:
        def sb(name, shape, dt=F32):
            return ctx.enter_context(nc.sbuf_tensor(name, shape, dt))

        def sem(name):
            return ctx.enter_context(nc.semaphore(name))

        ps = ctx.enter_context(nc.psum_tensor("ps", [P, 8, 512], F32))
        bias_dram = nc.dram_tensor("bias_rows", [A_H + B_H, 384], F32, kind="Internal").ap()

        raw = sb("raw", [P, NRAW, SLOTW])
        wh = sb("wh", [P, NW, SLOTW], F32R)
        wl = sb("wl", [P, NW, SLOTW], F32R)
        x = sb("x", [P, TT, D])
        z = sb("z", [P, TT, D])
        xh = sb("xh", [P, KC, S], F32R)
        xl = sb("xl", [P, KC, S], F32R)
        bias = sb("bias", [P, A_H + B_H, S])
        lnb = sb("lnb", [P, 2, D])
        scratch = sb("scratch", [P, 2, D])
        tw = scratch[:, 0, :].rearrange("p (t n) -> p t n", t=TT)
        junk = scratch[:, 1, :]
        arena = ctx.enter_context(nc.sbuf_tensor("arena", [P, ARENA], F32))
        base = nc.sbuf_base - 4 * ARENA
        place = [base]

        def at(name, shape, dt=F32, where=None):
            n = 4
            for v in shape[1:]:
                n *= v
            start = place[0] if where is None else where
            if where is None:
                place[0] += n
                assert place[0] <= base + 4 * ARENA
            return nc.alloc_sbuf_tensor_at(name, shape, dt, offset=start)

        ut = at("ut", [P, 22, S])
        proj = at("proj", [P, TT, IN2])
        cbuf_at = place[0]
        cbuf = at("cbuf", [P, TT, 1536])
        cT = at("cT", [P, 3, S])
        probs = at("probs", [P, 4, 384])
        pT = at("pT", [P, 2, 384])
        dmask = at("dmask", [P, 384])
        gh = at("gh", [P, FC, S], F32R, base)
        gl = at("gl", [P, FC, S], F32R, base + 4 * FC * S)
        rowsA = at("rowsA", [P, P], F32, cbuf_at)
        rowsB = at("rowsB", [P, P], F32, cbuf_at + 512)
        hot = at("hot", [34, 384], F32, cbuf_at + 1024)
        brow = at("brow", [A_H + B_H, 384], F32, cbuf_at + 1024 + 1536)
        lamin = at("lamin", [P, DEPTH, P], F32, cbuf_at + 4096)
        cst = sb("cst", [P, NCONST])
        fv = sb("fv", [P, N_A + N_B])
        modv = sb("modv", [P, 48])
        cact = sb("cact", [P, KC])
        ctmp = sb("ctmp", [P, KC])
        aff = sb("aff", [P, 4, KC])
        ones = sb("ones", [P, P])
        adasum = sb("adasum", [P, 512])
        half = sb("half", [P, 8])
        relb = sb("relb", [34, A_H + B_H])
        nmx = sb("nmx", [P, 4, TT])
        mx = sb("mx", [P, 4, TT])
        sums = sb("sums", [P, 2, TT, 8])
        rec = sb("rec", [P, 2, TT, 8])
        lamp = sb("lamp", [P, DEPTH, 2])
        neglam = sb("neglam", [P, DEPTH])
        sg = sb("sg", [P, DEPTH, HD])
        st = sb("st", [P, TT, 2, 6])
        mv = sb("mv", [P, TT, 2])
        va = sb("va", [P, TT, 4])
        rs = sb("rs", [P, TT, 4])
        vb = sb("vb", [P, TT, 4])
        rb = sb("rb", [P, TT, 4])
        gt = sb("gt", [P, TT, 24])
        wi = sb("wi", [P, TT, 8])
        m8 = sb("m8", [P, TT, 8])
        hid = sb("hid", [P, 4, 60])
        hb = sb("hb", [P, 2])
        kcmp = sb("kcmp", [P, 16])
        vcmp = sb("vcmp", [P, P])
        b2v = sb("b2v", [P, HD])

        def cv(name):
            a, b = CC[name]
            return cst[:, a:b]

        ident = cv("ident")
        spare = bias[:, :, :].rearrange("p h n -> p (h n)")
        VC, VD = 576, 512
        vc = cbuf[:, :, 576:960]
        vd = cbuf[:, :, 512:1024]
        dup = cbuf[:, :, 1024:1536]
        vcols = scratch[:, :, :].rearrange("p a (b n) -> p (a b) n", b=2)
        gsilu = scratch[:, 0, :].rearrange("p (s n) -> p s n", s=4)
        gated = scratch[:, 1, :].rearrange("p (s n) -> p s n", s=4)

        full, done_act, done_dve, used = sem("full"), sem("done_act"), sem("done_dve"), sem("used")
        done = {"act": done_act, "dve": done_dve}
        landed = [sem(f"landed{i}") for i in range(NRAW)]
        wh_ready, wl_ready, cols_ready, silu_ready, gated_ready = (
            sem(n) for n in ("wh_ready", "wl_ready", "cols_ready", "silu_ready", "gated_ready"))
        s_cst, s_const, s_x, s_vec, s_bias_out, s_bias_in, s_out = (sem(n) for n in ("s_cst", "s_const", "s_x", "s_vec", "s_bias_out", "s_bias_in", "s_out"))
        s_lnb = sem("s_lnb")
        probs_ready = sem("probs_ready")
        ada_scaled, ada_read, ada_summed = sem("ada_scaled"), sem("ada_read"), sem("ada_summed")
        act_step, dve_step, pool_step = sem("act_step"), sem("dve_step"), sem("pool_step")
        events = {}

        def ev(*name):
            if name not in events:
                events[name] = sem("ev_" + "_".join(map(str, name)))
            return events[name]

        def wait_full(eng, key):
            eng.wait_ge(full, U.full[key])

        def wait_done(eng, key):
            eng.wait_ge(done[U.eng[key]], U.mine[key])

        def wait_released(eng, item):
            how, key = released(item)
            if how == "full":
                wait_full(eng, key)
            elif how == "summed":
                eng.wait_ge(*((ada_summed if key[1] else ada_read), key[0] + 1))
            else:
                eng.wait_ge(used, USED[item])

        def mask_of(job, t):
            kind, h = job.mask
            if kind == "bias":
                return bias[:, h, P:S] if t == 0 else bias[:, h, :]
            if kind == "causal":
                return cv("causal")[:, P:S] if t == 0 else cv("causal")
            if kind == "dsa":
                return dmask[:, 0:P] if t == 0 else dmask[:, P:384]
            return cv("cmpmask").rearrange("p (t n) -> p t n", t=TT)[:, t, 0:NCMP]

        def score_cols(job, t):
            if job.kind == "cmp":
                return (16 * t, 16 * t + NCMP)
            return (0, P) if t == 0 else (P, 384)

        def value_of(job, kt, wide=HD):
            kind, a = job.v
            if kind == "proj":
                return proj[:, kt, a:a + wide]
            if kind == "cv":
                return cbuf[:, kt, VC + a * HD:VC + a * HD + wide]
            if kind == "vd":
                return cbuf[:, kt, VD + a * HD:VD + a * HD + wide]
            return vcmp[0:NCMP, a * HD:(a + 1) * HD]

        def win_views(L, i, t, n, b):
            if L == 2 and i == 0:
                return (proj[:, t, 0:512].rearrange("p (r g d) -> p g r d", g=2, d=HD),
                        ps[:, b, 0:512].rearrange("p (g r d) -> p g r d", g=2, d=HD))
            return proj[:, t, 512 * i:512 * i + n], ps[:, b, 0:n]

        def pt_views(L, n):
            b = U.bank[("pt", L, n)]
            if JOBS[L][n].kind == "cmp":
                return pT[0:NCMP, n % 2, 0:S], ps[0:NCMP, b, 0:S]
            return pT[:, n % 2, :], ps[:, b, 0:384]

        def proj_gates(eng):
            wait_done(eng, ("win", 2, 4, 1))
            wait_done(eng, ("win", 2, 4, 0))
            return proj[:, :, NGT:NGT + 24]

        def turned(n):
            s = {0: 0, 1: 2, 2: 4, 3: 6, 4: 12, 7: 8, 8: 10}[n]
            return ut[:, s:s + 2, :], ps[:, U.bank[("nT", n)], :].rearrange("p (c n) -> p c n", c=2)

        def shifted(copy, n, func):
            s = 15 + 2 * (n - 5)
            src = ps[:, U.bank[("nT", n)], :].rearrange("p (c n) -> p c n", c=2)
            copy(ut[0:64, s:s + 2, :], src[0:64], func)
            return copy(ut[64:P, s:s + 2, 0:S - 1], src[64:P, :, 1:S], func)

        block = ctx.enter_context(nc.Block())

        @block.sync
        def _(sp):
            def cols(w, a, n, k=KC):
                return w[:, a:a + n].rearrange("(k p) n -> p k n", p=P)

            def slot(n, a, k, w):
                return raw[:, n % NRAW, a:a + k * w].rearrange("p (k n) -> p k n", k=k)

            sp.dma_start(x[:, :, :], A["x"][0].rearrange("(t p) d -> p t d", p=P)).then_inc(s_x, 16)
            for n, item in enumerate(ITEMS):
                if n >= NRAW:
                    old = ITEMS[n - NRAW]
                    if old in SPLIT:
                        sp.wait_ge(wl_ready, SPLIT[old] + 1)
                    else:
                        wait_released(sp, old)
                got = landed[n % NRAW]
                kind, L = item[0], item[1] if len(item) > 1 else 2
                if kind == "win":
                    w = A["w_in"][L] if L < 2 else A["w_in_2"][0]
                    m, h = win_width(L, item[2]), item[3]
                    sp.dma_start(slot(n, 0, 4, m), cols(w[512 * h:512 * h + 512, :], 512 * item[2], m)).then_inc(got, 16)
                elif kind == "lora":
                    sp.dma_start(slot(n, 0, 2, 576), cols(A["w_uq"][L], 0, 576)).then_inc(got, 16)
                    sp.dma_start(raw[:, n % NRAW, 1152:1920], A["w_ukv"][L]).then_inc(got, 16)
                elif kind == "small":
                    sp.dma_start(slot(n, 0, 8, 48), A["w_uk_2"][0].rearrange("h r e -> r h e")).then_inc(got, 16)
                    sp.dma_start(slot(n, 384, 8, 64), A["w_uv_2"][0].rearrange("h r e -> r h e")).then_inc(got, 16)
                    sp.dma_start(slot(n, 896, 2, 64), A["cmp_w2_2"][0].rearrange("v r e -> r v e")).then_inc(got, 16)
                elif kind == "w1":
                    sp.dma_start(slot(n, 0, 16, P), A["cmp_w1_2"][0, item[1]].rearrange("(c p) n -> p c n", p=P)).then_inc(got, 16)
                elif kind in ("wo", "dn"):
                    w = {"wo": (A["w_o"], A["w_out_2"]), "dn": (A["w_down"], A["w_down_2"])}[kind]
                    w = w[0][L] if L < 2 else w[1][0]
                    sp.dma_start(slot(n, 0, 2, D), w[S * item[2]:S * item[2] + S, :].rearrange("(k p) n -> p k n", p=P)).then_inc(got, 16)
                elif kind == "ada":
                    w = A["w_ada_2"][0]
                    sp.dma_start(slot(n, 0, 4, 512), cols(w[512 * item[2]:512 * item[2] + 512, :], 512 * item[1], 512)).then_inc(got, 16)
                elif kind == "gu":
                    for v in range(2):
                        if L < 2:
                            src = cols(A[("w_gate", "w_up")[v]][L], P * item[2], P)
                        else:
                            src = cols(A["w_gate_up_2"][0], FF * v + P * item[2], P)
                        sp.dma_start(slot(n, 1024 * v, KC, P), src).then_inc(got, 16)
            for t in range(TT):
                sp.wait_ge(ev("out_rows", t), 1)
                sp.dma_start(out[0, t * P:(t + 1) * P, :], x[:, t, :]).then_inc(s_out, 16)
            sp.wait_ge(s_out, 32)

        @block.tensor
        def _(pe):
            filled = [0]
            use = [0]

            def fill(ins, key):
                filled[0] += 1
                assert U.full[key] == filled[0], key
                ins.then_inc(full, 1)

            def claim(key):
                if U.prev[key] is not None:
                    wait_done(pe, U.prev[key])
                return U.bank[key]

            def arrive(item):
                pe.wait_ge(landed[ITEM[item] % NRAW], LANDED[item])
                return raw[:, ITEM[item] % NRAW, :]

            def parts(item):
                m = SPLIT[item]
                pe.wait_ge(wl_ready, m + 1)
                return wh[:, m % NW, :], wl[:, m % NW, :]

            def columns_ready(name, L, u):
                if U.eng[name, L, u] == "dve":
                    wait_done(pe, (name, L, u))
                else:
                    pe.wait_ge(cols_ready, COLS[name, L] + u + 1)

            def leave(ins, item):
                use[0] += 1
                assert USED[item] == use[0]
                ins.then_inc(used, 1)

            mm = nc.tensor.matmul

            def to_columns(name, L, src, wait_rows):
                for t in range(TT):
                    wait_rows(t)
                    for u in range(4):
                        key = (name, L, u)
                        b = claim(key) if t == 0 else U.bank[key]
                        for c in range(2):
                            o = c * S + t * P
                            ins = nc.tensor.transpose(ps[:, b, o:o + P], src[:, t, (2 * u + c) * P:(2 * u + c + 1) * P], ident)
                        if t == 1:
                            fill(ins, key)

            def product_win(L):
                for i in range(5):
                    n = win_width(L, i)
                    for t in range(TT):
                        claim(("win", L, i, t))
                    for h in range(2):
                        a, b = (w[:, 0:4 * n].rearrange("p (k n) -> p k n", k=4) for w in parts(("win", L, i, h)))
                        for t in range(TT):
                            o = ps[:, U.bank["win", L, i, t], 0:n]
                            for k in range(4):
                                if i == 0 and t == 0 and k % 2 == 0:
                                    columns_ready("xT", L, (4 * h + k) // 2)
                                xs = slice(t * P, (t + 1) * P)
                                mm(o, xh[:, 4 * h + k, xs], a[:, k, :], start=h == k == 0, stop=False)
                                mm(o, xh[:, 4 * h + k, xs], b[:, k, :], start=False, stop=False)
                                ins = mm(o, xl[:, 4 * h + k, xs], a[:, k, :], start=False, stop=h == 1 and k == 3)
                            if h == 1:
                                fill(ins, ("win", L, i, t))
                        if h == 0:
                            leave(ins, ("win", L, i, h))

            def product_rows(kind, unit, L, sh, sl, nk, ready, after=None):
                ni = nk // 2
                for t in range(TT):
                    for h in range(2):
                        claim((unit, L, t, h))
                for i in range(ni):
                    a, b = (w.rearrange("p (k n) -> p k n", k=2) for w in parts((kind, L, i)))
                    for t in range(TT):
                        xs = slice(t * P, (t + 1) * P)
                        steps = [(k, x3, w3, h) for k in (2 * i, 2 * i + 1) for x3, w3 in ((sh, a), (sh, b), (sl, a)) for h in range(2)]
                        if i == ni - 1:
                            steps.sort(key=lambda v: v[3])
                        if t == 0:
                            ready(2 * i)
                            ready(2 * i + 1)
                        for k, x3, w3, h in steps:
                            ins = mm(ps[:, 2 * t + h, :], x3[:, k, xs], w3[:, k % 2, h * 512:(h + 1) * 512],
                                     start=k == 0 and w3 is a and x3 is sh, stop=k == nk - 1 and x3 is sl)
                            if k == nk - 1 and x3 is sl:
                                fill(ins, (unit, L, t, h))
                    if i < ni - 1:
                        leave(ins, (kind, L, i))
                    if after:
                        after(i)

            def ada(q):
                b = claim(("ada", q))
                pe.wait_ge(ada_summed, q + 1)
                for c in range(4):
                    ins = mm(ps[:, b, c:c + 1], adasum[:, c * P:(c + 1) * P], ones[:, 0:1], start=True, stop=True)
                fill(ins, ("ada", q))

            def ffn(L):
                for i in range(NGU):
                    a, b = (w.rearrange("p (v k n) -> p v k n", v=2, k=KC) for w in parts(("gu", L, i)))
                    bank = claim(("gu", L, i))
                    for v in range(2):
                        o = ps[:, bank, v * S:(v + 1) * S]
                        for k in range(KC):
                            if i == 0 and v == 0 and k % 2 == 0:
                                columns_ready("hT", L, k // 2)
                            mm(o, a[:, v, k, :], xh[:, k, :], start=k == 0, stop=False)
                            mm(o, a[:, v, k, :], xl[:, k, :], start=False, stop=False)
                            ins = mm(o, b[:, v, k, :], xh[:, k, :], start=False, stop=k == KC - 1)
                    fill(ins, ("gu", L, i))
                    if L < 2 and i in ADA_GU:
                        ada(ADA_FFN[L][ADA_GU[i]])
                product_rows("dn", "d", L, gh, gl, FC, lambda k: pe.wait_ge(gated_ready, FC * L + k + 1),
                             lambda i: ada(ADA_FFN[L][3]) if L < 2 and i == ADA_DN else None)

            def attention(L):
                js = JOBS[L]
                for k in range(len(js) + 3):
                    if k < len(js):
                        j = js[k]
                        b = claim(("s", L, k))
                        if k == 0 and L == 2:
                            wait_done(pe, ("nT", 8))
                            wait_done(pe, ("cmp2",))
                        (qs, qp), kk = j.q, j.kk
                        for t in range(TT):
                            a, e = score_cols(j, t)
                            if j.kind == "cmp":
                                keys = kcmp[qp:qp + kk, 0:NCMP]
                            else:
                                keys = ut[j.k[1]:j.k[1] + kk, j.k[0], 0:(t + 1) * P]
                            ins = mm(ps[:, b, a:e], ut[qp:qp + kk, qs, t * P:(t + 1) * P], keys, start=True, stop=True)
                        fill(ins, ("s", L, k))
                    if 0 <= k - 2 < len(js):
                        j, n = js[k - 2], k - 2
                        b = claim(("pt", L, n))
                        pe.wait_ge(probs_ready, JOB0[L] + n + 1)
                        src = probs[:, n % 4, :]
                        if j.kind == "cmp":
                            for t in range(TT):
                                ins = nc.tensor.transpose(ps[0:NCMP, b, t * P:(t + 1) * P], src[:, 16 * t:16 * t + NCMP], ident)
                        else:
                            for c in range(3):
                                ins = nc.tensor.transpose(ps[:, b, c * P:(c + 1) * P], src[:, c * P:(c + 1) * P], ident)
                        fill(ins, ("pt", L, n))
                    if 0 <= k - 3 < len(js):
                        j, n = js[k - 3], k - 3
                        if n == 0 or js[n - 1].group != j.group:
                            for t in range(TT):
                                claim(("o", L, j.group, t))
                        wait_done(pe, ("pt", L, n))
                        b = OBANK[j.group]
                        wide = P if j.kind != "cmp" and (j.col + 2) * HD <= 512 else HD
                        o = slice(j.col * HD, j.col * HD + wide)
                        src = pT[:, n % 2, :]
                        if j.kind == "cmp":
                            for t in range(TT):
                                ins = mm(ps[:, b + t, o], src[0:NCMP, t * P:(t + 1) * P], value_of(j, t), start=True, stop=True)
                                if j.last:
                                    fill(ins, ("o", L, j.group, t))
                        else:
                            ins = mm(ps[:, b, o], src[:, 0:P], value_of(j, 0, wide), start=True, stop=True)
                            if j.last:
                                fill(ins, ("o", L, j.group, 0))
                            mm(ps[:, b + 1, o], src[:, P:S], value_of(j, 0, wide), start=True, stop=False)
                            ins = mm(ps[:, b + 1, o], src[:, S:384], value_of(j, 1, wide), start=False, stop=True)
                            if j.last:
                                fill(ins, ("o", L, j.group, 1))
                    if L < 2 and k in ADA_STEP:
                        ada(ADA_ATT[L][ADA_STEP[k]])

            pe.wait_ge(s_cst, 16)
            to_columns("xT", 0, x, lambda t: pe.wait_ge(s_x, 16))

            for L in range(DEPTH):
                product_win(L)
                if L == 0:
                    pe.wait_ge(s_vec, 16 * 22)
                    for n, (rows, cnt) in enumerate(((rowsA, N_A), (rowsB, N_B))):
                        claim(("fv", n))
                        fill(nc.tensor.transpose(ps[:, 4 + n, 0:cnt], rows[0:cnt, :], ident[0:cnt, 0:cnt]), ("fv", n))
                    claim(("relb",))
                    pe.wait_ge(s_const, 16 * 3)
                    fill(mm(ps[0:A_H + B_H, 6, 0:384], relb[:, :], hot[:, :], start=True, stop=True), ("relb",))
                wait_done(pe, ("win", L, 4, 0))
                wait_done(pe, ("win", L, 4, 1))
                for n in range(5):
                    b = claim(("ab", L, n))
                    for c in range(2):
                        s = 2 * n + c
                        col = s * P if s < 6 else B_Q + (s - 6) * P
                        for t in range(TT):
                            o = c * S + t * P
                            ins = nc.tensor.transpose(ps[:, b, o:o + P], proj[:, t, col:col + P], ident)
                    fill(ins, ("ab", L, n))
                pe.wait_ge(ev("latent", L), 1)
                for n, cs in enumerate(((0, 1), (2,))):
                    b = claim(("c", L, n))
                    for c in cs:
                        for t in range(TT):
                            o = (c % 2) * S + t * P
                            ins = nc.tensor.transpose(ps[:, b, o:o + P], z[:, t, c * P:(c + 1) * P], ident)
                    fill(ins, ("c", L, n))
                w = arrive(("lora", L))
                wait_done(pe, ("c", L, 1))
                for t in range(TT):
                    for h in range(2):
                        b = claim(("uq", L, t, h))
                        for k in range(2):
                            ins = mm(ps[:, b, 0:288], cT[:, k, t * P:(t + 1) * P], w[:, 576 * k + 288 * h:576 * k + 288 * h + 288], start=k == 0, stop=k == 1)
                        fill(ins, ("uq", L, t, h))
                for t in range(TT):
                    for h in range(2):
                        b = claim(("ukv", L, t, h))
                        fill(mm(ps[:, b, 0:384], cT[:, 2, t * P:(t + 1) * P], w[:, 1152 + 384 * h:1536 + 384 * h], start=True, stop=True), ("ukv", L, t, h))
                pe.wait_ge(ev("latent_q", L), 1)
                pe.wait_ge(ev("latent_k", L), 1)
                for n in range(6):
                    b = claim(("ct", L, n))
                    for c in range(2):
                        s = 2 * n + c
                        col = s * CQ if s < 6 else 960 + (s - 6) * CQ
                        for t in range(TT):
                            o = c * S + t * P
                            ins = nc.tensor.transpose(ps[0:CQ, b, o:o + P], cbuf[:, t, col:col + CQ], ident)
                    fill(ins, ("ct", L, n))
                if L == 0:
                    pe.wait_ge(s_bias_in, 16)
                    for n in range(5):
                        b = claim(("flip", n))
                        fill(mm(ps[:, b, :], cv("flip"), bias[:, 2 * n:2 * n + 2, :].rearrange("p h n -> p (h n)"), start=True, stop=True), ("flip", n))
                wait_done(pe, ("ct", L, 4))
                wait_done(pe, ("ct", L, 5))
                attention(L)
                wait_done(pe, ("o", L, 2, 1))
                to_columns("ht", L, z, lambda t: None)
                product_rows("wo", "y", L, xh, xl, KC, lambda k: columns_ready("ht", L, k // 2))
                to_columns("hT", L, z, lambda t: pe.wait_ge(ev("norm1", L), t + 1))
                ffn(L)
                if L == 1:
                    for v in range(2):
                        pe.wait_ge(ev("diag", v), 1)
                        for h in range(2):
                            b = claim(("G", v, h))
                            for c in range(4):
                                o = (4 * h + c) * P
                                ins = mm(ps[:, b, c * P:(c + 1) * P], ones[:, :], spare[:, D * v + o:D * v + o + P], start=True, stop=True)
                            fill(ins, ("G", v, h))
                to_columns("xT", L + 1, z, lambda t: pe.wait_ge(ev("norm2" if L < 1 else "norm_in", L), t + 1))

            L = 2
            product_win(L)
            rows_at = [(proj, NQ, P), (proj, NQ + 2 * P, P), (proj, DQ, P), (proj, DQ + 2 * P, P), (proj, NKS, NKW - NKS),
                       (cbuf, 1024, P), (cbuf, 1024 + 2 * P, P), (cbuf, 0, P), (cbuf, 2 * P, P)]

            def turn(n):
                src, col, step = rows_at[n]
                b = claim(("nT", n))
                for c in range(2):
                    for t in range(TT):
                        o = c * S + t * P
                        ins = nc.tensor.transpose(ps[:, b, o:o + P], src[:, t, col + c * step:col + c * step + P], ident)
                fill(ins, ("nT", n))

            pe.wait_ge(ev("dup_rows"), 1)
            turn(5)
            turn(6)
            wait_done(pe, ("nT", 5))
            wait_done(pe, ("nT", 6))
            b = claim(("cmp1",))
            for v in range(2):
                w = arrive(("w1", v)).rearrange("p (c n) -> p c n", c=16)
                for c in range(16):
                    keys = ut[:, 15 + 2 * v:17 + 2 * v, 2 * c:2 * c + 16 * (NCMP - 1) + 1:16]
                    mm(ps[:, b, 32 * v:32 * v + 30].rearrange("p (g n) -> p g n", g=2), w[:, c, :], keys, start=c == 0, stop=c == 15)
            for v in range(2):
                pe.wait_ge(ev("pe_sum"), v + 1)
                ins = mm(ps[:, b, 32 * v + 30:32 * v + 31], spare[:, v * P:(v + 1) * P], ones[:, 0:1], start=True, stop=True)
            fill(ins, ("cmp1",))
            pe.wait_ge(ev("idx_rows"), 1)
            for n in range(3):
                b = claim(("idxT", n))
                for c in range(2 if n < 2 else 1):
                    for t in range(TT):
                        o = c * S + t * P
                        src = proj[:, t, IQ + (2 * n + c) * P:IQ + (2 * n + c + 1) * P] if n < 2 else z[:, t, 0:P]
                        ins = nc.tensor.transpose(ps[:, b, o:o + P], src, ident)
                fill(ins, ("idxT", n))
            wait_done(pe, ("idxT", 2))
            wait_done(pe, ("idxT", 1))
            for h in range(8):
                b = claim(("lg", h))
                q = 64 * (h % 2)
                for t in range(TT):
                    ins = mm(ps[:, b, 0:P] if t == 0 else ps[:, b, P:384], ut[q:q + 64, 8 + h // 2, t * P:(t + 1) * P], ut[q:q + 64, 14, 0:(t + 1) * P], start=True, stop=True)
                fill(ins, ("lg", h))
            pe.wait_ge(ev("ckv_rows"), 1)
            b = claim(("ckvT",))
            for t in range(TT):
                ins = nc.tensor.transpose(ps[:, b, t * P:(t + 1) * P], z[:, t, P:S], ident)
            fill(ins, ("ckvT",))
            wait_done(pe, ("ckvT",))
            wsm = arrive(("small",))
            for t in range(TT):
                b = claim(("kd", t))
                fill(mm(ps[:, b, 0:384], cT[:, 0, t * P:(t + 1) * P], wsm[:, 0:384], start=True, stop=True), ("kd", t))
            for t in range(TT):
                b = claim(("vd", t))
                fill(mm(ps[:, b, :], cT[:, 0, t * P:(t + 1) * P], wsm[:, 384:896], start=True, stop=True), ("vd", t))
            pe.wait_ge(ev("rope_rows"), 1)
            for n in range(5):
                turn(n)
            pe.wait_ge(ev("dk_rows"), 1)
            turn(7)
            turn(8)
            pe.wait_ge(ev("hidden"), 1)
            b = claim(("cmp2",))
            for g in range(2):
                mm(ps[64 * g:64 * g + 64, b, 0:NCMP], wsm[:, 896:960], hid[:, 3, NCMP * g:NCMP * (g + 1)], start=True, stop=True)
            for g in range(2):
                ins = mm(ps[0:NCMP, b, 64 + 64 * g:128 + 64 * g], hid[:, 3, 30 + NCMP * g:30 + NCMP * (g + 1)], wsm[:, 960:1024], start=True, stop=True)
            fill(ins, ("cmp2",))
            attention(L)
            wait_done(pe, ("o", L, 3, 1))
            to_columns("ht", L, z, lambda t: None)
            product_rows("wo", "y", L, xh, xl, KC, lambda k: columns_ready("ht", L, k // 2))
            to_columns("hT", L, z, lambda t: pe.wait_ge(ev("norm1", L), t + 1))
            ffn(L)

        def affine(name, L, c):
            if name == "xT" and L == 2:
                return aff[:, 0, c:c + 1], modv[:, c:c + 1]
            if name == "hT" and L == 2:
                return aff[:, 1, c:c + 1], modv[:, 24 + c:25 + c]
            k = ("ln2", L - 1) if name == "xT" else ("ln1", L)
            g, b = FVAT[k[0] + "_g"] + 8 * k[1] + c, FVAT[k[0] + "_b"] + 8 * k[1] + c
            return fv[:, g:g + 1], fv[:, b:b + 1]

        def feed(split, item, kind):
            m = SPLIT[item] + NW
            if m < len(SPLITS) and SPLITS[m][0] in kind:
                split(SPLITS[m])

        def start(split, kind, L, a=0, b=NW):
            m = SPLIT[(kind, L, 0, 0) if kind == "win" else (kind, L, 0)]
            for k in SPLITS[m + a:m + b]:
                split(k)

        @block.scalar
        def _(act):
            me = Steps(act, act_step, done_act, "act")
            activation = nc.scalar.activation

            def copy(dst, src, key):
                wait_full(act, key)
                me.empty(activation(dst, src, ACT.Copy), key)

            def split(item):
                m = SPLIT[item]
                if m >= NW:
                    wait_released(act, SPLITS[m - NW])
                act.wait_ge(landed[ITEM[item] % NRAW], LANDED[item])
                n = split_width(item)
                me.go(activation(wh[:, m % NW, 0:n], raw[:, ITEM[item] % NRAW, 0:n], ACT.Copy), wh_ready)

            def columns(name, L):
                if name == "xT" and L == 2:
                    act.wait_ge(ev("mod"), 1)
                for u in range(4):
                    key = (name, L, u)
                    wait_full(act, key)
                    b = U.bank[key]
                    if U.eng[key] == "dve":
                        me.go(activation(xh[:, 2 * u:2 * u + 2, :], ps[:, b, :].rearrange("p (c n) -> p c n", c=2), ACT.Copy), ev("upper"))
                        continue
                    for c in range(2):
                        g, s = affine(name, L, 2 * u + c)
                        ins = activation(vcols[:, u, c * S:(c + 1) * S], ps[:, b, c * S:(c + 1) * S], ACT.Identity, bias=s, scale=g)
                    me.empty(ins, key)

            def win(L):
                for i in range(5):
                    for h in range(2):
                        feed(split, ("win", L, i, h), "win")
                    copy(*win_views(L, i, 0, win_width(L, i), U.bank[("win", L, i, 0)]), ("win", L, i, 0))

            def softmax(L):
                js = JOBS[L]
                for k in range(len(js) + 3):
                    if k < len(js):
                        j = js[k]
                        wait_done(act, ("s", L, k))
                        for t in range(TT):
                            a, e = score_cols(j, t)
                            ins = activation(probs[:, k % 4, a:e], probs[:, k % 4, a:e], ACT.Exp, bias=nmx[:, k % 4, t:t + 1],
                                             accum_out=sums[:, j.group % 2, t, j.col:j.col + 1])
                        me.go(ins, probs_ready)
                    n = k - 2
                    if 0 <= n < len(js) and alt(n) == "act":
                        copy(*pt_views(L, n), ("pt", L, n))
                    if L < 2 and 1 <= k <= 16:
                        if L == k - 1 == 0:
                            act.wait_ge(ev("cact"), 1)
                        scale_ada(ADA_ATT[L][(k - 1) // 8], (k - 1) % 8)
                    if k >= len(js):
                        start(split, "wo", L, k - len(js), k - len(js) + 1)

            def squares(L, unit):
                for t in range(TT):
                    wait_full(act, (unit, L, t, 1))
                    if t == 1:
                        me.settle()
                    me.go(activation(tw[:, :, :], ps[:, 2 * t:2 * t + 2, :], ACT.Square, accum_out=va[:, t, 0:1]), ev("squares", unit))

            def scale_ada(q, n):
                item = ("ada", q, n // 4)
                if n % 4 == 0:
                    act.wait_ge(landed[ITEM[item] % NRAW], LANDED[item])
                w = raw[:, ITEM[item] % NRAW, (n % 4) * 512:(n % 4 + 1) * 512]
                me.go(activation(w, w, ACT.Copy, scale=cact[:, n:n + 1]), ada_scaled)

            def gates(L):
                for i in range(NGU):
                    feed(split, ("gu", L, i), ("gu", "dn"))
                    key = ("gu", L, i)
                    wait_full(act, key)
                    me.go(activation(gsilu[:, i % 4, :], ps[:, U.bank[key], 0:S], ACT.Silu), silu_ready)
                    if L < 2 and i + ADA_EARLY in ADA_AFTER:
                        h = ADA_AFTER[i + ADA_EARLY]
                        for n in range(4):
                            scale_ada(ADA_FFN[L][h // 2], 4 * (h % 2) + n)
                for i in range(FC // 2 - NW):
                    feed(split, ("dn", L, i), "dn")
                    if L < 2 and i + 2 in ADA_AFTER_DN:
                        for n in range(4):
                            scale_ada(ADA_FFN[L][3], ADA_AFTER_DN[i + 2] % 2 * 4 + n)
                if L < 2:
                    start(split, "win", L + 1, 0, 1)

            def products_wo(L):
                for i in range(KC // 2 - NW):
                    feed(split, ("wo", L, i), "wo")
                start(split, "gu", L, 0, 1)

            act.dma_start(cst[:, :], A["consts"]).then_inc(s_cst, 16)
            start(split, "win", 0, 0, 1)
            columns("xT", 0)
            start(split, "win", 0, 1)
            for L in range(DEPTH):
                win(L)
                if L == 0:
                    act.wait_ge(ev("fv"), 1)
                    act.wait_ge(ev("lamsum"), 1)
                    me.go(activation(ctmp[:, :], fv[:, FVAT["c_2"]:FVAT["c_2"] + KC], ACT.Exp, scale=-1.0), ev("cexp"))
                    me.go(activation(lamp[:, :, :], lamp[:, :, :], ACT.Exp), ev("lamexp"))
                for n in (0, 2, 4):
                    copy(ut[:, 2 * n:2 * n + 2, :], ps[:, U.bank[("ab", L, n)], :].rearrange("p (c n) -> p c n", c=2), ("ab", L, n))
                for n, cs in enumerate(((0, 1), (2,))):
                    key = ("c", L, n)
                    wait_full(act, key)
                    for c in cs:
                        g = FVAT["q_norm_g"] + 2 * L + c if c < 2 else FVAT["kv_norm_g"] + L
                        ins = activation(cT[:, c, :], ps[:, U.bank[key], (c % 2) * S:(c % 2 + 1) * S], ACT.Copy, scale=fv[:, g:g + 1])
                    me.empty(ins, key)
                for t in range(TT):
                    for h in range(2):
                        copy(cbuf[:, t, 288 * h:288 * h + 288], ps[:, U.bank[("uq", L, t, h)], 0:288], ("uq", L, t, h))
                for n in (0, 2, 4):
                    copy(ut[0:CQ, 10 + 2 * n:12 + 2 * n, :], ps[0:CQ, U.bank[("ct", L, n)], :].rearrange("p (c n) -> p c n", c=2), ("ct", L, n))
                softmax(L)
                columns("ht", L)
                products_wo(L)
                start(split, "gu", L, 1)
                columns("hT", L)
                gates(L)
                start(split, "win", L + 1, 1)
                if L == 1:
                    for t in range(TT):
                        act.wait_ge(ev("resid", 1, 2), t + 1)
                        act.wait_ge(ev("resid_left"), t + 1)
                        if t == 1:
                            me.settle()
                        me.go(activation(tw[:, :, :].rearrange("p a b -> p (a b)"), x[:, t, :], ACT.Square, accum_out=va[:, t, 0:1]), ev("squares", "in"))
                    for v in range(2):
                        for h in range(2):
                            copy(lnb[:, v, 512 * h:512 * h + 512], ps[:, U.bank[("G", v, h)], :], ("G", v, h))
                columns("xT", L + 1)
            L = 2
            win(L)
            me.go(activation(gt[:, :, :], proj_gates(act), ACT.Exp, scale=-1.0), ev("gexp"))
            wait_full(act, ("nT", 6))
            me.empty(shifted(activation, 6, ACT.Copy), ("nT", 6))
            for n in (0, 2):
                w = 2 if n == 0 else 1
                copy(ut[:, 8 if n == 0 else 14, :] if w == 1 else ut[:, 8:10, :], ps[:, U.bank[("idxT", n)], 0:w * S] if w == 1 else
                     ps[:, U.bank[("idxT", n)], :].rearrange("p (c n) -> p c n", c=2), ("idxT", n))
            act.wait_ge(ev("gelu_arg"), 1)
            me.go(activation(hid[:, 2, :], hid[:, 1, :], ACT.Exp, scale=-2.0 * GELU_C), ev("gelu_exp"))
            for h in range(8):
                if h >= 4:
                    act.wait_ge(ev("idx_added"), h - 3)
                wait_full(act, ("lg", h))
                me.empty(activation(probs[:, h % 4, :], ps[:, U.bank[("lg", h)], 0:384], ACT.Relu), ("lg", h))
            key = ("ckvT",)
            g = FVAT["g_kv_norm_2"]
            wait_full(act, key)
            me.empty(activation(cT[:, 0, :], ps[:, U.bank[key], 0:S], ACT.Copy, scale=fv[:, g:g + 1]), key)
            for t in range(TT):
                copy(vd[:, t, :], ps[:, U.bank[("vd", t)], :], ("vd", t))
            for n in (0, 2, 4):
                copy(*turned(n), ("nT", n))
            copy(*turned(8), ("nT", 8))
            softmax(L)
            columns("ht", L)
            products_wo(L)
            squares(L, "y")
            for t in range(TT):
                act.wait_ge(ev("mixed"), t + 1)
                if t == 1:
                    me.settle()
                me.go(activation(tw[:, :, :].rearrange("p a b -> p (a b)"), x[:, t, :], ACT.Square, accum_out=va[:, t, 1:2]), ev("squares", "mid"))
            start(split, "gu", L, 1)
            columns("hT", L)
            gates(L)
            squares(L, "d")

        @block.vector
        def _(dve):
            me = Steps(dve, dve_step, done_dve, "dve")
            V = nc.vector

            def copy(dst, src, key):
                wait_full(dve, key)
                me.empty(V.tensor_copy(dst, src), key)

            def split(item):
                m = SPLIT[item]
                dve.wait_ge(wh_ready, m + 1)
                n = split_width(item)
                me.go(V.tensor_tensor(wl[:, m % NW, 0:n], raw[:, ITEM[item] % NRAW, 0:n], wh[:, m % NW, 0:n].bitcast(F32), ALU.subtract), wl_ready)

            uppers = [0]

            def columns(name, L):
                for u in range(4):
                    key = (name, L, u)
                    a, b = xh[:, 2 * u:2 * u + 2, :], xl[:, 2 * u:2 * u + 2, :]
                    if U.eng[key] == "dve":
                        uppers[0] += 1
                        dve.wait_ge(ev("upper"), uppers[0])
                        src = ps[:, U.bank[key], :].rearrange("p (c n) -> p c n", c=2)
                        me.empty(V.tensor_tensor(b, src, a.bitcast(F32), ALU.subtract), key)
                        continue
                    wait_done(dve, key)
                    v = vcols[:, u, :].rearrange("p (c n) -> p c n", c=2)
                    me.go(V.tensor_copy(a, v))
                    me.settle()
                    me.go(V.tensor_tensor(b, v, a.bitcast(F32), ALU.subtract), cols_ready)

            def win(L):
                for i in range(5):
                    for h in range(2):
                        feed(split, ("win", L, i, h), "win")
                    copy(*win_views(L, i, 1, win_width(L, i), U.bank[("win", L, i, 1)]), ("win", L, i, 1))
                wait_done(dve, ("win", L, 4, 0))
                me.settle()

            def norm(L, unit, ln):
                if (L, unit) != (0, "y"):
                    dve.wait_ge(ev("resid", *((L, 1) if unit == "d" else (L - 1, 2))), 2)
                for t in range(TT):
                    for h in range(2):
                        key = (unit, L, t, h)
                        wait_full(dve, key)
                        xs = x[:, t, 512 * h:512 * h + 512]
                        me.empty(V.scalar_tensor_tensor(out=xs, in0=xs, scalar=ALPHA, in1=ps[:, U.bank[key], :], op0=ALU.mult, op1=ALU.add), key)
                        me.settle()
                        me.go(V.bn_stats(st[:, t, h, :], xs))
                    me.settle()
                    me.go(V.bn_aggr(mv[:, t, :], st[:, t, :, :].rearrange("p a b -> p (a b)")))
                    me.settle()
                    me.go(V.tensor_scalar(va[:, t, 0:1], mv[:, t, 1:2], 1e-5, None, ALU.add), ev("var", ln, L))
                    dve.wait_ge(ev("rstd", ln, L), t + 1)
                    me.go(V.tensor_scalar(z[:, t, :], x[:, t, :], mv[:, t, 0:1], rs[:, t, 0:1], ALU.subtract, ALU.mult), ev("norm%d" % ln, L))
                    if (L, unit) == (1, "d"):
                        dve.wait_ge(s_lnb, 32 * 4)
                        me.settle()
                        me.go(V.tensor_tensor(x[:, t, 0:LEFT], z[:, t, 0:LEFT], lnb[:, 0, 0:LEFT], ALU.mult))
                        me.settle()
                        me.go(V.tensor_tensor(x[:, t, 0:LEFT], x[:, t, 0:LEFT], lnb[:, 1, 0:LEFT], ALU.add), ev("resid_left"))

            def ada(q):
                copy(modv[:, 4 * q:4 * q + 4], ps[:, U.bank["ada", q], 0:4], ("ada", q))

            def ffn(L):
                for i in range(NGU):
                    feed(split, ("gu", L, i), ("gu", "dn"))
                    key = ("gu", L, i)
                    dve.wait_ge(silu_ready, NGU * L + i + 1)
                    g = gated[:, i % 4, :]
                    me.empty(V.tensor_tensor(g, gsilu[:, i % 4, :], ps[:, U.bank[key], S:2 * S], ALU.mult), key)
                    me.settle()
                    me.go(V.tensor_copy(gh[:, i, :], g))
                    me.settle()
                    me.go(V.tensor_tensor(gl[:, i, :], g, gh[:, i, :].bitcast(F32), ALU.subtract), gated_ready)
                    if L < 2 and i in ADA_GU:
                        ada(ADA_FFN[L][ADA_GU[i]])
                for i in range(FC // 2 - NW):
                    feed(split, ("dn", L, i), "dn")
                if L < 2:
                    ada(ADA_FFN[L][3])
                    start(split, "win", L + 1, 0, 1)

            def products_wo(L):
                for i in range(KC // 2 - NW):
                    feed(split, ("wo", L, i), "wo")
                start(split, "gu", L, 0, 1)

            def outputs(L, g):
                gp, n = g % 2, {0: (6, 8, 6), 1: (6, 8, 6), 2: (8, 8, 8, 8)}[L][g]
                kind = GROUPS[L][g]
                r = rec[:, gp, :, 0:n]
                for t in range(TT):
                    wait_full(dve, ("o", L, g, t))
                me.go(V.reciprocal(r, sums[:, gp, :, 0:n]))
                me.settle()
                if kind == "B":
                    me.go(V.tensor_scalar(rec[:, gp, :, 1:8:2], rec[:, gp, :, 1:8:2], neglam[:, L:L + 1], None, ALU.mult))
                    me.settle()
                if kind in ("slc", "win", "cmp"):
                    a = {"cmp": 0, "slc": 8, "win": 16}[kind]
                    me.go(V.tensor_tensor(r, r, gt[:, :, a:a + 8], ALU.mult))
                    me.settle()
                for t in range(TT):
                    key = ("o", L, g, t)
                    o = ps[:, U.bank[key], 0:n * HD].rearrange("p (h d) -> p h d", d=HD)
                    rr = rec[:, gp, t, 0:n].unsqueeze(2).broadcast_to([P, n, HD])
                    dst = {"A": (z, 0), "B": (tw, 0), "C": (z, 640), "slc": (z, 0), "win": (tw, 0), "cmp": (tw, 0), "dsa": (z, 512)}[kind]
                    d = dst[0][:, t, dst[1]:dst[1] + n * HD]
                    me.empty(V.tensor_tensor(d.rearrange("p (h d) -> p h d", d=HD), o, rr, ALU.mult), key)
                    yield
                if kind in ("win", "cmp"):
                    me.settle()
                    for t in range(TT):
                        me.go(V.tensor_tensor(z[:, t, 0:512], z[:, t, 0:512], tw[:, t, :], ALU.add))
                        yield
                if kind == "B":
                    me.settle()
                    for t in range(TT):
                        w = tw[:, t, :].rearrange("p (h i d) -> p h i d", i=2, d=HD)
                        me.go(V.tensor_tensor(z[:, t, 384:640].rearrange("p (h d) -> p h d", d=HD), w[:, :, 0, :], w[:, :, 1, :], ALU.add))
                    yield
                    me.settle()
                    for t in range(TT):
                        me.go(V.tensor_tensor(tw[:, t, 0:256], z[:, t, 384:640], z[:, t, 384:640], ALU.mult))
                    yield
                    me.settle()
                    for t in range(TT):
                        me.go(V.tensor_reduce(vb[:, t, :], tw[:, t, 0:256].rearrange("p (h d) -> p h d", d=HD), AX.X, ALU.add))
                    me.settle()
                    me.go(V.tensor_scalar(vb[:, :, :], vb[:, :, :], 1.0 / HD, 1e-5, ALU.mult, ALU.add), ev("var_b", L))

            def subnorm(L):
                dve.wait_ge(ev("rstd_b", L), 1)
                for t in range(TT):
                    o = z[:, t, 384:640].rearrange("p (h d) -> p h d", d=HD)
                    me.go(V.tensor_tensor(o, o, rb[:, t, :].unsqueeze(2).broadcast_to([P, B_H, HD]), ALU.mult))
                me.settle()
                for t in range(TT):
                    o = z[:, t, 384:640].rearrange("p (h d) -> p h d", d=HD)
                    me.go(V.tensor_tensor(o, o, sg[:, L, :].unsqueeze(1).broadcast_to([P, B_H, HD]), ALU.mult))

            def top_keys(r):
                if r < TOPK // 8:
                    for t, (a, e) in enumerate(((0, P), (P, 384))):
                        me.go(V.max(m8[:, t, :], dmask[:, a:e]))
                    me.settle()
                    for t, (a, e) in enumerate(((0, P), (P, 384))):
                        me.go(V.match_replace(out=dmask[:, a:e], in_to_replace=m8[:, t, :], in_values=dmask[:, a:e], imm_value=TAKEN))
                    me.settle()
                    return
                me.go(V.tensor_scalar(dmask[:, :], dmask[:, :], TAKEN / 1.5, NEG, ALU.is_gt, ALU.mult))
                me.settle()
                me.go(V.tensor_tensor(dmask[:, 0:P], dmask[:, 0:P], cv("causal")[:, P:S], ALU.add))
                me.go(V.tensor_tensor(dmask[:, P:384], dmask[:, P:384], cv("causal"), ALU.add))
                me.settle()

            def softmax(L):
                js = JOBS[L]
                todo = {}
                if L == 2:
                    for r in range(TOPK // 8 + 1):
                        todo[2 * r + 2] = [lambda r=r: top_keys(r)]
                for k in range(len(js) + 3):
                    if k < len(js):
                        j, key = js[k], ("s", L, k)
                        wait_full(dve, key)
                        for t in range(TT):
                            a, e = score_cols(j, t)
                            me.go(V.tensor_tensor_reduce(out=probs[:, k % 4, a:e], in0=ps[:, U.bank[key], a:e], in1=mask_of(j, t), scale=j.scale,
                                                         scalar=-3.4e38, op0=ALU.add, op1=ALU.max, accum_out=mx[:, k % 4, t:t + 1]))
                        me.settle()
                        me.empty(V.tensor_scalar(nmx[:, k % 4, :], mx[:, k % 4, :], -1.0, None, ALU.mult), key)
                    n = k - 2
                    if 0 <= n < len(js) and alt(n) == "dve":
                        copy(*pt_views(L, n), ("pt", L, n))
                    for f in todo.pop(k, []):
                        f()
                    if k >= len(js):
                        start(split, "wo", L, k - len(js), k - len(js) + 1)
                    if 0 <= k - 3 < len(js) and js[k - 3].last:
                        g = js[k - 3].group
                        pieces = outputs(L, g)
                        for n in range(PIECES[GROUPS[L][g]]):
                            todo.setdefault(k + 1 + n, []).append(lambda pieces=pieces: next(pieces, None))
                        if L < 2 and g == 1:
                            todo.setdefault(k + 7, []).append(lambda: subnorm(L))
                    if L < 2 and k in ADA_STEP:
                        todo.setdefault(k + 1, []).append(lambda q=ADA_ATT[L][ADA_STEP[k]]: ada(q))
                for k in sorted(todo):
                    for f in todo[k]:
                        f()

            def mean_rms(t, unit, col, sem_in, want, out_sem):
                dve.wait_ge(sem_in, want)
                me.go(V.tensor_scalar(va[:, t, col:col + 1], va[:, t, col:col + 1], 1.0 / D, 1e-6, ALU.mult, ALU.add), out_sem)

            def add_gated(L, unit, v, out_ev):
                for t in range(TT):
                    mean_rms(t, unit, 0, ev("squares", unit), t + 1, ev("var_" + unit))
                for t in range(TT):
                    dve.wait_ge(ev("rstd_" + unit), t + 1)
                    for h in range(2):
                        key = (unit, L, t, h)
                        me.empty(V.scalar_tensor_tensor(out=junk[:, 512 * h:512 * h + 512], in0=ps[:, U.bank[key], :], scalar=rs[:, t, 0:1],
                                                        in1=lnb[:, v, 512 * h:512 * h + 512], op0=ALU.mult, op1=ALU.mult), key)
                    me.settle()
                    me.go(V.tensor_tensor(x[:, t, :], x[:, t, :], junk[:, :], ALU.add), out_ev(t))
                    me.settle()

            def rope(xs, c, s, tmp, n, half, dst=None):
                a, b = xs[:, :, :, 0:half], xs[:, :, :, half:2 * half]
                cb, sb_ = (v.unsqueeze(2).broadcast_to([P, TT, n, half]) for v in (c, s))
                w = [tmp[:, i * TT * n * half:(i + 1) * TT * n * half].rearrange("p (t h d) -> p t h d", t=TT, h=n) for i in range(4)]
                for i, (u, v) in enumerate(((a, cb), (b, sb_), (b, cb), (a, sb_))):
                    me.go(V.tensor_tensor(w[i], u, v, ALU.mult))
                me.settle()
                me.go(V.tensor_tensor(a, w[0], w[1], ALU.subtract))
                return V.tensor_tensor(b, w[2], w[3], ALU.add)

            c1, s1, c2, s2 = (cv(n).rearrange("p (t d) -> p t d", t=TT) for n in ("cos1", "sin1", "cos2", "sin2"))
            start(split, "win", 0, 0, 1)
            columns("xT", 0)
            start(split, "win", 0, 1)
            for L in range(DEPTH):
                win(L)
                if L == 0:
                    dve.wait_ge(s_vec, 16 * 22)
                    dve.wait_ge(s_cst, 16)
                    for l in range(DEPTH):
                        v = lamin[:, l, :].rearrange("p (i j d) -> p i j d", i=2, j=2)
                        me.go(V.tensor_tensor(junk[:, 64 * l:64 * l + 64].rearrange("p (i d) -> p i d", i=2), v[:, :, 0, :], v[:, :, 1, :], ALU.mult))
                    me.settle()
                    me.go(V.tensor_reduce(lamp[:, :, :].rearrange("p a b -> p (a b)"), junk[:, 0:128].rearrange("p (i d) -> p i d", d=32), AX.X, ALU.add), ev("lamsum"))
                    for n, cnt in enumerate((N_A, N_B)):
                        wait_full(dve, ("fv", n))
                        me.empty(V.tensor_copy(fv[:, n * N_A:n * N_A + cnt], ps[:, 4 + n, 0:cnt]), ("fv", n))
                    me.settle()
                    for l in range(DEPTH):
                        ins = V.tensor_scalar(sg[:, l, :], sg[:, l, :], 1.0 - LAM0[l], None, ALU.mult)
                    me.go(ins, ev("fv"))
                    wait_full(dve, ("relb",))
                    me.empty(V.tensor_scalar(brow[:, :], ps[0:A_H + B_H, 6, 0:384], cv("biasscale")[0:A_H + B_H, :], None, ALU.mult), ("relb",))
                    me.settle()
                    me.go(V.tensor_copy(mx[0:1, 0, 0:1], brow[0:1, 0:1]), ev("brow"))
                    dve.wait_ge(ev("cexp"), 1)
                    me.go(V.tensor_scalar(ctmp[:, :], ctmp[:, :], 1.0, None, ALU.add))
                    me.settle()
                    me.go(V.reciprocal(ctmp[:, :], ctmp[:, :]))
                    me.settle()
                    c0 = FVAT["c_2"]
                    me.go(V.tensor_tensor(cact[:, :], ctmp[:, :], fv[:, c0:c0 + KC], ALU.mult), ev("cact"))
                    dve.wait_ge(ev("lamexp"), 1)
                    for l in range(DEPTH):
                        me.go(V.tensor_tensor(neglam[:, l:l + 1], lamp[:, l, 1:2], lamp[:, l, 0:1], ALU.subtract))
                    me.settle()
                    for l in range(DEPTH):
                        me.go(V.tensor_scalar(neglam[:, l:l + 1], neglam[:, l:l + 1], -LAM0[l], None, ALU.add))
                for t in range(TT):
                    for i, (a, n) in enumerate(((C_IN, QL), (C_IN + QL, KVL))):
                        v = proj[:, t, a:a + n]
                        me.go(V.tensor_tensor_reduce(out=junk[:, 512 * t + a - C_IN:512 * t + a - C_IN + n], in0=v, in1=v, scale=1.0, scalar=0.0, op0=ALU.mult, op1=ALU.add, accum_out=va[:, t, i:i + 1]))
                me.settle()
                me.go(V.tensor_scalar(va[:, :, 0:1], va[:, :, 0:1], 1.0 / QL, 1e-6, ALU.mult, ALU.add))
                me.go(V.tensor_scalar(va[:, :, 1:2], va[:, :, 1:2], 1.0 / KVL, 1e-6, ALU.mult, ALU.add), ev("var_lat", L))
                copy(ut[:, 2:4, :], ps[:, U.bank[("ab", L, 1)], :].rearrange("p (c n) -> p c n", c=2), ("ab", L, 1))
                copy(ut[:, 6:8, :], ps[:, U.bank[("ab", L, 3)], :].rearrange("p (c n) -> p c n", c=2), ("ab", L, 3))
                if L:
                    dve.wait_ge(ev("resid", L - 1, 2), 2)
                dve.wait_ge(ev("rstd_lat", L), 1)
                for t in range(TT):
                    for i, (a, n) in enumerate(((0, QL), (QL, KVL))):
                        ins = V.tensor_scalar(z[:, t, a:a + n], proj[:, t, C_IN + a:C_IN + a + n], rs[:, t, i:i + 1], None, ALU.mult)
                        me.go(ins, ev("latent", L) if (t, i) == (1, 1) else None)
                kr = proj[:, :, C_KR:C_KR + ROPE].unsqueeze(2)
                me.go(rope(kr, c1, s1, junk, 1, 16))
                if L == 0:
                    dve.wait_ge(s_bias_out, 16)
                for t in range(TT):
                    for h in range(2):
                        key = ("ukv", L, t, h)
                        wait_full(dve, key)
                        src = ps[:, U.bank[key], 0:384].rearrange("p (h d) -> p h d", d=P)
                        me.go(V.tensor_copy(cbuf[:, t, 960 + 288 * h:960 + 288 * h + 288].rearrange("p (h d) -> p h d", d=CQ)[:, :, 0:NOPE], src[:, :, 0:NOPE]))
                        me.empty(V.tensor_copy(vc[:, t, 192 * h:192 * h + 192].rearrange("p (h d) -> p h d", d=HD), src[:, :, NOPE:P]), key)
                me.settle()
                for t in range(TT):
                    ins = V.tensor_copy(cbuf[:, t, 960:1536].rearrange("p (h d) -> p h d", d=CQ)[:, :, NOPE:CQ],
                                        proj[:, t, C_KR:C_KR + ROPE].unsqueeze(1).broadcast_to([P, C_H, ROPE]))
                    me.go(ins, ev("latent_k", L) if t == 1 else None)
                wait_done(dve, ("uq", L, 1, 1))
                q = cbuf[:, :, 0:576].rearrange("p t (h d) -> p t h d", d=CQ)[:, :, :, NOPE:CQ]
                me.go(rope(q, c1, s1, junk, C_H, 16), ev("latent_q", L))
                for n in (1, 3, 5):
                    copy(ut[0:CQ, 10 + 2 * n:12 + 2 * n, :], ps[0:CQ, U.bank[("ct", L, n)], :].rearrange("p (c n) -> p c n", c=2), ("ct", L, n))
                if L == 0:
                    for n in range(5):
                        copy(bias[:, 2 * n:2 * n + 2, :].rearrange("p h n -> p (h n)"), ps[:, U.bank[("flip", n)], :], ("flip", n))
                    me.settle()
                softmax(L)
                columns("ht", L)
                products_wo(L)
                norm(L, "y", 1)
                columns("hT", L)
                start(split, "gu", L, 1)
                ffn(L)
                if L == 1:
                    a = FVAT["b_ada_2"]
                    me.settle()
                    me.go(V.tensor_tensor(modv[:, :], modv[:, :], fv[:, a:a + 48], ALU.add))
                    me.settle()
                    for n, (m, add, g) in enumerate(((8, 1.0, "g_pre_mix_2"), (32, 1.0, "g_pre_ffn_2"), (16, 0.0, "g_post_mix_2"), (40, 0.0, "g_post_ffn_2"))):
                        me.go(V.scalar_tensor_tensor(out=aff[:, n, :], in0=modv[:, m:m + 8], scalar=add, in1=fv[:, FVAT[g]:FVAT[g] + 8], op0=ALU.add, op1=ALU.mult),
                              ev("mod") if n == 3 else None)
                    me.settle()
                    for v in range(2):
                        for c in range(KC):
                            me.go(V.tensor_scalar(spare[:, D * v + c * P:D * v + (c + 1) * P], ident, aff[:, 2 + v, c:c + 1], None, ALU.mult), ev("diag", v) if c == KC - 1 else None)
                norm(L, "d", 2)
                if L == 1:
                    for t in range(TT):
                        mean_rms(t, "in", 0, ev("squares", "in"), t + 1, ev("var_in"))
                    for t in range(TT):
                        dve.wait_ge(ev("rstd_in"), t + 1)
                        me.go(V.tensor_scalar(z[:, t, :], x[:, t, :], rs[:, t, 0:1], None, ALU.mult), ev("norm_in", 1))
                columns("xT", L + 1)
                start(split, "win", L + 1, 1)

            L = 2
            win(L)

            def rope2(col, n, semaphore=None):
                xs = proj[:, :, col:col + n * HD] if n > 1 else proj[:, :, col:col + R2]
                xs = xs.rearrange("p t (h d) -> p t h d", h=n)[:, :, :, 0:R2]
                me.go(rope(xs, c2, s2, junk, n, R2 // 2), semaphore)

            rope2(NKC, 2)
            me.settle()
            for v in range(2):
                for t in range(TT):
                    src = proj[:, t, (NKC, NVC)[v]:(NKC, NVC)[v] + P].rearrange("p (g d) -> p g d", g=2).unsqueeze(2).broadcast_to([P, 2, 2, HD])
                    me.go(V.tensor_copy(dup[:, t, S * v:S * v + S].rearrange("p (g r d) -> p g r d", g=2, r=2), src), ev("dup_rows") if (v, t) == (1, 1) else None)
            rope2(IQ, 9)
            me.settle()
            me.go(V.tensor_scalar(wi[:, :, :], proj[:, :, IW:IW + 8], 8 ** -0.5 * 64 ** -0.5, None, ALU.mult))
            for i in range(2):
                me.go(V.tensor_copy(z[:, :, 64 * i:64 * i + 64], proj[:, :, IK:IK + 64]), ev("idx_rows") if i else None)
            wait_full(dve, ("nT", 5))
            me.empty(shifted(lambda o, i, f: V.tensor_copy(o, i), 5, None), ("nT", 5))
            for t in range(TT):
                v = proj[:, t, DCKV:DCKV + KVL]
                me.go(V.tensor_tensor_reduce(out=tw[:, t, 0:KVL], in0=v, in1=v, scale=1.0, scalar=0.0, op0=ALU.mult, op1=ALU.add, accum_out=va[:, t, 0:1]))
            me.settle()
            me.go(V.tensor_scalar(va[:, :, 0:1], va[:, :, 0:1], 1.0 / KVL, 1e-6, ALU.mult, ALU.add), ev("var_ckv"))
            dve.wait_ge(ev("rstd_ckv"), 1)
            for t in range(TT):
                me.go(V.tensor_scalar(z[:, t, P:S], proj[:, t, DCKV:DCKV + KVL], rs[:, t, 0:1], None, ALU.mult), ev("ckv_rows") if t else None)
            for col, n in ((NQ, 8), (NKS, 2), (NKW, 2), (DQ, 8), (DKR, 1)):
                me.settle()
                rope2(col, n, ev("rope_rows") if col == DKR else None)
            me.settle()
            dve.wait_ge(ev("gexp"), 1)
            me.go(V.tensor_scalar(gt[:, :, :], gt[:, :, :], 1.0, None, ALU.add))
            me.settle()
            me.go(V.reciprocal(gt[:, :, :], gt[:, :, :]))
            me.settle()
            for t in range(TT):
                me.go(V.tensor_scalar(gt[:, t, 0:8], gt[:, t, 0:8], cv("cmpvalid")[:, t:t + 1], None, ALU.mult))
            key = ("cmp1",)
            b = U.bank[key]
            wait_full(dve, key)
            for v in range(2):
                a = FVAT["cmp_b1_2"] + v
                me.go(V.tensor_tensor(hb[:, v:v + 1], ps[:, b, 32 * v + 30:32 * v + 31], fv[:, a:a + 1], ALU.add))
            me.settle()
            me.go(V.tensor_scalar(hid[:, 0, 0:30], ps[:, b, 0:30], hb[:, 0:1], None, ALU.add))
            me.empty(V.tensor_scalar(hid[:, 0, 30:60], ps[:, b, 32:62], hb[:, 1:2], None, ALU.add), key)
            me.settle()
            me.go(V.tensor_tensor(hid[:, 1, :], hid[:, 0, :], hid[:, 0, :], ALU.mult))
            me.settle()
            me.go(V.tensor_scalar(hid[:, 1, :], hid[:, 1, :], 0.044715, 1.0, ALU.mult, ALU.add))
            me.settle()
            me.go(V.tensor_tensor(hid[:, 1, :], hid[:, 1, :], hid[:, 0, :], ALU.mult), ev("gelu_arg"))
            copy(ut[:, 10:12, :], ps[:, U.bank[("idxT", 1)], :].rearrange("p (c n) -> p c n", c=2), ("idxT", 1))
            for h in range(8):
                wait_done(dve, ("lg", h))
                if h:
                    me.settle()
                for t, (a, e) in enumerate(((0, P), (P, 384))):
                    prev = dmask[:, a:e] if h else (cv("causal")[:, P:S] if t == 0 else cv("causal"))
                    me.go(V.scalar_tensor_tensor(out=dmask[:, a:e], in0=probs[:, h % 4, a:e], scalar=wi[:, t, h:h + 1], in1=prev, op0=ALU.mult, op1=ALU.add),
                          ev("idx_added") if t else None)
            dve.wait_ge(ev("gelu_exp"), 1)
            me.go(V.tensor_scalar(hid[:, 2, :], hid[:, 2, :], 1.0, None, ALU.add))
            me.settle()
            me.go(V.reciprocal(hid[:, 2, :], hid[:, 2, :]))
            me.settle()
            me.go(V.tensor_tensor(hid[:, 3, :], hid[:, 2, :], hid[:, 0, :], ALU.mult), ev("hidden"))
            for t in range(TT):
                key = ("kd", t)
                wait_full(dve, key)
                kd = cbuf[:, t, 0:512].rearrange("p (h d) -> p h d", d=HD)
                me.empty(V.tensor_copy(kd[:, :, R2:HD], ps[:, U.bank[key], 0:384].rearrange("p (h d) -> p h d", d=48)), key)
                me.go(V.tensor_copy(kd[:, :, 0:R2], proj[:, t, DKR:DKR + R2].unsqueeze(1).broadcast_to([P, 8, R2])), ev("dk_rows") if t else None)
            for n in (1, 3):
                copy(*turned(n), ("nT", n))
            copy(*turned(7), ("nT", 7))
            key = ("cmp2",)
            b = U.bank[key]
            wait_full(dve, key)
            me.go(V.tensor_scalar(kcmp[:, 0:NCMP], ps[:, b, 0:NCMP], fv[:, B2K:B2K + 1], None, ALU.add))
            me.empty(V.tensor_tensor(vcmp[0:NCMP, :].rearrange("p (g d) -> p g d", g=2), ps[0:NCMP, b, 64:192].rearrange("p (g d) -> p g d", g=2),
                                     b2v[0:NCMP, :].unsqueeze(1).broadcast_to([NCMP, 2, HD]), ALU.add), key)
            softmax(L)
            columns("ht", L)
            products_wo(L)
            add_gated(L, "y", 0, lambda t: ev("mixed"))
            for t in range(TT):
                mean_rms(t, "mid", 1, ev("squares", "mid"), t + 1, ev("var_mid"))
            for t in range(TT):
                dve.wait_ge(ev("rstd_mid"), t + 1)
                me.go(V.tensor_scalar(z[:, t, :], x[:, t, :], rs[:, t, 1:2], None, ALU.mult), ev("norm1", L))
            columns("hT", L)
            start(split, "gu", L, 1)
            ffn(L)
            add_gated(L, "d", 1, lambda t: ev("out_rows", t))

        @block.gpsimd
        def _(gp):
            me = Steps(gp, pool_step)
            gp.dma_start(hot[:, :], A["hot"]).then_inc(s_const, 16)
            gp.dma_start(relb[0:32, :], A["rel_bias"]).then_inc(s_const, 16)
            gp.dma_start(relb[32:34, :], A["which"]).then_inc(s_const, 16)
            for rows, names, base in ((rowsA, ROWS_A, 0), (rowsB, ROWS_B, N_A)):
                for n, k in names:
                    at = FVAT[n] - base
                    gp.dma_start(rows[at:at + k, :], A["rows_" + n]).then_inc(s_vec, 16)
            for i in range(2):
                gp.dma_start(rowsA[B2K:B2K + 1, 64 * i:64 * i + 64], A["cmp_b2_2"][0, 0:1, :]).then_inc(s_vec, 16)
            for l in range(DEPTH):
                gp.dma_start(lamin[:, l, :], A["diff_lambda"][l].rearrange("a b -> (a b)").partition_broadcast(P)).then_inc(s_vec, 16)
                gp.dma_start(sg[:, l, :], A["subln_g"][l].partition_broadcast(P)).then_inc(s_vec, 16)
            gp.dma_start(b2v[0:NCMP, :], A["cmp_b2_2"][0, 1].partition_broadcast(NCMP)).then_inc(s_vec, 16)
            me.go(gp.memset(ones[:, :], 1.0))
            me.go(gp.memset(half[:, :], -0.5))
            me.settle()
            loads = [0]

            def load_affine(name, l):
                for i, s in enumerate("gb"):
                    gp.dma_start(lnb[:, i, :], A[name + "_" + s][l].partition_broadcast(P)).then_inc(s_lnb, 16)
                loads[0] += 1

            def power(dst, src, wait, value, signal):
                gp.wait_ge(wait, value)
                n = src.shape[-1]
                h = half[:, 0:n] if len(src.shape) == 2 else half[:, 0:2 * n].rearrange("p (a b) -> p a b", a=2)
                gp.tensor_tensor(dst, src, h, ALU.pow).then_inc(signal, 1)

            def residual(L, ln):
                gp.wait_ge(s_lnb, 32 * loads[0])
                a = LEFT if (L, ln) == (1, 2) else 0
                for t in range(TT):
                    gp.wait_ge(ev("norm%d" % ln, L), t + 1)
                    me.go(gp.tensor_tensor(x[:, t, a:D], z[:, t, a:D], lnb[:, 0, a:D], ALU.mult))
                    me.settle()
                    me.go(gp.tensor_tensor(x[:, t, a:D], x[:, t, a:D], lnb[:, 1, a:D], ALU.add), ev("resid", L, ln))
                me.settle()

            def modulation(q):
                if q:
                    wait_full(gp, ("ada", q - 1))
                for h in range(2):
                    w = raw[:, ITEM["ada", q, h] % NRAW, :].rearrange("p (k n) -> p k n", k=4)
                    for k in range(4):
                        if h == k == 0:
                            continue
                        gp.wait_ge(ada_scaled, 8 * q + 4 * h + k + 1)
                        if 4 * h + k > 1:
                            me.settle()
                        other = w[:, 0, :] if 4 * h + k == 1 else adasum[:, :]
                        me.go(gp.tensor_tensor(adasum[:, :], other, w[:, k, :], ALU.add), (ada_summed if h else ada_read) if k == 3 else None)

            load_affine("ln1", 0)
            gp.wait_ge(ev("brow"), 1)
            gp.dma_start(bias_dram, brow[:, :]).then_inc(s_bias_out, 16)
            gp.wait_ge(s_bias_out, 16)
            gp.dma_start(bias[:, :, :], bass.AP(bias_dram.tensor, bias_dram.offset, [[1, P], [384, A_H + B_H], [1, S]])).then_inc(s_bias_in, 16)
            for L in range(DEPTH):
                power(rs[:, :, 0:2], va[:, :, 0:2], ev("var_lat", L), 1, ev("rstd_lat", L))
                for q in ADA_ATT[L]:
                    modulation(q)
                power(rb[:, :, :], vb[:, :, :], ev("var_b", L), 1, ev("rstd_b", L))
                for ln in (1, 2):
                    for t in range(TT):
                        power(rs[:, t, 0:1], va[:, t, 0:1], ev("var", ln, L), t + 1, ev("rstd", ln, L))
                    residual(L, ln)
                    if ln == 1:
                        load_affine("ln2", L)
                        for q in ADA_FFN[L]:
                            modulation(q)
                    elif L == 0:
                        load_affine("ln1", 1)
            for t in range(TT):
                power(rs[:, t, 0:1], va[:, t, 0:1], ev("var_in"), t + 1, ev("rstd_in"))
            wait_full(gp, ("G", 1, 1))
            for v in range(2):
                gp.wait_ge(landed[ITEM["w1", v] % NRAW], LANDED["w1", v])
                w = raw[:, ITEM["w1", v] % NRAW, :].rearrange("p (c n) -> p c n", c=16)
                col, o = FVAT["cmp_pe_2"] + 16 * v, v * P
                me.go(gp.tensor_tensor(spare[:, o:o + SLOTW].rearrange("p (c n) -> p c n", c=16), w, fv[:, col:col + 16].unsqueeze(2).broadcast_to([P, 16, P]), ALU.mult))
                n = SLOTW // 2
                while n >= P:
                    me.settle()
                    me.go(gp.tensor_tensor(spare[:, o:o + n], spare[:, o:o + n], spare[:, o + n:o + 2 * n], ALU.add), ev("pe_sum") if n == P else None)
                    n //= 2
                me.settle()
            power(rs[:, :, 0:1], va[:, :, 0:1], ev("var_ckv"), 1, ev("rstd_ckv"))
            for t in range(TT):
                power(rs[:, t, 0:1], va[:, t, 0:1], ev("var_y"), t + 1, ev("rstd_y"))
            for t in range(TT):
                power(rs[:, t, 1:2], va[:, t, 1:2], ev("var_mid"), t + 1, ev("rstd_mid"))
            for t in range(TT):
                power(rs[:, t, 0:1], va[:, t, 0:1], ev("var_d"), t + 1, ev("rstd_d"))


INPUTS = ["x", "rel_bias", "w_in", "q_norm_g", "kv_norm_g", "w_uq", "w_ukv", "diff_lambda", "subln_g", "w_o", "ln1_g",
          "ln1_b", "ln2_g", "ln2_b", "w_gate", "w_up", "w_down", "c_2", "w_ada_2", "b_ada_2", "g_pre_mix_2",
          "g_post_mix_2", "g_pre_ffn_2", "g_post_ffn_2", "w_in_2", "cmp_pe_2", "cmp_w1_2", "cmp_b1_2", "cmp_w2_2",
          "cmp_b2_2", "g_kv_norm_2", "w_uk_2", "w_uv_2", "w_out_2", "w_gate_up_2", "w_down_2"]


def kernel(**inputs):
    import concourse.bacc as bacc
    from concourse.bass_utils import run_bass_kernel_spmd

    nc = bacc.Bacc("TRN2", target_bir_lowering=False, num_devices=1)
    arrays = {}
    for name in INPUTS:
        arrays[name] = np.ascontiguousarray(inputs[name])
    arrays["consts"], arrays["hot"], arrays["which"] = constants()
    A = {}
    for name, a in arrays.items():
        A[name] = nc.dram_tensor("in_" + name, a.shape, mybir.dt.from_np(a.dtype), kind="ExternalInput").ap()
    for name, k in ROWS_A + ROWS_B:
        ap = A[name]
        A["rows_" + name] = bass.AP(ap.tensor, 0, [[P, k], [1, P]])
    out = nc.dram_tensor("out", (1, S, D), F32, kind="ExternalOutput").ap()
    program(nc, A, out)
    r = run_bass_kernel_spmd(nc, [{"in_" + n: a for n, a in arrays.items()}], core_ids=[0])
    return r.results[0]["out"]
```
